# Optimizing a Trainium2 kernel written in Bass

```python
import jax, jax.numpy as jnp
from jax import lax
import numpy as np
import math

D_MODEL = 1024
BATCH = 1
SEQ = 512
DEPTH = 1

CHUNK = 64
N_MEM = 256
HEAD_DIM = 64
FOX_HEADS = 8
CHUNK_HEADS = 8
FOX_WIDTH = FOX_HEADS * HEAD_DIM
CHUNK_WIDTH = CHUNK_HEADS * HEAD_DIM
IN_COLS = 3 * FOX_WIDTH + FOX_HEADS + 3 * CHUNK_WIDTH
Q_BLOCK = 128
LEFT_CHUNKS = 8
REL_CLIP = 128
NUM_REL = CHUNK + REL_CLIP
MEM_HEADS = 4
MEM_HEAD_DIM = D_MODEL // MEM_HEADS
D_FF = -(-8 * D_MODEL // 768) * 256
EPS = 1e-6
NEG_INF = -1e30


def rms_norm(x, g):
    xf = x.astype(jnp.float32)
    y = xf * lax.rsqrt(jnp.mean(xf * xf, axis=-1, keepdims=True) + EPS)
    return (y * g.astype(jnp.float32)).astype(x.dtype)

def fox_attention(q, k, v, log_f):
    B, S, H, D = q.shape
    nb = S // Q_BLOCK
    scale = D ** -0.5
    c = lax.cumsum(log_f, axis=1)
    c_keys = jnp.transpose(c, (0, 2, 1))
    k_pos = jnp.arange(S)
    q_blocks = jnp.transpose(q.reshape(B, nb, Q_BLOCK, H, D), (1, 0, 2, 3, 4))
    c_blocks = jnp.transpose(c.reshape(B, nb, Q_BLOCK, H), (1, 0, 3, 2))

    def one_block(args):
        i, q_i, c_i = args
        q_pos = i * Q_BLOCK + jnp.arange(Q_BLOCK)
        s = jnp.einsum('bqhd,bkhd->bhqk', q_i, k).astype(jnp.float32) * scale
        s = s + c_i[..., :, None] - c_keys[:, :, None, :]
        s = jnp.where((k_pos[None, :] <= q_pos[:, None])[None, None], s, NEG_INF)
        p = jax.nn.softmax(s, axis=-1)
        return jnp.einsum('bhqk,bkhd->bqhd', p.astype(v.dtype), v)

    out = lax.map(one_block, (jnp.arange(nb), q_blocks, c_blocks))
    return jnp.transpose(out, (1, 0, 2, 3, 4)).reshape(B, S, H, D)

def chunked_rel_attention(q, k, v, rel_bias):
    B, S, H, D = q.shape
    nc = S // CHUNK
    band = (LEFT_CHUNKS + 1) * CHUNK
    pad = LEFT_CHUNKS * CHUNK
    scale = D ** -0.5
    kp = jnp.pad(k, ((0, 0), (pad, 0), (0, 0), (0, 0)))
    vp = jnp.pad(v, ((0, 0), (pad, 0), (0, 0), (0, 0)))
    idx = (jnp.arange(nc) * CHUNK)[:, None] + jnp.arange(band)[None, :]
    k_band = kp[:, idx]
    v_band = vp[:, idx]
    q_c = q.reshape(B, nc, CHUNK, H, D)
    s = jnp.einsum('bnqhd,bnkhd->bhnqk', q_c, k_band).astype(jnp.float32) * scale
    dist = jnp.arange(CHUNK)[:, None] + pad - jnp.arange(band)[None, :]
    rel_idx = jnp.clip(dist, -(CHUNK - 1), REL_CLIP) + (CHUNK - 1)
    bias = rel_bias.astype(jnp.float32)[:, rel_idx]
    s = s + bias[None, :, None]
    valid = (idx - pad) >= 0
    s = jnp.where(valid[None, None, :, None, :], s, NEG_INF)
    p = jax.nn.softmax(s, axis=-1)
    o = jnp.einsum('bhnqk,bnkhd->bnqhd', p.astype(v.dtype), v_band)
    return o.reshape(B, S, H, D)

def memory_cross_attention(h, m, w_q, w_kv, w_o):
    B, S, _ = h.shape
    q = (h @ w_q).reshape(B, S, MEM_HEADS, MEM_HEAD_DIM)
    k, v = jnp.split(m @ w_kv, 2, axis=-1)
    k = k.reshape(B, N_MEM, MEM_HEADS, MEM_HEAD_DIM)
    v = v.reshape(B, N_MEM, MEM_HEADS, MEM_HEAD_DIM)
    s = jnp.einsum('bshd,bmhd->bhsm', q, k).astype(jnp.float32) * (MEM_HEAD_DIM ** -0.5)
    p = jax.nn.softmax(s, axis=-1)
    o = jnp.einsum('bhsm,bmhd->bshd', p.astype(v.dtype), v).reshape(B, S, D_MODEL)
    return o @ w_o

def swiglu(h, w_gate_up, w_down):
    g, u = jnp.split(h @ w_gate_up, 2, axis=-1)
    return (jax.nn.silu(g) * u) @ w_down

def first_inputs(seed: int = 0) -> dict:
    key = jax.random.key(seed)
    ks = jax.random.split(key, 24)

    def nrm(k, shape, scale):
        return scale * jax.random.normal(k, shape, jnp.float32)

    def gain(k, n):
        return 1.0 + nrm(k, (DEPTH, n), 0.05)

    s_d = D_MODEL ** -0.5
    w_in = jnp.concatenate([
        nrm(ks[0], (DEPTH, D_MODEL, 3 * FOX_WIDTH), s_d),
        nrm(ks[1], (DEPTH, D_MODEL, FOX_HEADS), 0.1 * s_d),
        nrm(ks[2], (DEPTH, D_MODEL, 3 * CHUNK_WIDTH), s_d),
    ], axis=-1)
    b_fgate = jnp.linspace(3.0, 7.0, FOX_HEADS)[None, :] + nrm(ks[3], (DEPTH, FOX_HEADS), 0.3)
    return {
        "x": jax.random.normal(ks[4], (BATCH, SEQ, D_MODEL), jnp.float32),
        "mem": jax.random.normal(ks[5], (BATCH, N_MEM, D_MODEL), jnp.float32),
        "g_mix_pre": gain(ks[6], D_MODEL),
        "w_in": w_in,
        "b_fgate": b_fgate,
        "rel_bias": nrm(ks[7], (DEPTH, CHUNK_HEADS, NUM_REL), 0.5),
        "g_fox_out": gain(ks[8], FOX_WIDTH),
        "g_chunk_out": gain(ks[9], CHUNK_WIDTH),
        "w_out": nrm(ks[10], (DEPTH, D_MODEL, D_MODEL), s_d),
        "g_mix_post": gain(ks[11], D_MODEL),
        "g_mem_pre": gain(ks[12], D_MODEL),
        "g_mem_kv": gain(ks[13], D_MODEL),
        "w_mem_q": nrm(ks[14], (DEPTH, D_MODEL, D_MODEL), s_d),
        "w_mem_kv": nrm(ks[15], (DEPTH, D_MODEL, 2 * D_MODEL), s_d),
        "w_mem_o": nrm(ks[16], (DEPTH, D_MODEL, D_MODEL), s_d),
        "g_mem_post": gain(ks[17], D_MODEL),
        "g_ffn_pre": gain(ks[18], D_MODEL),
        "w_gate_up": nrm(ks[19], (DEPTH, D_MODEL, 2 * D_FF), s_d),
        "w_down": nrm(ks[20], (DEPTH, D_FF, D_MODEL), D_FF ** -0.5),
        "g_ffn_post": gain(ks[21], D_MODEL),
    }

def first_block(x, mem, g_mix_pre, w_in, b_fgate, rel_bias, g_fox_out, g_chunk_out, w_out,
              g_mix_post, g_mem_pre, g_mem_kv, w_mem_q, w_mem_kv, w_mem_o, g_mem_post,
              g_ffn_pre, w_gate_up, w_down, g_ffn_post):
    B, S, _ = x.shape
    splits = [FOX_WIDTH, 2 * FOX_WIDTH, 3 * FOX_WIDTH, 3 * FOX_WIDTH + FOX_HEADS,
              3 * FOX_WIDTH + FOX_HEADS + CHUNK_WIDTH, 3 * FOX_WIDTH + FOX_HEADS + 2 * CHUNK_WIDTH]
    for l in range(DEPTH):
        h = rms_norm(x, g_mix_pre[l])
        proj = h @ w_in[l]
        q_f, k_f, v_f, f_logit, q_c, k_c, v_c = jnp.split(proj, splits, axis=-1)
        log_f = jax.nn.log_sigmoid((f_logit + b_fgate[l]).astype(jnp.float32))
        o_f = fox_attention(q_f.reshape(B, S, FOX_HEADS, HEAD_DIM),
                            k_f.reshape(B, S, FOX_HEADS, HEAD_DIM),
                            v_f.reshape(B, S, FOX_HEADS, HEAD_DIM), log_f)
        o_c = chunked_rel_attention(q_c.reshape(B, S, CHUNK_HEADS, HEAD_DIM),
                                    k_c.reshape(B, S, CHUNK_HEADS, HEAD_DIM),
                                    v_c.reshape(B, S, CHUNK_HEADS, HEAD_DIM), rel_bias[l])
        o_f = rms_norm(o_f.reshape(B, S, FOX_WIDTH), g_fox_out[l])
        o_c = rms_norm(o_c.reshape(B, S, CHUNK_WIDTH), g_chunk_out[l])
        mix = jnp.concatenate([o_f, o_c], axis=-1) @ w_out[l]
        x = x + rms_norm(mix, g_mix_post[l])
        h = rms_norm(x, g_mem_pre[l])
        m = rms_norm(mem, g_mem_kv[l])
        ca = memory_cross_attention(h, m, w_mem_q[l], w_mem_kv[l], w_mem_o[l])
        x = x + rms_norm(ca, g_mem_post[l])
        h = rms_norm(x, g_ffn_pre[l])
        x = x + rms_norm(swiglu(h, w_gate_up[l], w_down[l]), g_ffn_post[l])
    return x


DEPTH_2 = 2

N_A = DEPTH_2 // 2
N_B = DEPTH_2 - N_A

A_HEADS = 8
A_QK_DIM = D_MODEL // 2 // A_HEADS
A_V_DIM = D_MODEL // A_HEADS
A_QK_W = A_HEADS * A_QK_DIM
A_V_W = A_HEADS * A_V_DIM
A_IN_WIDTH = 2 * A_QK_W + A_V_W + 2 * A_HEADS + A_V_W
A_CHUNK = 128

B_HEADS = 8
B_Q_LORA = 384
B_KV_LORA = 256
B_NOPE = 128
B_ROPE = 64
B_V = 128
B_QBLOCK = 128
ROPE_THETA = 10000.0

D_FF_2 = 4 * D_MODEL


def rmsnorm(x, g):
    xf = x.astype(jnp.float32)
    y = xf * lax.rsqrt(jnp.mean(xf * xf, axis=-1, keepdims=True) + EPS)
    return (y * g.astype(jnp.float32)).astype(x.dtype)

def modulate(h, shift, scale):
    return h * (1 + scale[:, None, :]) + shift[:, None, :]

def rope_tables(positions):
    half = B_ROPE // 2
    inv = ROPE_THETA ** (-jnp.arange(half, dtype=jnp.float32) / half)
    ang = positions.astype(jnp.float32)[..., None] * inv
    return jnp.cos(ang), jnp.sin(ang)

def apply_rope(x, cos, sin):
    xf = x.astype(jnp.float32)
    x1, x2 = jnp.split(xf, 2, axis=-1)
    out = jnp.concatenate([x1 * cos - x2 * sin, x2 * cos + x1 * sin], axis=-1)
    return out.astype(x.dtype)

def mlstm_chunkwise(q, k, v, i_pre, f_pre):
    B_, H, S, dk = q.shape
    dv = v.shape[-1]
    L = A_CHUNK
    nc = S // L
    f32 = jnp.float32
    qf = q.astype(f32)
    kf = k.astype(f32) * (dk ** -0.5)
    vf = v.astype(f32)
    lf = jax.nn.log_sigmoid(f_pre.astype(f32))
    ig = i_pre.astype(f32)

    def chunks(a):
        return jnp.moveaxis(a.reshape(B_, H, nc, L, *a.shape[3:]), 2, 0)

    qc, kc, vc, ic = chunks(qf), chunks(kf), chunks(vf), chunks(ig)
    bc = jnp.cumsum(chunks(lf), axis=-1)
    tri = jnp.tril(jnp.ones((L, L), dtype=bool))

    def step(carry, xs):
        C, n, m = carry
        qb, kb, vb, ib, bb = xs
        log_d = bb[..., :, None] - bb[..., None, :] + ib[..., None, :]
        log_d = jnp.where(tri, log_d, -jnp.inf)
        log_inter = bb + m[..., None]
        m_t = jnp.maximum(log_inter, jnp.max(log_d, axis=-1))
        w_intra = jnp.exp(log_d - m_t[..., None])
        w_inter = jnp.exp(log_inter - m_t)
        s = jnp.einsum('bhtd,bhsd->bhts', qb, kb) * w_intra
        num = (w_inter[..., None] * jnp.einsum('bhtd,bhde->bhte', qb, C)
               + jnp.einsum('bhts,bhse->bhte', s, vb))
        den = w_inter * jnp.einsum('bhtd,bhd->bht', qb, n) + jnp.sum(s, axis=-1)
        h = num / jnp.maximum(jnp.abs(den), jnp.exp(-m_t))[..., None]
        b_last = bb[..., -1]
        log_w = b_last[..., None] - bb + ib
        m_new = jnp.maximum(b_last + m, jnp.max(log_w, axis=-1))
        w = jnp.exp(log_w - m_new[..., None])
        decay = jnp.exp(b_last + m - m_new)
        C_new = decay[..., None, None] * C + jnp.einsum('bhs,bhsd,bhse->bhde', w, kb, vb)
        n_new = decay[..., None] * n + jnp.einsum('bhs,bhsd->bhd', w, kb)
        return (C_new, n_new, m_new), h

    init = (jnp.zeros((B_, H, dk, dv), f32), jnp.zeros((B_, H, dk), f32), jnp.zeros((B_, H), f32))
    _, hc = lax.scan(step, init, (qc, kc, vc, ic, bc))
    return jnp.moveaxis(hc, 0, 2).reshape(B_, H, S, dv).astype(q.dtype)

def mlstm_mixer(h, w_in, gate_b, head_g, w_out):
    B_, S, _ = h.shape
    proj = h @ w_in
    splits = [A_QK_W, 2 * A_QK_W, 2 * A_QK_W + A_V_W, 2 * A_QK_W + A_V_W + A_HEADS,
              2 * A_QK_W + A_V_W + 2 * A_HEADS]
    q, k, v, ig, fg, og = jnp.split(proj, splits, axis=-1)
    heads = lambda a, d: a.reshape(B_, S, A_HEADS, d).transpose(0, 2, 1, 3)
    i_pre = (ig + gate_b[0]).transpose(0, 2, 1)
    f_pre = (fg + gate_b[1]).transpose(0, 2, 1)
    hh = mlstm_chunkwise(heads(q, A_QK_DIM), heads(k, A_QK_DIM), heads(v, A_V_DIM), i_pre, f_pre)
    hh = rmsnorm(hh.transpose(0, 2, 1, 3), head_g).reshape(B_, S, A_V_W)
    return (hh * jax.nn.sigmoid(og)) @ w_out

def mla_shared_kv(x, shift, scale, g_in, w_a, g_latent, w_b, cos, sin):
    B_, S, _ = x.shape
    h = modulate(rmsnorm(x, g_in), shift, scale)
    kv = h @ w_a
    c_kv, k_rope = jnp.split(kv, [B_KV_LORA], axis=-1)
    c_kv = rmsnorm(c_kv, g_latent)
    kvb = (c_kv @ w_b).reshape(B_, S, B_HEADS, B_NOPE + B_V)
    k_nope, v = jnp.split(kvb, [B_NOPE], axis=-1)
    k_rope = apply_rope(k_rope, cos, sin)
    return k_nope, k_rope, v

def causal_mla_attention(q_nope, q_rope, k_nope, k_rope, v):
    B_, S, H, _ = q_nope.shape
    nb = S // B_QBLOCK
    scale = (B_NOPE + B_ROPE) ** -0.5
    qn = jnp.moveaxis(q_nope.reshape(B_, nb, B_QBLOCK, H, B_NOPE), 1, 0)
    qr = jnp.moveaxis(q_rope.reshape(B_, nb, B_QBLOCK, H, B_ROPE), 1, 0)
    kpos = jnp.arange(S, dtype=jnp.int32)
    starts = jnp.arange(nb, dtype=jnp.int32) * B_QBLOCK

    def block(args):
        qn_b, qr_b, start = args
        s = (jnp.einsum('bqhd,bkhd->bhqk', qn_b, k_nope)
             + jnp.einsum('bqhd,bkd->bhqk', qr_b, k_rope)).astype(jnp.float32) * scale
        qpos = start + jnp.arange(B_QBLOCK, dtype=jnp.int32)
        s = jnp.where(kpos[None, :] <= qpos[:, None], s, -jnp.inf)
        p = jax.nn.softmax(s, axis=-1)
        return jnp.einsum('bhqk,bkhd->bqhd', p.astype(v.dtype), v)

    o = lax.map(block, (qn, qr, starts))
    return jnp.moveaxis(o, 0, 1).reshape(B_, S, H, B_V)

def mla_mixer(h, w_q_a, g_q_latent, w_q_b, w_out, k_nope, k_rope, v, cos, sin):
    B_, S, _ = h.shape
    cq = rmsnorm(h @ w_q_a, g_q_latent)
    q = (cq @ w_q_b).reshape(B_, S, B_HEADS, B_NOPE + B_ROPE)
    q_nope, q_rope = jnp.split(q, [B_NOPE], axis=-1)
    q_rope = apply_rope(q_rope, cos[:, :, None, :], sin[:, :, None, :])
    o = causal_mla_attention(q_nope, q_rope, k_nope, k_rope, v)
    return o.reshape(B_, S, B_HEADS * B_V) @ w_out

def sqrelu_mlp(h, w1, w2):
    return jnp.square(jax.nn.relu(h @ w1)) @ w2

def second_inputs(seed: int = 0) -> dict:
    key = jax.random.key(seed)
    ks = jax.random.split(key, 24)
    f32 = jnp.float32

    def nrm(k, shape, fan_in, s=1.0):
        return s * (fan_in ** -0.5) * jax.random.normal(k, shape, f32)

    def gain(k, shape):
        return 1.0 + 0.02 * jax.random.normal(k, shape, f32)

    x = jax.random.normal(ks[0], (BATCH, SEQ, D_MODEL), f32)
    c = jax.random.normal(ks[1], (BATCH, D_MODEL), f32)
    positions = (jax.random.randint(ks[2], (BATCH, 1), 0, 4096, dtype=jnp.int32)
                 + jnp.arange(SEQ, dtype=jnp.int32)[None, :])
    ada_w = nrm(ks[3], (DEPTH_2, D_MODEL, 6 * D_MODEL), D_MODEL, 0.5)
    ada_b = 0.02 * jax.random.normal(ks[4], (DEPTH_2, 6 * D_MODEL), f32)
    norm_g = gain(ks[5], (DEPTH_2, 4, D_MODEL))
    a_w_in = nrm(ks[6], (N_A, D_MODEL, A_IN_WIDTH), D_MODEL)
    kg1, kg2 = jax.random.split(ks[7])
    i_bias = 0.1 * jax.random.normal(kg1, (N_A, A_HEADS), f32)
    f_bias = jnp.linspace(3.0, 6.0, A_HEADS, dtype=f32)[None, :] + 0.1 * jax.random.normal(kg2, (N_A, A_HEADS), f32)
    a_gate_b = jnp.stack([i_bias, f_bias], axis=1)
    a_head_g = gain(ks[8], (N_A, A_HEADS, A_V_DIM))
    a_w_out = nrm(ks[9], (N_A, A_V_W, D_MODEL), A_V_W)
    kv_ada_w = nrm(ks[10], (D_MODEL, 2 * D_MODEL), D_MODEL, 0.5)
    kv_ada_b = 0.02 * jax.random.normal(ks[11], (2 * D_MODEL,), f32)
    kv_norm_g = gain(ks[12], (D_MODEL,))
    kv_w_a = nrm(ks[13], (D_MODEL, B_KV_LORA + B_ROPE), D_MODEL)
    kv_latent_g = gain(ks[14], (B_KV_LORA,))
    kv_w_b = nrm(ks[15], (B_KV_LORA, B_HEADS * (B_NOPE + B_V)), B_KV_LORA)
    b_w_q_a = nrm(ks[16], (N_B, D_MODEL, B_Q_LORA), D_MODEL)
    b_q_latent_g = gain(ks[17], (N_B, B_Q_LORA))
    b_w_q_b = nrm(ks[18], (N_B, B_Q_LORA, B_HEADS * (B_NOPE + B_ROPE)), B_Q_LORA)
    b_w_out = nrm(ks[19], (N_B, B_HEADS * B_V, D_MODEL), B_HEADS * B_V)
    mlp_w1 = nrm(ks[20], (DEPTH_2, D_MODEL, D_FF_2), D_MODEL)
    mlp_w2 = nrm(ks[21], (DEPTH_2, D_FF_2, D_MODEL), D_FF_2)
    return {"x": x, "c": c, "positions": positions, "ada_w": ada_w, "ada_b": ada_b,
            "norm_g": norm_g, "a_w_in": a_w_in, "a_gate_b": a_gate_b, "a_head_g": a_head_g,
            "a_w_out": a_w_out, "kv_ada_w": kv_ada_w, "kv_ada_b": kv_ada_b, "kv_norm_g": kv_norm_g,
            "kv_w_a": kv_w_a, "kv_latent_g": kv_latent_g, "kv_w_b": kv_w_b, "b_w_q_a": b_w_q_a,
            "b_q_latent_g": b_q_latent_g, "b_w_q_b": b_w_q_b, "b_w_out": b_w_out,
            "mlp_w1": mlp_w1, "mlp_w2": mlp_w2}

def second_block(x, c, positions, ada_w, ada_b, norm_g, a_w_in, a_gate_b, a_head_g, a_w_out,
              kv_ada_w, kv_ada_b, kv_norm_g, kv_w_a, kv_latent_g, kv_w_b, b_w_q_a, b_q_latent_g,
              b_w_q_b, b_w_out, mlp_w1, mlp_w2):
    cond = jax.nn.silu(c)
    cos, sin = rope_tables(positions)
    shared_kv = None
    for l in range(DEPTH_2):
        ada = cond @ ada_w[l] + ada_b[l]
        sh1, sc1, g1, sh2, sc2, g2 = jnp.split(ada, 6, axis=-1)
        h = modulate(rmsnorm(x, norm_g[l, 0]), sh1, sc1)
        if l < N_A:
            y = mlstm_mixer(h, a_w_in[l], a_gate_b[l], a_head_g[l], a_w_out[l])
        else:
            if shared_kv is None:
                kv_shift, kv_scale = jnp.split(cond @ kv_ada_w + kv_ada_b, 2, axis=-1)
                shared_kv = mla_shared_kv(x, kv_shift, kv_scale, kv_norm_g, kv_w_a, kv_latent_g,
                                          kv_w_b, cos, sin)
            k_nope, k_rope, v = shared_kv
            j = l - N_A
            y = mla_mixer(h, b_w_q_a[j], b_q_latent_g[j], b_w_q_b[j], b_w_out[j],
                          k_nope, k_rope, v, cos, sin)
        x = x + g1[:, None, :] * rmsnorm(y, norm_g[l, 1])
        h = modulate(rmsnorm(x, norm_g[l, 2]), sh2, sc2)
        y = sqrelu_mlp(h, mlp_w1[l], mlp_w2[l])
        x = x + g2[:, None, :] * rmsnorm(y, norm_g[l, 3])
    return x


def setup_inputs(seed=0):
    out = dict(first_inputs(seed))
    for name, value in second_inputs(seed + 1).items():
        if name != "x":
            out[name + "_2"] = value
    return out


def reference(
    x, mem, g_mix_pre, w_in, b_fgate, rel_bias, g_fox_out, g_chunk_out, w_out, g_mix_post,
    g_mem_pre, g_mem_kv, w_mem_q, w_mem_kv, w_mem_o, g_mem_post, g_ffn_pre, w_gate_up, w_down,
    g_ffn_post, c_2, positions_2, ada_w_2, ada_b_2, norm_g_2, a_w_in_2, a_gate_b_2, a_head_g_2,
    a_w_out_2, kv_ada_w_2, kv_ada_b_2, kv_norm_g_2, kv_w_a_2, kv_latent_g_2, kv_w_b_2,
    b_w_q_a_2, b_q_latent_g_2, b_w_q_b_2, b_w_out_2, mlp_w1_2, mlp_w2_2,
):
    x = first_block(
        x, mem, g_mix_pre, w_in, b_fgate, rel_bias, g_fox_out, g_chunk_out, w_out, g_mix_post,
        g_mem_pre, g_mem_kv, w_mem_q, w_mem_kv, w_mem_o, g_mem_post, g_ffn_pre, w_gate_up,
        w_down, g_ffn_post,
    )
    return second_block(
        x, c_2, positions_2, ada_w_2, ada_b_2, norm_g_2, a_w_in_2, a_gate_b_2, a_head_g_2,
        a_w_out_2, kv_ada_w_2, kv_ada_b_2, kv_norm_g_2, kv_w_a_2, kv_latent_g_2, kv_w_b_2,
        b_w_q_a_2, b_q_latent_g_2, b_w_q_b_2, b_w_out_2, mlp_w1_2, mlp_w2_2,
    )


_drawn_inputs = setup_inputs


def setup_inputs(seed=0):
    import zlib

    import numpy as np

    out = dict(_drawn_inputs(seed))
    spreads = {}
    factors = {'norm_g_2': 5.68,
     'a_head_g_2': 8.0,
     'kv_ada_b_2': 8.0,
     'kv_norm_g_2': 8.0,
     'kv_latent_g_2': 8.0,
     'b_q_latent_g_2': 8.0}
    for name, (base, spread) in spreads.items():
        noise = np.random.default_rng([zlib.crc32(name.encode()), seed]).standard_normal(out[name].shape)
        drawn = base * np.exp(spread * noise) if base else spread * noise
        out[name] = __import__('jax').numpy.asarray(drawn.astype(out[name].dtype))
    for name, factor in factors.items():
        out[name] = (out[name] * factor).astype(out[name].dtype)
    return out
```

```python
from contextlib import ExitStack

import numpy as np
import concourse.bass as bass
from concourse import mybir

F32 = mybir.dt.float32
F32R = mybir.dt.float32r
I32 = mybir.dt.int32
ALU = mybir.AluOpType
ACT = mybir.ActivationFunctionType
AX = mybir.AxisListType.X

P = 128
S = 512
D = 1024
KC = D // P
NT = S // P
MEM = 256
DFF1 = 2816
DFF2 = 4096
HEADS = 8
EPS = 1e-6
NEG = -1e30
REL = 128
CH = 64

PANELS = [("w_in", 24), ("w_out", 8), ("mem_kv", 16), ("mem_q", 8), ("mem_o", 8), ("ffn", 3 * DFF1 // P),
          ("a_in", 24), ("a_out", 8), ("mlp0", 2 * DFF2 // P), ("kv_a", 3), ("kv_b", 4), ("q_a", 3), ("q_b", 6),
          ("b_out", 8), ("mlp1", 2 * DFF2 // P)]
PANEL0 = {}
_n = 0
for _name, _count in PANELS:
    PANEL0[_name] = _n
    _n += _count
NPANEL = _n
assert NPANEL % 2 == 0

PROJ = [("w_in", 16), ("w_out", 8), ("mem_k", 8), ("mem_q", 8), ("mem_o", 8), ("a_in", 16), ("a_out", 8),
        ("kv_a", 3), ("k_nope", 8), ("q_a", 3), ("q_nope", 8), ("q_rope", 4), ("b_out", 8)]
STATS = [("x", 8, D), ("fox", 4, 512), ("chunk", 4, 512), ("mem", 8, D), ("mix", 8, D), ("x_mem", 8, D),
         ("ca", 8, D), ("x_ffn", 8, D), ("ffn", 8, D), ("x_a", 8, D), ("a", 8, D), ("x_mlp0", 8, D), ("mlp0", 8, D), ("x_b", 8, D), ("c_kv", 2, 256), ("c_q", 3, 384),
         ("b", 8, D), ("x_mlp1", 8, D), ("mlp1", 8, D)]
MAKES = [("x", 8, 1), ("o_fox", 4, 1), ("o_chunk", 4, 1), ("mem", 8, 1), ("x_mem", 8, 1), ("o_mem", 8, 0), ("x_ffn", 8, 1),
         ("x_a", 8, 1), ("cells", 8, 0), ("x_mlp0", 8, 1), ("x_kv", 8, 1), ("c_kv", 2, 1), ("x_b", 8, 1),
         ("c_q", 3, 1), ("o_b", 8, 0), ("x_mlp1", 8, 1)]
MAKES_T = [(name, n * normed) for name, n, normed in MAKES]
TURN = 2 * np.pi
TURN_PARTS = (6.28125, float(np.float32(TURN - 6.28125)), float(TURN - 6.28125 - np.float32(TURN - 6.28125)))
PI_IN = 3.1415925
ROUND = 1.5 * 2 ** 23
RESID = ["mix", "ca", "ffn", "a", "mlp0", "b", "mlp1"]
FFNS = [("ffn", DFF1 // P // 2, True), ("mlp0", DFF2 // P // 2, False), ("mlp1", DFF2 // P // 2, False)]


VTILES = [("w_in", 8), ("mem", 4), ("a_in", 8), ("kv_b", 8)]
ADDS = [(name, n - 1) for name, n, _ in STATS]


def ff_up(name, g):
    size = 6 if name == "ffn" else 4
    return PANEL0[name] if isinstance(g, int) and g == 0 else g * size + (PANEL0[name] - 2)


def ff_down(name, g, last=False):
    size = 6 if name == "ffn" else 4
    return g * size + (PANEL0[name] + (size - 2 if last else 2 * size - 4))


def before(table, name, column=1):
    total = 0
    for row in table:
        if row[0] == name:
            return total
        total += row[column]
    raise KeyError(name)


def row(table, name):
    return [r for r in table if r[0] == name][0]


VEC = {}
_v = 0
for _name, _count in [("g_mix_pre", 8), ("g_out", 8), ("g_mix_post", 8), ("g_mem_pre", 8), ("g_mem_kv", 8),
                      ("g_mem_post", 8), ("g_ffn_pre", 8), ("g_ffn_post", 8), ("norm_g", 64), ("ada_b", 112),
                      ("kv_norm_g", 8), ("head_g", 8), ("kv_latent_g", 2), ("q_latent_g", 3), ("c", 8),
                      ("zero", 8), ("b_f", 8), ("gate_b", 16)]:
    VEC[_name] = _v
    _v += _count
NVEC = _v
CON = {}
_c = 0
for _name, _count in [("ident", P), ("ones", P), ("mask", P), ("maskT", P), ("upper", S), ("minus_onehot", 8),
                      ("inv_freq", 1), ("rope_sign", 1)]:
    CON[_name] = _c
    _c += _count
NCON = _c
SH1, SC1, G1, SH2, SC2, G2, KVSH, KVSC = range(8)
LAYER1 = 8


class Chain:

    def __init__(self, eng, sem):
        self.eng, self.sem, self.n = eng, sem, 0

    def link(self, ins):
        ins.then_inc(self.sem, 1)
        self.n = self.n + 1
        self.eng.wait_ge(self.sem, self.n)


def program(nc, xT, memT, panels, ada, vecs, cons, gates_w, bias, pos, outT):
    ctx = ExitStack()
    with ctx:
        def sb(name, shape, dt=F32, where=ctx):
            return where.enter_context(nc.sbuf_tensor(name, shape, dt))

        def sem(name):
            return ctx.enter_context(nc.semaphore(name))

        x = sb("x", [P, KC, S])
        Y = sb("Y", [P, KC, S])
        stage = sb("stage", [P, 2, D])
        WH = sb("WH", [P, 2, D], F32R)
        WL = sb("WL", [P, 2, D], F32R)
        apiece = sb("apiece", [P, 2, D])
        aacc = sb("aacc", [P, D])
        con = sb("con", [P, NCON])
        vec = sb("vec", [P, NVEC])
        adac = sb("adac", [P, 112])
        cond = sb("cond", [P, KC])
        pre_g = sb("pre_g", [P, 5, KC])
        post_g = sb("post_g", [P, 4, KC])
        identr = sb("identr", [P, P], F32R)
        onesr = sb("onesr", [P, P], F32R)
        maskr = sb("maskr", [P, P], F32R)
        maskTr = sb("maskTr", [P, P], F32R)
        wgate = sb("wgate", [P, KC, 24])
        wgateH = sb("wgateH", [P, KC, 24], F32R)
        wgateL = sb("wgateL", [P, KC, 24], F32R)
        stat = sb("stat", [P, 24])
        lf = sb("lf", [P, NT, 8])
        gi = sb("gi", [P, NT, 8])
        gs = sb("gs", [P, NT, 8])
        gz = sb("gz", [P, NT, 8])
        gw = sb("gw", [P, NT, 8])
        sq = sb("sq", [P, 2, S])
        acc = sb("acc", [P, S])
        rstd = sb("rstd", [P, S])
        eps = sb("eps", [P, 1])
        t = sb("t", [P, 2, S])
        region = ExitStack()
        QK = sb("QK", [P, 16, S], F32, region)
        V = sb("V", [P, NT, D], F32, region)
        X = sb("X", [P, 4, S], F32, region)
        part = ExitStack()
        H = sb("H", [P, KC, 2, S], F32R, part)
        HM = sb("HM", [P, KC, 2, MEM], F32R, part)
        part.close()
        part = ExitStack()
        QS = sb("QS", [P, 2, 2, 2, S], F32R, part)
        KS = sb("KS", [P, 2, 2, S], F32R, part)
        VS = sb("VS", [P, 2, 2, S], F32R, part)
        PT = sb("PT", [P, 2, NT, S], F32R, part)
        RB = sb("RB", [40, S], F32R, part)
        RBS = sb("RBS", [40, 2, S], F32R, part)
        part.close()
        part = ExitStack()
        sb("under_kr", [P, 24 * S], F32R, part)
        KR = sb("KR", [P, 2, S], F32R, part)
        part.close()
        region.close()
        region = ExitStack()
        HID = sb("HID", [P, 2, 2, 2, S], F32R, region)
        region.close()

        bank = [ctx.enter_context(nc.psum_tensor(f"bank{i}", [P, S], F32)) for i in range(8)]
        G, T, O = bank[0:2], bank[2:4], bank[4:6]
        ST, AD = bank[6], bank[7]

        ident = con[:, CON["ident"]:CON["ident"] + P]
        ones = con[:, CON["ones"]:CON["ones"] + P]
        upper = con[:, CON["upper"]:CON["upper"] + S]

        memf = V[:, 0:2, :].rearrange("p a (c t) -> p (a c) t", t=MEM)
        memK = QK[:, 8:12, :].rearrange("p a (c t) -> p (a c) t", t=MEM)
        QKf = QK[:].rearrange("p a b -> p (a b)")
        Xf = X[:].rearrange("p a b -> p (a b)")
        ropeF, ropeA, ropeB = apiece[:, 0, S:2 * S], apiece[:, 1, 0:S], apiece[:, 1, S:2 * S]
        swapped = [apiece[:, 0, 0:S], apiece[:, 0, S:2 * S]]
        rstd_x = apiece[:, 1, 0:S]
        gu = sq[:, 1, :]
        gsf = gs[:].rearrange("p a b -> p (a b)")
        cos, sin = aacc[:, 0:S], aacc[:, S:2 * S]
        half_rows = [slice(0, 64), slice(64, 128)]

        def col(name, m=0):
            return vec[:, VEC[name] + m:VEC[name] + m + 1]

        s_const = sem("const_loaded")
        s_x = sem("x_loaded")
        s_mem = sem("mem_loaded")
        s_gw = sem("gate_weights_loaded")
        s_bias = sem("bias_loaded")
        s_pos = sem("positions_loaded")
        s_stage = [sem("panel0_loaded"), sem("panel1_loaded")]
        s_split = sem("panel_split")
        s_hisplit = sem("panel_high")
        s_used = sem("panel_used")
        s_piece = [sem("piece0_loaded"), sem("piece1_loaded")]
        s_pused = sem("piece_used")
        s_asum = sem("ada_summed")
        s_acol = sem("ada_columns")
        s_proj = sem("projected")
        s_free = sem("projection_bank_free")
        s_vev = sem("values_evacuated")
        s_sq = sem("squares")
        s_add = sem("squares_added")
        s_ms = sem("mean_squares")
        s_rt = sem("roots")
        s_rstd = sem("rstd_ready")
        s_t = sem("scaled")
        s_hi = sem("input_high")
        s_h = sem("input_split")
        s_hold = sem("waits_held")
        s_phold = sem("panel_waits_held")
        s_eps = sem("eps_set")
        s_wgh = sem("gate_weights_high")
        s_gz = sem("gate_magnitude")
        s_scan = sem("running_max")
        s_rbl = sem("rows_split")
        s_kr = sem("shared_keys_high")
        s_res = sem("residual_added")
        s_rt2 = sem("residual_scaled")
        s_dve = sem("vector_chain")
        s_act = sem("scalar_chain")
        s_cr = sem("consts_rounded")
        s_wg = sem("gate_weights_split")
        s_gl = sem("gate_logits")
        s_gact = sem("gate_exp_ln")
        s_gate = sem("gates_ready")
        s_row = sem("gate_rows")
        s_rb = sem("rows_high")
        s_cond = sem("cond_ready")
        s_out = sem("out_stored")
        s_rope = sem("rope_angles")
        s_rsin = sem("rope_sines")
        s_roped = sem("rotated")
        att = {}
        for name in ("fox", "chunk", "mem", "mla"):
            att[name] = {k: sem(f"{name}_{k}") for k in (
                "qk_high", "qk_split", "v_high", "v_split", "scores", "max", "exp", "probs", "turned",
                "pt_high", "pt_split", "pv", "out", "recip")}
        s_pad = sem("queries_padded")
        cell = {k: sem(f"cell_{k}") for k in (
            "qk_high", "qk_split", "v_high", "v_split", "scores", "exp", "probs", "pt_high", "pt_split",
            "pv", "guard", "gexp", "den", "normed", "out", "square", "mean", "root")}
        ff = {}
        for name, _, _ in FFNS:
            ff[name] = {k: sem(f"{name}_{k}") for k in ("act", "hidden", "high", "split", "down", "added")}

        block = ctx.enter_context(nc.Block())

        @block.sync
        def _(sp):
            sp.dma_start(con[:], cons).then_inc(s_const, 16)
            sp.dma_start(vec[:], vecs).then_inc(s_const, 16)
            sp.dma_start(x[:], xT.rearrange("(c p) t -> p c t", p=P)).then_inc(s_x, 16)

            def load_panel(p, slot, first=False):
                if not first:
                    sp.wait_ge(s_split, p - 1)
                sp.dma_start(stage[:, slot, :], panels[p]).then_inc(s_stage[slot], 16)

            def load_piece(q, slot, first=False):
                if not first:
                    sp.wait_ge(s_pused, q - 1)
                sp.dma_start(apiece[:, slot, :], ada[q]).then_inc(s_piece[slot], 16)

            def with_pieces(p0, q0, n):
                with sp.Fori(0, n) as i:
                    for j in range(4):
                        load_panel(i * 4 + (p0 + j), j % 2)
                        load_piece(i * 8 + (q0 + 2 * j), 0)
                        load_piece(i * 8 + (q0 + 2 * j + 1), 1)

            def plain(p0, p1):
                if p1 - p0 >= 4:
                    with sp.Fori(0, (p1 - p0) // 2) as i:
                        for j in range(2):
                            load_panel(i * 2 + (p0 + j), j)
                else:
                    for p in range(p0, p1):
                        load_panel(p, p % 2)

            load_panel(0, 0, True)
            load_panel(1, 1, True)
            load_piece(0, 0, True)
            load_piece(1, 1, True)
            sp.dma_start(wgate[:], gates_w).then_inc(s_gw, 16)
            sp.dma_start(X[:].rearrange("p a b -> p (a b)"), bias).then_inc(s_bias, 16)
            for j in range(2, 4):
                load_panel(j, j % 2)
            for q in range(2, 8):
                load_piece(q, q % 2)
            with_pieces(4, 8, 5)
            sp.wait_ge(att["chunk"]["v_split"], HEADS)
            sp.dma_start(memf, memT.rearrange("(c p) t -> p c t", p=P)).then_inc(s_mem, 16)
            plain(24, PANEL0["mem_kv"])
            plain(PANEL0["mem_kv"], PANEL0["mem_q"])
            with_pieces(PANEL0["mem_q"], 48, 2)
            plain(PANEL0["mem_o"], PANEL0["a_in"])
            with_pieces(PANEL0["a_in"], 64, 6)
            sp.wait_ge(s_acol, 15)
            sp.dma_start(apiece[:].bitcast(I32)[:, 0, 0:S], pos).then_inc(s_pos, 16)
            plain(PANEL0["a_out"], NPANEL)
            sp.wait_ge(s_res, 8 * len(RESID))
            sp.dma_start(outT.rearrange("(c p) t -> p c t", p=P), x[:]).then_inc(s_out, 16)
            sp.wait_ge(s_out, 16)

        @block.gpsimd
        def _(pool):
            def split(p, i, slot, first=False):
                pool.wait_ge(s_stage[slot], 16 * i + 16)
                if not first:
                    pool.wait_ge(s_used, p - 1)
                pool.sem_inc(s_phold, 1)
                pool.tensor_copy(WH[:, slot, :], stage[:, slot, :]).then_inc(s_hisplit, 1)
                pool.wait_ge(s_hisplit, p + 1)
                pool.tensor_tensor(WL[:, slot, :], stage[:, slot, :], WH[:, slot, :].bitcast(F32),
                                   ALU.subtract).then_inc(s_split, 1)

            split(0, 0, 0, True)
            split(1, 0, 1, True)
            with pool.Fori(1, NPANEL // 2) as i:
                for slot in range(2):
                    split(i * 2 + slot, i, slot)

        @block.tensor
        def _(pe):
            def three(out, wh, wl, rh, rl, start, stop):
                pe.matmul(out, wh, rh, start=start, stop=False)
                pe.matmul(out, wh, rl, start=False, stop=False)
                return pe.matmul(out, wl, rh, start=False, stop=stop)

            def chunk_of(p, n, slot, src, width):
                pe.wait_ge(s_split, p + 1)
                pe.wait_ge(s_free, n + 1)
                for k in range(KC):
                    last = three(G[slot][:, 0:width], WH[:, slot, k * P:(k + 1) * P],
                                 WL[:, slot, k * P:(k + 1) * P], src[:, k, 0, 0:width], src[:, k, 1, 0:width],
                                 k == 0, k == KC - 1)
                last.then_inc(s_used, 1)

            def project(stage_name, proj_name, count, src=H, width=S, pieces=None):
                p0, n0 = PANEL0[stage_name], before(PROJ, proj_name)
                if pieces is None:
                    with pe.Fori(0, count // 2) as i:
                        for j in range(2):
                            chunk_of(i * 2 + (p0 + j), i * 2 + (n0 + j), j, src, width)
                else:
                    with pe.Fori(0, count // 4) as i:
                        for j in range(4):
                            chunk_of(i * 4 + (p0 + j), i * 4 + (n0 + j), j % 2, src, width)
                        ada_sum(i + pieces)

            def ada_sum(g):
                pe.wait_ge(s_pused, g * 8 + 8)
                pe.wait_ge(s_acol, g + 1)
                for m in range(KC):
                    last = pe.matmul(AD[:, m:m + 1], aacc[:, m * P:(m + 1) * P], ones[:, 0:1], start=True, stop=True)
                last.then_inc(s_asum, 1)

            def values(p0, name, tiles, src=H, pieces=None):
                banks = [T[0], T[1], O[0], O[1]]
                with pe.Fori(0, 2) as i:
                    pe.wait_ge(s_vev, i * tiles + before(VTILES, name) + 1)
                    for pp in range(4):
                        slot = pp % 2
                        pe.wait_ge(s_split, i * 4 + (p0 + pp + 1))
                        for kk in range(2):
                            k = 2 * pp + kk
                            for tt in range(tiles):
                                last = three(banks[tt][:, :], src[:, k, 0, tt * P:(tt + 1) * P],
                                             src[:, k, 1, tt * P:(tt + 1) * P], WH[:, slot, kk * S:(kk + 1) * S],
                                             WL[:, slot, kk * S:(kk + 1) * S], k == 0, k == KC - 1)
                        last.then_inc(s_used, 1)
                    if pieces is not None:
                        ada_sum(i + pieces)

            def wait_h(name):
                pe.wait_ge(s_h, before(MAKES, name) + row(MAKES, name)[1])

            def mean_square(name, width=S):
                at = [r[0] for r in STATS].index(name)
                pe.wait_ge(s_add, before(ADDS, name) + row(ADDS, name)[1])
                pe.wait_ge(s_rt, at)
                pe.matmul(ST[:, 0:width], ones, acc[:, 0:width], start=True, stop=True).then_inc(s_ms, 1)

            def gate_logits(first, n):
                for tt in range(NT):
                    for k in range(KC):
                        last = three(ST[:, 16 * tt:16 * tt + n], H[:, k, 0, tt * P:(tt + 1) * P],
                                     H[:, k, 1, tt * P:(tt + 1) * P], wgateH[:, k, first:first + n],
                                     wgateL[:, k, first:first + n], k == 0, k == KC - 1)
                last.then_inc(s_gl, 1)

            def cumulate(out, gate, stop=True):
                for st in range(NT):
                    last = pe.matmul(out[0:8, st * P:S], gate[:, st, :], upper[:, 0:S - st * P],
                                     start=st == 0, stop=stop and st == NT - 1, skip_group_check=True)
                return last

            def attention(name, heads, scores, turned_tiles, pv):
                sm = att[name]

                def score(n, slot, qb):
                    if qb == 0:
                        pe.wait_ge(sm["qk_split"], n + 1)
                    if not (isinstance(n, int) and n == 0 and qb < 2):
                        pe.wait_ge(sm["exp"], n * 4 + qb - 1)
                    scores(n, slot, qb, G[qb % 2]).then_inc(sm["scores"], 1)

                def turn(n, slot, qb):
                    pe.wait_ge(sm["probs"], n * 4 + qb + 1)
                    if not (isinstance(n, int) and n == 0 and qb < 2):
                        pe.wait_ge(sm["pt_split"], n * 4 + qb - 1)
                    for kb in range(turned_tiles(qb)):
                        last = pe.transpose(T[qb % 2][:, kb * P:(kb + 1) * P], t[:, qb % 2, kb * P:(kb + 1) * P], ident)
                    last.then_inc(sm["turned"], 1)

                def weigh(n, slot):
                    pe.wait_ge(sm["pt_split"], n * 4 + 4)
                    pe.wait_ge(sm["v_split"], n + 1)
                    if not (isinstance(n, int) and n == 0):
                        pe.wait_ge(sm["out"], n)
                    pv(n, slot).then_inc(sm["pv"], 1)

                def head(n, slot, prev):
                    score(n, slot, 0)
                    if prev:
                        turn(n - 1, 1 - slot, 3)
                    score(n, slot, 1)
                    if prev:
                        weigh(n - 1, 1 - slot)
                    turn(n, slot, 0)
                    score(n, slot, 2)
                    turn(n, slot, 1)
                    score(n, slot, 3)
                    turn(n, slot, 2)

                head(0, 0, False)
                with pe.Fori(0, (heads - 2) // 2) as i:
                    head(i * 2 + 1, 1, True)
                    head(i * 2 + 2, 0, True)
                head(heads - 1, 1, True)
                turn(heads - 1, 1, 3)
                weigh(heads - 1, 1)

            def qk(out, slot, part_, qb, kh, kl, width, start, stop):
                return three(out[:, 0:width], QS[:, slot, part_, 0, qb * P:(qb + 1) * P],
                             QS[:, slot, part_, 1, qb * P:(qb + 1) * P], kh, kl, start, stop)

            def causal_pv(n, slot):
                for kb in range(NT):
                    last = three(O[slot][:, kb * P:S], VS[:, slot, 0, kb * P:(kb + 1) * P],
                                 VS[:, slot, 1, kb * P:(kb + 1) * P], PT[:, 0, kb, kb * P:S], PT[:, 1, kb, kb * P:S],
                                 kb == 0, kb == NT - 1)
                return last

            def fox_scores(n, slot, qb, out):
                w = (qb + 1) * P
                qk(out, slot, 0, qb, KS[:, slot, 0, 0:w], KS[:, slot, 1, 0:w], w, True, False)
                pe.matmul(out[:, 0:w], onesr[0:40, :], RBS[:, slot, 0:w], start=False, stop=False)
                return pe.matmul(out[:, qb * P:w], identr[:, :], maskr[:, :], start=False, stop=True)

            def chunk_scores(n, slot, qb, out):
                w = (qb + 1) * P
                near = max(0, qb - 1) * P
                qk(out, slot, 0, qb, KS[:, slot, 0, 0:w], KS[:, slot, 1, 0:w], w, True, False)
                if near:
                    pe.matmul(out[:, 0:near], ident, Xf[:, bass.ds(n * 256, 1)].to_broadcast([P, near]),
                              start=False, stop=False)
                return pe.matmul(out[:, near:w], ident, Xf[:, bass.ds(n * 256 + (256 - (w - near)), w - near)],
                                 start=False, stop=True)

            def mem_scores(n, slot, qb, out):
                for c in range(2):
                    last = qk(out, slot, c, qb, KS[:, slot, 0, c * MEM:(c + 1) * MEM],
                              KS[:, slot, 1, c * MEM:(c + 1) * MEM], MEM, c == 0, c == 1)
                return last

            def mem_pv(n, slot):
                for dc in range(2):
                    for kb in range(2):
                        at = kb * MEM + dc * P
                        last = three(O[dc][:, :], VS[:, slot, 0, at:at + P], VS[:, slot, 1, at:at + P],
                                     PT[:, 0, kb, :], PT[:, 1, kb, :], kb == 0, kb == 1)
                return last

            def mla_scores(n, slot, qb, out):
                w = (qb + 1) * P
                qk(out, slot, 0, qb, KS[:, slot, 0, 0:w], KS[:, slot, 1, 0:w], w, True, False)
                qk(out, slot, 1, qb, KR[:, 0, 0:w], KR[:, 1, 0:w], w, False, False)
                return pe.matmul(out[:, qb * P:w], identr[:, :], maskr[:, :], start=False, stop=True)

            def feed_forward(name, groups, gated):
                sm = ff[name]
                banks = [G[0], G[1], ST, AD] if gated else [G[0], None, G[1], None]
                per = 2 if gated else 1

                def up(g, slot):
                    p = ff_up(name, g)
                    for j in range(2):
                        for u in range(per):
                            q = j * per + u
                            pe.wait_ge(s_split, p + (q + 1))
                            if not (isinstance(g, int) and g == 0):
                                pe.wait_ge(sm["hidden"], g * 2 + j - 1)
                            for k in range(KC):
                                last = three(banks[2 * j + u][:, :], WH[:, q % 2, k * P:(k + 1) * P],
                                             WL[:, q % 2, k * P:(k + 1) * P], H[:, k, 0, :], H[:, k, 1, :],
                                             k == 0, k == KC - 1)
                            last.then_inc(s_used, 1)

                def down(g, slot, last_group=False):
                    p = ff_down(name, g, last_group)
                    pe.wait_ge(sm["split"], g * 2 + 2)
                    pe.wait_ge(s_split, p + 2)
                    for m in range(KC):
                        pe.wait_ge(sm["added"], g * 8 + (m + 1))
                        for j in range(2):
                            last = three((T + O)[m % 4][:, :], WH[:, j, m * P:(m + 1) * P], WL[:, j, m * P:(m + 1) * P],
                                         HID[:, slot, j, 0, :], HID[:, slot, j, 1, :], j == 0, j == 1)
                            if m == KC - 1 and j == 0:
                                last.then_inc(s_used, 1)
                        last.then_inc(sm["down"] if m < KC - 1 else s_used, 1)

                up(0, 0)
                with pe.Fori(0, (groups - 1) // 2) as i:
                    up(i * 2 + 1, 1)
                    down(i * 2, 0)
                    up(i * 2 + 2, 0)
                    down(i * 2 + 1, 1)
                if groups % 2 == 0:
                    up(groups - 1, 1)
                    down(groups - 2, 0)
                down(groups - 1, (groups - 1) % 2, True)

            def small_project(p0, n0, chunks, ks, per_panel):
                for c in range(chunks):
                    p, at = p0 + c // per_panel, c % per_panel
                    slot, n = p % 2, n0 + c
                    if at == 0:
                        pe.wait_ge(s_split, p + 1)
                    pe.wait_ge(s_free, n + 1)
                    for k in range(ks):
                        w = (at * ks + k) * P
                        last = three(G[n % 2][:, :], WH[:, slot, w:w + P], WL[:, slot, w:w + P],
                                     H[:, k, 0, :], H[:, k, 1, :], k == 0, k == ks - 1)
                    last.then_inc(s_used if at == per_panel - 1 or c == chunks - 1 else s_proj, 1)

            pe.wait_ge(s_const, 32)
            mean_square("x")
            wait_h("x")
            project("w_in", "w_in", 16, pieces=0)
            values(PANEL0["w_in"] + 16, "w_in", NT, pieces=4)
            pe.wait_ge(s_wg, 1)
            gate_logits(0, 8)
            pe.wait_ge(s_gate, 1)
            pe.wait_ge(s_vev, 2 * NT + 1)
            cumulate(T[0], lf).then_inc(s_row, 1)
            pe.wait_ge(s_cr, 1)
            pe.wait_ge(s_rbl, 1)
            attention("fox", HEADS, fox_scores, lambda qb: qb + 1, causal_pv)
            pe.wait_ge(s_bias, 16)
            attention("chunk", HEADS, chunk_scores, lambda qb: qb + 1, causal_pv)
            mean_square("fox")
            mean_square("chunk")
            mean_square("mem", MEM)
            wait_h("o_chunk")
            project("w_out", "w_out", 8)
            wait_h("mem")
            project("mem_kv", "mem_k", 8, HM, MEM)
            mean_square("mix")
            values(PANEL0["mem_kv"] + 8, "mem", 2, HM)
            mean_square("x_mem")
            wait_h("x_mem")
            project("mem_q", "mem_q", 8, pieces=6)
            attention("mem", 4, mem_scores, lambda qb: 2, mem_pv)
            wait_h("o_mem")
            project("mem_o", "mem_o", 8)
            mean_square("ca")
            mean_square("x_ffn")
            wait_h("x_ffn")
            feed_forward(*FFNS[0])
            mean_square("ffn")
            mean_square("x_a")
            wait_h("x_a")
            project("a_in", "a_in", 16, pieces=8)
            values(PANEL0["a_in"] + 16, "a_in", NT, pieces=12)
            gate_logits(8, 16)
            pe.wait_ge(s_gate, 2)
            pe.wait_ge(s_vev, before(VTILES, "kv_b") + 1)
            cumulate(T[0], gz, stop=False)
            for tt in range(NT):
                last = pe.matmul(T[0][0:8, tt * P:(tt + 1) * P], gi[:, tt, :], ident, start=False, stop=tt == NT - 1,
                                 skip_group_check=True)
            last.then_inc(s_row, 1)
            cumulate(T[1], lf).then_inc(s_row, 1)
            for tt in range(NT):
                for st in range(tt + 1):
                    pe.matmul(O[0][:, tt * 8:tt * 8 + 8], upper[:, 0:P] if st == tt else ones, gz[:, st, :],
                              start=st == 0, stop=False)
                last = pe.matmul(O[0][:, tt * 8:tt * 8 + 8], ident, gi[:, tt, :], start=False, stop=True)
            last.then_inc(s_row, 1)
            pe.wait_ge(s_rbl, 2)

            def cell_head(n, slot):
                pe.wait_ge(cell["qk_split"], n + 1)
                for kb in range(NT):
                    w = S - kb * P
                    if not (isinstance(n, int) and n == 0 and kb < 2):
                        pe.wait_ge(cell["probs"], n * 4 + kb - 1)
                    three(G[kb % 2][:, 0:w], KS[:, slot, 0, kb * P:(kb + 1) * P], KS[:, slot, 1, kb * P:(kb + 1) * P],
                          QS[:, slot, 0, 0, kb * P:S], QS[:, slot, 0, 1, kb * P:S], True, True)
                    pe.matmul(T[kb % 2][:, 0:w], onesr[0:40, :], RBS[:, slot, kb * P:S], start=True, stop=False)
                    pe.matmul(T[kb % 2][:, 0:P], identr[:, :], maskTr[:, :], start=False, stop=True)\
                        .then_inc(cell["scores"], 1)
                if not (isinstance(n, int) and n == 0):
                    pe.wait_ge(cell["out"], n)
                pe.matmul(AD[:, :], ones[0:8, :], aacc[0:8, slot * S:(slot + 1) * S], start=True, stop=True).then_inc(cell["guard"], 1)
                pe.wait_ge(cell["v_split"], n + 1)
                for kb in range(NT):
                    pe.wait_ge(cell["pt_split"], n * 4 + kb + 1)
                    three(O[0][:, kb * P:S], VS[:, slot, 0, kb * P:(kb + 1) * P], VS[:, slot, 1, kb * P:(kb + 1) * P],
                          PT[:, 0, kb, kb * P:S], PT[:, 1, kb, kb * P:S], kb == 0, kb == NT - 1)
                    for hl in range(2):
                        last = pe.matmul(O[1][:, kb * P:S], onesr[:, :], PT[:, hl, kb, kb * P:S],
                                         start=kb == 0 and hl == 0, stop=kb == NT - 1 and hl == 1)
                last.then_inc(cell["pv"], 1)

            cell_head(0, 0)
            cell_head(1, 1)
            with pe.Fori(1, HEADS // 2) as i:
                cell_head(i * 2, 0)
                cell_head(i * 2 + 1, 1)
            for h in range(HEADS):
                pe.wait_ge(cell["square"], h + 1)
                if h:
                    pe.wait_ge(cell["root"], h)
                pe.matmul(ST[:, :], ones, sq[:, h % 2, :], start=True, stop=True).then_inc(cell["mean"], 1)
            wait_h("cells")
            project("a_out", "a_out", 8)
            mean_square("a")
            mean_square("x_mlp0")
            wait_h("x_mlp0")
            feed_forward(*FFNS[1])
            mean_square("mlp0")
            mean_square("x_b")
            wait_h("x_kv")
            small_project(PANEL0["kv_a"], before(PROJ, "kv_a"), 3, 8, 1)
            mean_square("c_kv")
            wait_h("c_kv")
            small_project(PANEL0["kv_b"], before(PROJ, "k_nope"), 8, 2, 4)
            for half in range(2):
                p = PANEL0["kv_b"] + 2 + half
                pe.wait_ge(s_split, p + 1)
                pe.wait_ge(s_vev, before(VTILES, "kv_b") + half * NT + 1)
                for k in range(2):
                    for tt in range(NT):
                        last = three((T + O)[tt][:, :], H[:, k, 0, tt * P:(tt + 1) * P],
                                     H[:, k, 1, tt * P:(tt + 1) * P], WH[:, p % 2, k * S:(k + 1) * S],
                                     WL[:, p % 2, k * S:(k + 1) * S], k == 0, k == 1)
                last.then_inc(s_used, 1)
            wait_h("x_b")
            small_project(PANEL0["q_a"], before(PROJ, "q_a"), 3, 8, 1)
            mean_square("c_q")
            wait_h("c_q")
            small_project(PANEL0["q_b"], before(PROJ, "q_nope"), 8, 3, 2)
            small_project(PANEL0["q_b"] + 4, before(PROJ, "q_rope"), 4, 3, 2)
            pe.wait_ge(s_vev, before(VTILES, "kv_b") + 2 * NT + 1)
            attention("mla", HEADS, mla_scores, lambda qb: qb + 1, causal_pv)
            wait_h("o_b")
            project("b_out", "b_out", 8)
            mean_square("b")
            mean_square("x_mlp1")
            wait_h("x_mlp1")
            feed_forward(*FFNS[2])
            mean_square("mlp1")

        def staged_qk(name, n, pair, slot):
            rows = half_rows[slot]
            if name == "fox":
                return [(QK[rows, pair, :], QS[rows, slot, 0, 0, :], QS[rows, slot, 0, 1, :], 0.125),
                        (QK[:, pair + 4, :], KS[:, slot, 0, :], KS[:, slot, 1, :], 1.0)]
            if name == "chunk":
                return [(QK[rows, pair + 8, :], QS[rows, slot, 0, 0, :], QS[rows, slot, 0, 1, :], 0.125),
                        (QK[:, pair + 12, :], KS[:, slot, 0, :], KS[:, slot, 1, :], 1.0)]
            if name == "mem":
                return [(QK[:, bass.ds(n * 2, 2), :], QS[:, slot, :, 0, :], QS[:, slot, :, 1, :], 256 ** -0.5),
                        (QKf[:, bass.ds(n * S + 8 * S, S)], KS[:, slot, 0, :], KS[:, slot, 1, :], 1.0)]
            return [(QK[:, n, :], QS[:, slot, 0, 0, :], QS[:, slot, 0, 1, :], 192 ** -0.5),
                    (X[rows, pair, :], QS[rows, slot, 1, 0, :], QS[rows, slot, 1, 1, :], 192 ** -0.5),
                    (QK[:, n + 8, :], KS[:, slot, 0, :], KS[:, slot, 1, :], 1.0)]

        def staged_v(name, n, pair, slot):
            if name == "mem":
                wide = dict(b=MEM)
                src = V[:, 2:4, bass.ds(n * MEM, MEM)]
            else:
                wide = dict(b=P)
                src = V[:, :, bass.ds(pair * P + (S if name == "chunk" else 0), P) if name in ("fox", "chunk")
                        else bass.ds(n * P, P)]
            return [(src, VS[:, slot, 0, :].rearrange("p (a b) -> p a b", **wide),
                     VS[:, slot, 1, :].rearrange("p (a b) -> p a b", **wide), 1.0)]

        def cell_qk(n, pair, slot):
            rows = half_rows[slot]
            return [(QK[rows, pair, :], QS[rows, slot, 0, 0, :], QS[rows, slot, 0, 1, :], 0.125),
                    (QK[:, pair + 4, :], KS[:, slot, 0, :], KS[:, slot, 1, :], 1.0)]

        def keys_of(name, qb):
            return MEM if name == "mem" else (qb + 1) * P

        value_banks = [T[0], T[1], O[0], O[1]]

        @block.scalar
        def _(act):
            def hold():
                act.sem_inc(s_hold, 1)

            def squares(name, source, ready, width=S):
                at = [r[0] for r in STATS].index(name)
                act.wait_ge(s_rstd, at)
                for m in range(row(STATS, name)[1]):
                    ready(m)
                    act.wait_ge(s_add, before(ADDS, name) + max(m - 1, 0))
                    act.activation(sq[:, m % 2, 0:width], source(m), ACT.Square).then_inc(s_sq, 1)

            def root(name, width=S):
                at = [r[0] for r in STATS].index(name)
                act.wait_ge(s_ms, at + 1)
                act.activation(sq[:, 0, 0:width], ST[:, 0:width], ACT.Sqrt, bias=eps[:, :],
                               scale=1.0 / row(STATS, name)[2]).then_inc(s_rt, 1)

            def high(name, source, dest, shift=None):
                _, count, normed = row(MAKES, name)
                h0, t0 = before(MAKES, name), before(MAKES_T, name)
                for m in range(count):
                    if normed:
                        act.wait_ge(s_t, t0 + m + 1)
                        act.activation(dest(m), t[:, m % 2, 0:dest(m).shape[-1]], ACT.Identity, bias=shift(m))\
                            .then_inc(s_hi, 1)
                    else:
                        act.activation(dest(m), source(m), ACT.Copy).then_inc(s_hi, 1)

            def evacuate(stage_name, name, count, dest, width=S, first=0, func=ACT.Copy):
                p0 = PANEL0[stage_name] + first
                with act.Fori(0, count // 2) as i:
                    for j in range(2):
                        act.wait_ge(s_used, i * 2 + (p0 + j + 1))
                        hold()
                        act.activation(dest(i * 2 + j), G[j][:, 0:width], func).then_inc(s_free, 1)

            def evacuate_values(p0, tiles, first=0):
                with act.Fori(0, 2) as i:
                    act.wait_ge(s_used, i * 4 + (p0 + 4))
                    hold()
                    for tt in range(tiles):
                        act.activation(V[:, first + tt, bass.ds(i * S, S)], value_banks[tt][:, :], ACT.Copy)\
                            .then_inc(s_vev, 1)

            def evacuated(name):
                act.wait_ge(s_free, before(PROJ, name) + row(PROJ, name)[1] + 2)

            def attention(name, heads, out_of):
                sm = att[name]

                def stage_qk(n, pair, slot, early=False):
                    if not early:
                        act.wait_ge(sm["scores"], n * 4 - 4)
                    hold()
                    for source, hi, _, scale in staged_qk(name, n, pair, slot):
                        last = act.activation(hi, source, ACT.Copy, scale=scale)
                    last.then_inc(sm["qk_high"], 1)

                def stage_v(n, pair, slot, early=False):
                    if not early:
                        act.wait_ge(sm["pv"], n - 1)
                    hold()
                    for source, hi, _, _ in staged_v(name, n, pair, slot):
                        act.activation(hi, source, ACT.Copy).then_inc(sm["v_high"], 1)

                def exp(n, qb):
                    if not (isinstance(n, int) and n == 0 and qb < 2):
                        act.wait_ge(sm["turned"], n * 4 + qb - 1)
                    act.wait_ge(sm["max"], n * 4 + qb + 1)
                    w = keys_of(name, qb)
                    act.activation(t[:, qb % 2, 0:w], G[qb % 2][:, 0:w], ACT.Exp, bias=stat[:, qb:qb + 1],
                                   accum_out=stat[:, 4 + qb:5 + qb]).then_inc(sm["exp"], 1)

                def pt_high(n, qb):
                    act.wait_ge(sm["turned"], n * 4 + qb + 1)
                    if qb == 0 and not (isinstance(n, int) and n == 0):
                        act.wait_ge(sm["pv"], n)
                    w = keys_of(name, qb)
                    act.activation(PT[:, 0, 0:w // P, qb * P:(qb + 1) * P],
                                   T[qb % 2][:, 0:w].rearrange("p (k q) -> p k q", q=P), ACT.Copy)\
                        .then_inc(sm["pt_high"], 1)

                def out(n, pair, slot):
                    act.wait_ge(sm["pv"], n + 1)
                    hold()
                    for dest, source in out_of(n, pair, slot):
                        last = act.activation(dest, source, ACT.Copy)
                    last.then_inc(sm["out"], 1)

                def head(n, pair, slot, prev, nxt, prev_pair, next_pair):
                    early = isinstance(n, int) and n == 0
                    exp(n, 0)
                    if prev:
                        pt_high(n - 1, 3)
                    if nxt:
                        stage_qk(n + 1, next_pair, 1 - slot, early)
                    exp(n, 1)
                    if prev:
                        out(n - 1, prev_pair, 1 - slot)
                    if nxt:
                        stage_v(n + 1, next_pair, 1 - slot, early)
                    pt_high(n, 0)
                    exp(n, 2)
                    pt_high(n, 1)
                    exp(n, 3)
                    pt_high(n, 2)

                stage_qk(0, 0, 0, True)
                stage_v(0, 0, 0, True)
                head(0, 0, 0, False, True, None, 0)
                with act.Fori(0, (heads - 2) // 2) as i:
                    head(i * 2 + 1, i, 1, True, True, i, i + 1)
                    head(i * 2 + 2, i + 1, 0, True, True, i, i + 1)
                head(heads - 1, heads // 2 - 1, 1, True, False, heads // 2 - 1, None)
                pt_high(heads - 1, 3)
                out(heads - 1, heads // 2 - 1, 1)

            def half_out(base):
                return lambda n, pair, slot: [(Y[half_rows[slot], pair + base, :], O[slot][half_rows[slot], :])]

            def feed_forward(name, groups, gated):
                sm = ff[name]
                banks = [G[0], None, ST, None] if gated else [G[0], None, G[1], None]
                per = 2 if gated else 1
                size = 6 if gated else 4

                def activate(g):
                    p = ff_up(name, g)
                    for j in range(2):
                        act.wait_ge(s_used, p + (j * per + 1))
                        if not (isinstance(g, int) and g == 0):
                            act.wait_ge(sm["split"], g * 2 + j - 1)
                        act.activation(t[:, j, :], banks[2 * j][:, :], ACT.Silu if gated else ACT.Relu)\
                            .then_inc(sm["act"], 1)

                def hidden_high(g, slot):
                    for j in range(2):
                        act.wait_ge(sm["hidden"], g * 2 + j + 1)
                        act.wait_ge(s_used, g * size + (PANEL0[name] - 2))
                        act.activation(HID[:, slot, j, 0, :], t[:, j, :], ACT.Copy).then_inc(sm["high"], 1)

                activate(0)
                hidden_high(0, 0)
                with act.Fori(0, (groups - 1) // 2) as i:
                    activate(i * 2 + 1)
                    hidden_high(i * 2 + 1, 1)
                    activate(i * 2 + 2)
                    hidden_high(i * 2 + 2, 0)
                if groups % 2 == 0:
                    activate(groups - 1)
                    hidden_high(groups - 1, 1)

            def after_residual(name):
                base = 8 * RESID.index(name)
                return lambda m: act.wait_ge(s_res, base + m + 1)

            def once(sem_, value):
                return lambda m: act.wait_ge(sem_, value)

            def xc(m):
                return x[:, m, :]

            def yc(m):
                return Y[:, m, :]

            def hh(m):
                return H[:, m, 0, :]

            act.wait_ge(s_const, 32)
            act.wait_ge(s_eps, 1)
            act.activation(identr[:], ident, ACT.Copy).then_inc(s_free, 1)
            act.activation(onesr[:], ones, ACT.Copy).then_inc(s_free, 1)
            act.activation(maskr[:], con[:, CON["mask"]:CON["mask"] + P], ACT.Copy).then_inc(s_vev, 1)
            act.activation(maskTr[:], con[:, CON["maskT"]:CON["maskT"] + P], ACT.Copy).then_inc(s_cr, 1)
            act.activation(cond[:], vec[:, VEC["c"]:VEC["c"] + 8], ACT.Silu).then_inc(s_cond, 1)
            squares("x", xc, once(s_x, 16))
            root("x")
            high("x", None, hh, lambda m: col("zero"))
            evacuate("w_in", "w_in", 16, lambda c: QK[:, c, :])
            evacuate_values(PANEL0["w_in"] + 16, NT)
            act.wait_ge(s_gw, 16)
            act.activation(wgateH[:], wgate[:], ACT.Copy).then_inc(s_wgh, 1)
            act.wait_ge(s_gz, 1)
            act.activation(gw[:], gw[:], ACT.Exp).then_inc(s_gact, 1)
            act.wait_ge(s_gact, 1)
            act.activation(gw[:], gw[:], ACT.Ln, bias=1.0).then_inc(s_gact, 1)
            act.wait_ge(s_row, 1)
            act.wait_ge(s_pad, 2)
            act.activation(RB[0:8, :], T[0][0:8, :], ACT.Copy).then_inc(s_rb, 1)
            attention("fox", HEADS, half_out(0))
            attention("chunk", HEADS, half_out(4))
            act.wait_ge(att["chunk"]["out"], HEADS)
            squares("fox", yc, once(att["fox"]["out"], HEADS))
            root("fox")
            high("o_fox", None, hh, lambda m: col("zero"))
            squares("chunk", lambda m: yc(m + 4), lambda m: None)
            root("chunk")
            high("o_chunk", None, lambda m: hh(4 + m), lambda m: col("zero"))
            squares("mem", lambda m: memf[:, m, :], once(s_mem, 16), MEM)
            root("mem", MEM)
            high("mem", None, lambda m: HM[:, m, 0, :], lambda m: col("zero"))
            evacuate("w_out", "w_out", 8, lambda c: Y[:, c, :])
            evacuated("w_out")
            squares("mix", yc, lambda m: None)
            evacuate("mem_kv", "mem_k", 8, lambda c: memK[:, c, :], MEM)
            root("mix")
            squares("x_mem", xc, after_residual("mix"))
            evacuate_values(PANEL0["mem_kv"] + 8, 2, 2)
            root("x_mem")
            high("x_mem", None, hh, lambda m: col("zero"))
            evacuate("mem_q", "mem_q", 8, lambda c: QK[:, c, :])
            evacuated("mem_q")
            attention("mem", 4, lambda n, pair, slot: [(Y[:, n * 2 + c, :], O[c][:, :]) for c in range(2)])
            act.wait_ge(att["mem"]["out"], 4)
            high("o_mem", yc, hh)
            evacuate("mem_o", "mem_o", 8, lambda c: Y[:, c, :])
            evacuated("mem_o")
            squares("ca", yc, lambda m: None)
            root("ca")
            squares("x_ffn", xc, after_residual("ca"))
            root("x_ffn")
            high("x_ffn", None, hh, lambda m: col("zero"))
            feed_forward(*FFNS[0])
            squares("ffn", yc, once(ff["ffn"]["added"], 8 * FFNS[0][1] + 4))
            root("ffn")
            squares("x_a", xc, after_residual("ffn"))
            root("x_a")
            high("x_a", None, hh, lambda m: adac[:, SH1 * 8 + m:SH1 * 8 + m + 1])
            evacuate("a_in", "a_in", 8, lambda c: QK[:, c, :])
            evacuate("a_in", "a_in", 8, lambda c: QK[:, c + 8, :], first=8, func=ACT.Sigmoid)
            evacuate_values(PANEL0["a_in"] + 16, NT)
            act.wait_ge(s_gz, 2)
            act.activation(gw[:], gw[:], ACT.Exp).then_inc(s_gact, 1)
            act.wait_ge(s_gact, 3)
            act.activation(gw[:], gw[:], ACT.Ln, bias=1.0).then_inc(s_gact, 1)
            act.wait_ge(s_scan, 1)
            act.activation(RB[0:8, :], t[0:8, 0, :], ACT.Copy).then_inc(s_rb, 1)

            def cell_stage(n, pair, slot, early=False):
                if not early:
                    act.wait_ge(cell["scores"], n * 4 - 4)
                hold()
                for source, hi, _, scale in cell_qk(n, pair, slot):
                    last = act.activation(hi, source, ACT.Copy, scale=scale)
                last.then_inc(cell["qk_high"], 1)

            def cell_stage_v(n, slot, early=False):
                if not early:
                    act.wait_ge(cell["pv"], n - 1)
                hold()
                for source, hi, _, _ in staged_v("cell", n, None, slot):
                    act.activation(hi, source, ACT.Copy).then_inc(cell["v_high"], 1)

            def cell_head(n, pair, slot, nxt=True):
                zero = isinstance(n, int) and n == 0

                def weight(kb):
                    if not (zero and kb < 2):
                        act.wait_ge(cell["probs"], n * 4 + kb - 1)
                    act.wait_ge(cell["scores"], n * 4 + kb + 1)
                    hold()
                    act.activation(sq[:, kb % 2, 0:S - kb * P], T[kb % 2][:, 0:S - kb * P], ACT.Exp,
                                   bias=gsf[:, bass.ds(n + kb * 8, 1)]).then_inc(cell["exp"], 1)

                def pt_high(kb):
                    if kb == 0 and not zero:
                        act.wait_ge(cell["pv"], n)
                    act.wait_ge(cell["probs"], n * 4 + kb + 1)
                    act.activation(PT[:, 0, kb, kb * P:S], t[:, kb % 2, 0:S - kb * P], ACT.Copy)\
                        .then_inc(cell["pt_high"], 1)

                weight(0)
                weight(1)
                pt_high(0)
                if nxt:
                    cell_stage(n + 1, pair if slot == 0 else pair + 1, 1 - slot, zero)
                weight(2)
                pt_high(1)
                weight(3)
                pt_high(2)
                if nxt:
                    cell_stage_v(n + 1, 1 - slot, zero)
                pt_high(3)
                act.wait_ge(cell["guard"], n + 1)
                if not zero:
                    act.wait_ge(cell["out"], n)
                act.activation(X[:, 0, :], AD[:, :], ACT.Exp).then_inc(cell["gexp"], 1)

            cell_stage(0, 0, 0, True)
            cell_stage_v(0, 0, True)
            cell_head(0, 0, 0)
            with act.Fori(0, (HEADS - 2) // 2) as i:
                cell_head(i * 2 + 1, i, 1)
                cell_head(i * 2 + 2, i + 1, 0)
            cell_head(HEADS - 1, HEADS // 2 - 1, 1, False)
            act.wait_ge(cell["out"], HEADS)

            def cell_square(h):
                if h >= 2:
                    act.wait_ge(cell["mean"], h - 1)
                act.activation(sq[:, h % 2, :], Y[:, h, :], ACT.Square).then_inc(cell["square"], 1)

            cell_square(0)
            for h in range(HEADS):
                if h + 1 < HEADS:
                    cell_square(h + 1)
                act.wait_ge(cell["mean"], h + 1)
                if h >= 2:
                    act.wait_ge(cell["normed"], h - 1)
                act.activation(X[:, h % 2, :], ST[:, :], ACT.Sqrt, bias=eps[:, :], scale=1.0 / P)\
                    .then_inc(cell["root"], 1)
            act.wait_ge(cell["normed"], HEADS)
            high("cells", yc, hh)
            evacuate("a_out", "a_out", 8, lambda c: Y[:, c, :])
            evacuated("a_out")
            squares("a", yc, lambda m: None)
            root("a")
            squares("x_mlp0", xc, after_residual("a"))
            root("x_mlp0")
            high("x_mlp0", None, hh, lambda m: adac[:, SH2 * 8 + m:SH2 * 8 + m + 1])
            feed_forward(*FFNS[1])
            squares("mlp0", yc, once(ff["mlp0"]["added"], 8 * FFNS[1][1] + 4))
            root("mlp0")
            act.wait_ge(s_rope, 1)
            act.activation(sin, ropeA, ACT.Sin, scale=con[:, CON["rope_sign"]:CON["rope_sign"] + 1]).then_inc(s_rsin, 1)
            act.activation(cos, ropeB, ACT.Sin).then_inc(s_rsin, 1)
            squares("x_b", xc, after_residual("mlp0"))
            root("x_b")
            high("x_kv", None, hh, lambda m: adac[:, KVSH * 8 + m:KVSH * 8 + m + 1])

            def evacuate_small(p0, name, chunks, per_panel, proj0, dest, swap=None):
                n0, passed = before(PROJ, name), 0
                for c in range(chunks):
                    if c % per_panel == per_panel - 1 or c == chunks - 1:
                        act.wait_ge(s_used, p0 + c // per_panel + 1)
                    else:
                        passed += 1
                        act.wait_ge(s_proj, proj0 + passed)
                    last = act.activation(dest(c), G[(n0 + c) % 2][:, :], ACT.Copy)
                    turned = swap(c) if swap else None
                    if turned is not None:
                        for b in range(4):
                            r = b ^ 1
                            last = act.activation(turned[32 * r:32 * r + 32, :],
                                                  G[(n0 + c) % 2][32 * b:32 * b + 32, :], ACT.Copy)
                    last.then_inc(s_free, 1)

            act.wait_ge(s_rsin, 2)
            evacuate_small(PANEL0["kv_a"], "kv_a", 3, 1, 0, yc, lambda c: swapped[0] if c == 2 else None)
            evacuated("kv_a")
            squares("c_kv", yc, lambda m: None)
            act.wait_ge(s_roped, 1)
            act.activation(KR[:, 0, :], Y[:, 2, :], ACT.Copy).then_inc(s_kr, 1)
            root("c_kv")
            high("c_kv", None, hh, lambda m: col("zero"))
            evacuate_small(PANEL0["kv_b"], "k_nope", 8, 4, 0, lambda c: QK[:, 8 + c, :])
            for half in range(2):
                act.wait_ge(s_used, PANEL0["kv_b"] + 3 + half)
                for tt in range(NT):
                    act.activation(V[:, tt, half * S:(half + 1) * S], value_banks[tt][:, :], ACT.Copy)\
                        .then_inc(s_vev, 1)
            high("x_b", None, hh, lambda m: adac[:, (LAYER1 + SH1) * 8 + m:(LAYER1 + SH1) * 8 + m + 1])
            evacuate_small(PANEL0["q_a"], "q_a", 3, 1, 0, lambda c: Y[:, 3 + c, :])
            evacuated("q_a")
            squares("c_q", lambda m: Y[:, 3 + m, :], lambda m: None)
            root("c_q")
            high("c_q", None, hh, lambda m: col("zero"))
            evacuate_small(PANEL0["q_b"], "q_nope", 8, 2, 6, lambda c: QK[:, c, :])

            def swap_q(c):
                if c >= 2:
                    act.wait_ge(s_roped, c)
                return swapped[c % 2]

            evacuate_small(PANEL0["q_b"] + 4, "q_rope", 4, 2, 10, lambda c: X[:, c, :], swap_q)
            act.wait_ge(s_roped, 5)
            act.wait_ge(s_pad, 4)
            attention("mla", HEADS, lambda n, pair, slot: [(Y[:, n, :], O[slot][:, :])])
            act.wait_ge(att["mla"]["out"], HEADS)
            high("o_b", yc, hh)
            evacuate("b_out", "b_out", 8, lambda c: Y[:, c, :])
            evacuated("b_out")
            squares("b", yc, lambda m: None)
            root("b")
            squares("x_mlp1", xc, after_residual("b"))
            root("x_mlp1")
            high("x_mlp1", None, hh, lambda m: adac[:, (LAYER1 + SH2) * 8 + m:(LAYER1 + SH2) * 8 + m + 1])
            feed_forward(*FFNS[2])
            squares("mlp1", yc, once(ff["mlp1"]["added"], 8 * FFNS[2][1] + 4))
            root("mlp1")

        @block.vector
        def _(dve):
            chain = Chain(dve, s_dve)

            def low(out, source, hi, scale=1.0):
                return dve.scalar_tensor_tensor(out, source, scale, hi.bitcast(F32), ALU.mult, ALU.subtract)

            def add_squares(name, width=S):
                at = [r[0] for r in STATS].index(name)
                count, base = row(STATS, name)[1], before(ADDS, name)
                dve.wait_ge(s_ms, at)
                for m in range(1, count):
                    dve.wait_ge(s_sq, before(STATS, name) + m + 1)
                    first = sq[:, 0, 0:width] if m == 1 else acc[:, 0:width]
                    dve.tensor_tensor(acc[:, 0:width], first, sq[:, m % 2, 0:width], ALU.add).then_inc(s_add, 1)
                    dve.wait_ge(s_add, base + m)

            def invert(name, width=S):
                at = [r[0] for r in STATS].index(name)
                dve.wait_ge(s_rt, at + 1)
                dve.reciprocal(rstd[:, 0:width], sq[:, 0, 0:width]).then_inc(s_rstd, 1)
                dve.wait_ge(s_rstd, at + 1)

            def make_scaled(name, source, gain, dest, shift, after=0, width=S, inv=None):
                _, count, _ = row(MAKES, name)
                h0, t0 = before(MAKES, name), before(MAKES_T, name)
                scale_by = rstd if inv is None else inv
                dve.wait_ge(s_used, after)

                def lows(m):
                    dve.wait_ge(s_hi, h0 + m + 1)
                    dve.scalar_tensor_tensor(dest(m), t[:, m % 2, 0:width], shift(m),
                                             dest_hi(m, name), ALU.add, ALU.subtract).then_inc(s_h, 1)

                for m in range(count):
                    if m >= 2:
                        dve.wait_ge(s_h, h0 + m - 1)
                    dve.scalar_tensor_tensor(t[:, m % 2, 0:width], source(m), gain(m), scale_by[:, 0:width],
                                             ALU.mult, ALU.mult).then_inc(s_t, 1)
                    dve.wait_ge(s_t, t0 + m + 1)
                    if m:
                        lows(m - 1)
                lows(count - 1)
                dve.wait_ge(s_h, h0 + count)

            def dest_hi(m, name):
                if name == "mem":
                    return HM[:, m, 0, :].bitcast(F32)
                return H[:, m + 4 if name == "o_chunk" else m, 0, :].bitcast(F32)

            def hl(m):
                return H[:, m, 1, :]

            def make_plain(name, source):
                _, count, _ = row(MAKES, name)
                h0 = before(MAKES, name)
                for m in range(count):
                    dve.wait_ge(s_hi, h0 + m + 1)
                    dve.tensor_tensor(H[:, m, 1, :], source(m), H[:, m, 0, :].bitcast(F32), ALU.subtract)\
                        .then_inc(s_h, 1)
                dve.wait_ge(s_h, h0 + count)

            def residual(name, gain):
                base = 8 * RESID.index(name)

                def add(m):
                    dve.tensor_tensor(x[:, m, :], x[:, m, :], t[:, m % 2, :], ALU.add).then_inc(s_res, 1)

                for m in range(KC):
                    if m >= 2:
                        dve.wait_ge(s_res, base + m - 1)
                    dve.scalar_tensor_tensor(t[:, m % 2, :], Y[:, m, :], gain(m), rstd[:, :], ALU.mult, ALU.mult)\
                        .then_inc(s_rt2, 1)
                    dve.wait_ge(s_rt2, base + m + 1)
                    if m:
                        add(m - 1)
                add(KC - 1)
                dve.wait_ge(s_res, base + KC)

            def adaptive(g0, n):
                with dve.Fori(0, n) as i:
                    for k in range(KC):
                        dve.wait_ge(s_piece[k % 2], i * 64 + 16 * (4 * g0 + k // 2 + 1))
                        if k == 0:
                            dve.tensor_scalar(aacc[:], apiece[:, 0, :], cond[:, 0:1], None, ALU.mult)\
                                .then_inc(s_pused, 1)
                        else:
                            dve.scalar_tensor_tensor(aacc[:], apiece[:, k % 2, :], cond[:, k:k + 1], aacc[:],
                                                     ALU.mult, ALU.add).then_inc(s_pused, 1)
                        dve.wait_ge(s_pused, i * 8 + (8 * g0 + k + 1))
                    dve.wait_ge(s_asum, i + (g0 + 1))
                    dve.tensor_tensor(adac[:, bass.ds(i * 8 + g0 * 8, 8)], AD[:, 0:8],
                                      vec[:, bass.ds(i * 8 + (VEC["ada_b"] + g0 * 8), 8)], ALU.add)\
                        .then_inc(s_acol, 1)
                dve.wait_ge(s_acol, g0 + n + 1)

            def one_plus(dest, scale_group, gain_col):
                chain.link(dve.scalar_tensor_tensor(dest, adac[:, scale_group * 8:scale_group * 8 + 8], 1.0,
                                                    vec[:, gain_col:gain_col + 8], ALU.add, ALU.mult))

            def gated(dest, gate_group, gain_col):
                chain.link(dve.tensor_tensor(dest, adac[:, gate_group * 8:gate_group * 8 + 8],
                                             vec[:, gain_col:gain_col + 8], ALU.mult))

            def norm_col(layer, which):
                return VEC["norm_g"] + (layer * 4 + which) * 8

            def gains(layer, group0):
                one_plus(pre_g[:, 3 * layer, :], group0 + SC1, norm_col(layer, 0))
                one_plus(pre_g[:, 3 * layer + 1, :], group0 + SC2, norm_col(layer, 2))
                gated(post_g[:, 2 * layer, :], group0 + G1, norm_col(layer, 1))
                gated(post_g[:, 2 * layer + 1, :], group0 + G2, norm_col(layer, 3))

            def log_gates(mixer, first, bias_col):
                for tt in range(NT):
                    chain.link(dve.tensor_tensor(gz[:, tt, :], ST[:, 16 * tt + first:16 * tt + first + 8],
                                                 vec[:, bias_col:bias_col + 8], ALU.add))
                dve.scalar_tensor_tensor(gw[:], gz[:], -1.0, gz[:], ALU.mult, ALU.min).then_inc(s_gz, 1)
                dve.wait_ge(s_gact, 2 * mixer + 2)
                chain.link(dve.scalar_tensor_tensor(lf[:], gz[:], 0.0, gw[:], ALU.min, ALU.subtract))

            def select_rows(dest, source, n):
                rows = source.shape[0]
                return dve.tensor_scalar(dest, source, con[0:rows, bass.ds(n + CON["minus_onehot"], 1)], None, ALU.mult)

            def attention(name, heads):
                sm = att[name]

                def stage_qk(n, pair, slot):
                    dve.wait_ge(sm["qk_high"], n + 1)
                    if name == "fox":
                        select_rows(RBS[:, slot, :], RB[:].bitcast(F32), n)
                    for source, hi, lo, scale in staged_qk(name, n, pair, slot):
                        last = low(lo, source, hi, scale)
                    last.then_inc(sm["qk_split"], 1)

                def stage_v(n, pair, slot):
                    dve.wait_ge(sm["v_high"], n + 1)
                    for source, hi, lo, _ in staged_v(name, n, pair, slot):
                        dve.tensor_tensor(lo, source, hi.bitcast(F32), ALU.subtract).then_inc(sm["v_split"], 1)

                def maximum(n, qb):
                    w = keys_of(name, qb)
                    dve.wait_ge(sm["scores"], n * 4 + qb + 1)
                    dve.tensor_reduce(stat[:, qb:qb + 1], G[qb % 2][:, 0:w], AX, ALU.max, negate=True)\
                        .then_inc(sm["max"], 1)

                def scale(n, qb):
                    w = keys_of(name, qb)
                    dve.wait_ge(sm["exp"], n * 4 + qb + 1)
                    dve.reciprocal(stat[:, 8 + qb:9 + qb], stat[:, 4 + qb:5 + qb]).then_inc(sm["recip"], 1)
                    dve.wait_ge(sm["recip"], n * 4 + qb + 1)
                    dve.tensor_scalar(t[:, qb % 2, 0:w], t[:, qb % 2, 0:w], stat[:, 8 + qb:9 + qb], None, ALU.mult)\
                        .then_inc(sm["probs"], 1)

                def pt_low(n, qb):
                    w = keys_of(name, qb)
                    dve.wait_ge(sm["pt_high"], n * 4 + qb + 1)
                    dve.tensor_tensor(PT[:, 1, 0:w // P, qb * P:(qb + 1) * P],
                                      T[qb % 2][:, 0:w].rearrange("p (k q) -> p k q", q=P),
                                      PT[:, 0, 0:w // P, qb * P:(qb + 1) * P].bitcast(F32), ALU.subtract)\
                        .then_inc(sm["pt_split"], 1)

                def head(n, slot, prev, nxt, next_pair):
                    maximum(n, 0)
                    if prev:
                        pt_low(n - 1, 3)
                    scale(n, 0)
                    maximum(n, 1)
                    if nxt:
                        stage_qk(n + 1, next_pair, 1 - slot)
                    scale(n, 1)
                    if nxt:
                        stage_v(n + 1, next_pair, 1 - slot)
                    pt_low(n, 0)
                    maximum(n, 2)
                    scale(n, 2)
                    pt_low(n, 1)
                    maximum(n, 3)
                    scale(n, 3)
                    pt_low(n, 2)

                stage_qk(0, 0, 0)
                stage_v(0, 0, 0)
                head(0, 0, False, True, 0)
                with dve.Fori(0, (heads - 2) // 2) as i:
                    head(i * 2 + 1, 1, True, True, i + 1)
                    head(i * 2 + 2, 0, True, True, i + 1)
                head(heads - 1, 1, True, False, None)
                pt_low(heads - 1, 3)

            def feed_forward(name, groups, gated_):
                sm = ff[name]
                up_banks = [G[1], AD] if gated_ else [G[0], G[1]]
                per = 2 if gated_ else 1
                dve.memset(Y[:], 0.0).then_inc(sm["added"], 4)
                dve.wait_ge(sm["added"], 4)

                def hidden(g, slot):
                    p = ff_up(name, g)
                    for j in range(2):
                        dve.wait_ge(sm["act"], g * 2 + j + 1)
                        if gated_:
                            dve.wait_ge(s_used, p + (2 * j + 2))
                            ins = dve.tensor_tensor(t[:, j, :], up_banks[j][:, :], t[:, j, :], ALU.mult)
                        else:
                            ins = dve.scalar_tensor_tensor(t[:, j, :], up_banks[j][:, :], 0.0, t[:, j, :],
                                                           ALU.max, ALU.mult)
                        ins.then_inc(sm["hidden"], 1)
                        dve.wait_ge(sm["high"], g * 2 + j + 1)
                        dve.tensor_tensor(HID[:, slot, j, 1, :], t[:, j, :], HID[:, slot, j, 0, :].bitcast(F32),
                                          ALU.subtract).then_inc(sm["split"], 1)

                def add(g, last_group=False):
                    p = ff_down(name, g, last_group)
                    for m in range(KC):
                        if m < KC - 1:
                            dve.wait_ge(sm["down"], g * 7 + (m + 1))
                        else:
                            dve.wait_ge(s_used, p + 2)
                        dve.tensor_tensor(Y[:, m, :], (T + O)[m % 4][:, :], Y[:, m, :], ALU.add)\
                            .then_inc(sm["added"], 1)

                hidden(0, 0)
                with dve.Fori(0, (groups - 1) // 2) as i:
                    hidden(i * 2 + 1, 1)
                    add(i * 2)
                    hidden(i * 2 + 2, 0)
                    add(i * 2 + 1)
                if groups % 2 == 0:
                    hidden(groups - 1, 1)
                    add(groups - 2)
                add(groups - 1, True)
                dve.wait_ge(sm["added"], groups * 8 + 4)

            def vcol(name):
                return lambda m: col(name, m)

            def adash(group):
                return lambda m: adac[:, group * 8 + m:group * 8 + m + 1]

            def preg(i):
                return lambda m: pre_g[:, i, m:m + 1]

            def postg(i):
                return lambda m: post_g[:, i, m:m + 1]

            def xc(m):
                return x[:, m, :]

            def yc(m):
                return Y[:, m, :]

            def zero(m):
                return col("zero")

            dve.memset(eps[:], EPS).then_inc(s_eps, 1)
            dve.sem_inc(s_acol, 1)
            dve.wait_ge(s_const, 32)
            add_squares("x")
            invert("x")
            make_scaled("x", xc, vcol("g_mix_pre"), hl, zero)
            dve.wait_ge(s_cond, 1)
            adaptive(0, 6)
            gains(0, 0)
            dve.wait_ge(s_wgh, 1)
            dve.tensor_tensor(wgateL[:], wgate[:], wgateH[:].bitcast(F32), ALU.subtract).then_inc(s_wg, 1)
            dve.wait_ge(s_gl, 1)
            log_gates(0, 0, VEC["b_f"])
            dve.tensor_copy(gs[:], lf[:]).then_inc(s_gate, 1)
            dve.memset(RB[:].bitcast(F32), 0.0).then_inc(s_pad, 1)
            dve.memset(QS[:].bitcast(F32), 0.0).then_inc(s_pad, 1)
            dve.wait_ge(s_rb, 1)
            dve.tensor_tensor(RB[32:40, :], T[0][0:8, :], RB[0:8, :].bitcast(F32), ALU.subtract).then_inc(s_rbl, 1)
            dve.wait_ge(s_rbl, 1)
            attention("fox", HEADS)
            attention("chunk", HEADS)
            add_squares("fox")
            invert("fox")
            make_scaled("o_fox", yc, vcol("g_out"), hl, zero)
            add_squares("chunk")
            invert("chunk")
            make_scaled("o_chunk", lambda m: Y[:, 4 + m, :], lambda m: col("g_out", 4 + m), lambda m: hl(4 + m), zero)
            add_squares("mem", MEM)
            invert("mem", MEM)
            make_scaled("mem", lambda m: memf[:, m, :], vcol("g_mem_kv"), lambda m: HM[:, m, 1, :], zero, width=MEM)
            add_squares("mix")
            invert("mix")
            residual("mix", vcol("g_mix_post"))
            add_squares("x_mem")
            invert("x_mem")
            make_scaled("x_mem", xc, vcol("g_mem_pre"), hl, zero)
            adaptive(6, 2)
            one_plus(pre_g[:, 2, :], KVSC, VEC["kv_norm_g"])
            dve.wait_ge(s_used, PANEL0["mem_o"])
            attention("mem", 4)
            make_plain("o_mem", yc)
            add_squares("ca")
            invert("ca")
            residual("ca", vcol("g_mem_post"))
            add_squares("x_ffn")
            invert("x_ffn")
            make_scaled("x_ffn", xc, vcol("g_ffn_pre"), hl, zero)
            feed_forward(*FFNS[0])
            add_squares("ffn")
            invert("ffn")
            residual("ffn", vcol("g_ffn_post"))
            add_squares("x_a")
            invert("x_a")
            make_scaled("x_a", xc, preg(0), hl, adash(SH1))
            adaptive(8, 6)
            gains(1, LAYER1)
            dve.wait_ge(s_gl, 2)
            for tt in range(NT):
                chain.link(dve.tensor_tensor(gi[:, tt, :], ST[:, 16 * tt:16 * tt + 8],
                                             vec[:, VEC["gate_b"]:VEC["gate_b"] + 8], ALU.add))
            log_gates(1, 8, VEC["gate_b"] + 8)
            dve.tensor_scalar(gz[:], lf[:], -1.0, None, ALU.mult).then_inc(s_gate, 1)
            dve.memset(QS[:].bitcast(F32), 0.0).then_inc(s_pad, 1)
            dve.wait_ge(s_row, 4)
            dve.tensor_copy(gu[0:8, :], T[0][0:8, :]).then_inc(s_dve, 1)
            chain.n += 1
            dve.wait_ge(s_dve, chain.n)
            dve.tensor_tensor_scan(t[0:8, 0, :], gu[0:8, :], gu[0:8, :], 0.0, ALU.max, ALU.max).then_inc(s_scan, 1)
            dve.wait_ge(s_scan, 1)
            chain.link(dve.tensor_tensor(X[0:8, 2, :], T[1][0:8, :], t[0:8, 0, :], ALU.add))
            chain.link(dve.tensor_copy(gs[:], O[0][:, 0:8 * NT].rearrange("p (a b) -> p a b", b=8)))
            dve.wait_ge(s_rb, 2)
            dve.tensor_tensor(RB[32:40, :], t[0:8, 0, :], RB[0:8, :].bitcast(F32), ALU.subtract).then_inc(s_rbl, 1)
            dve.wait_ge(s_rbl, 2)

            def cell_stage(n, pair, slot):
                dve.wait_ge(cell["qk_high"], n + 1)
                select_rows(RBS[:, slot, :], RB[:].bitcast(F32), n)
                select_rows(aacc[0:8, slot * S:(slot + 1) * S], X[0:8, 2, :], n)
                for source, hi, lo, scale in cell_qk(n, pair, slot):
                    last = low(lo, source, hi, scale)
                last.then_inc(cell["qk_split"], 1)

            def cell_stage_v(n, slot):
                dve.wait_ge(cell["v_high"], n + 1)
                for source, hi, lo, _ in staged_v("cell", n, None, slot):
                    dve.tensor_tensor(lo, source, hi.bitcast(F32), ALU.subtract).then_inc(cell["v_split"], 1)

            def cell_head(n, pair, slot, nxt=True):
                def weigh(kb):
                    dve.wait_ge(cell["exp"], n * 4 + kb + 1)
                    if not (isinstance(n, int) and n == 0 and kb < 2):
                        dve.wait_ge(cell["pt_split"], n * 4 + kb - 1)
                    dve.tensor_tensor(t[:, kb % 2, 0:S - kb * P], G[kb % 2][:, 0:S - kb * P],
                                      sq[:, kb % 2, 0:S - kb * P], ALU.mult).then_inc(cell["probs"], 1)

                def pt_low(kb):
                    dve.wait_ge(cell["pt_high"], n * 4 + kb + 1)
                    dve.tensor_tensor(PT[:, 1, kb, kb * P:S], t[:, kb % 2, 0:S - kb * P],
                                      PT[:, 0, kb, kb * P:S].bitcast(F32), ALU.subtract).then_inc(cell["pt_split"], 1)

                weigh(0)
                weigh(1)
                pt_low(0)
                if nxt:
                    cell_stage(n + 1, pair if slot == 0 else pair + 1, 1 - slot)
                weigh(2)
                pt_low(1)
                weigh(3)
                pt_low(2)
                if nxt:
                    cell_stage_v(n + 1, 1 - slot)
                pt_low(3)
                dve.wait_ge(cell["gexp"], n + 1)
                dve.wait_ge(cell["pv"], n + 1)
                dve.tensor_tensor(X[:, 1, :], O[1][:, :], X[:, 0, :], ALU.max).then_inc(cell["den"], 1)
                dve.wait_ge(cell["den"], n * 3 + 1)
                dve.scalar_tensor_tensor(X[:, 1, :], O[1][:, :], -1.0, X[:, 1, :], ALU.mult, ALU.max)\
                    .then_inc(cell["den"], 1)
                dve.wait_ge(cell["den"], n * 3 + 2)
                dve.reciprocal(X[:, 1, :], X[:, 1, :]).then_inc(cell["den"], 1)
                dve.wait_ge(cell["den"], n * 3 + 3)
                dve.tensor_tensor(Y[:, n, :], O[0][:, :], X[:, 1, :], ALU.mult).then_inc(cell["out"], 1)

            cell_stage(0, 0, 0)
            cell_stage_v(0, 0)
            cell_head(0, 0, 0)
            with dve.Fori(0, (HEADS - 2) // 2) as i:
                cell_head(i * 2 + 1, i, 1)
                cell_head(i * 2 + 2, i + 1, 0)
            cell_head(HEADS - 1, HEADS // 2 - 1, 1, False)
            dve.wait_ge(cell["out"], HEADS)
            for h in range(HEADS):
                dve.wait_ge(cell["root"], h + 1)
                chain.link(dve.reciprocal(X[:, h % 2, :], X[:, h % 2, :]))
                chain.link(dve.scalar_tensor_tensor(Y[:, h, :], Y[:, h, :], col("head_g", h), X[:, h % 2, :],
                                                    ALU.mult, ALU.mult))
                dve.tensor_tensor(Y[:, h, :], Y[:, h, :], QK[:, 8 + h, :], ALU.mult).then_inc(cell["normed"], 1)
            dve.wait_ge(cell["normed"], HEADS)
            make_plain("cells", yc)
            add_squares("a")
            invert("a")
            residual("a", postg(0))
            add_squares("x_mlp0")
            invert("x_mlp0")
            make_scaled("x_mlp0", xc, preg(1), hl, adash(SH2))
            feed_forward(*FFNS[1])
            add_squares("mlp0")
            invert("mlp0")
            residual("mlp0", postg(1))
            dve.wait_ge(s_pos, 16)
            chain.link(dve.tensor_copy(ropeF, apiece[:].bitcast(I32)[:, 0, 0:S]))
            chain.link(dve.tensor_scalar(ropeA, ropeF, con[:, CON["inv_freq"]:CON["inv_freq"] + 1], None, ALU.mult))
            chain.link(dve.tensor_scalar(ropeB, ropeA, 1.0 / TURN, ROUND, ALU.mult, ALU.add))
            chain.link(dve.tensor_scalar(ropeB, ropeB, ROUND, None, ALU.subtract))
            for part_of_turn in TURN_PARTS:
                chain.link(dve.scalar_tensor_tensor(ropeA, ropeB, -part_of_turn, ropeA, ALU.mult, ALU.add))
            chain.link(dve.tensor_scalar(ropeA, ropeA, PI_IN, -PI_IN, ALU.min, ALU.max))
            chain.link(dve.scalar_tensor_tensor(ropeB, ropeA, -1.0, ropeA, ALU.mult, ALU.min))
            dve.tensor_scalar(ropeB, ropeB, float(TURN / 4), None, ALU.add).then_inc(s_rope, 1)
            add_squares("x_b")
            invert("x_b")
            chain.link(dve.tensor_copy(rstd_x, rstd[:]))
            make_scaled("x_kv", xc, preg(2), hl, adash(KVSH))

            def rotate(part_, turned, count):
                chain.link(dve.tensor_tensor(part_, part_, cos, ALU.mult))
                chain.link(dve.tensor_tensor(turned, turned, sin, ALU.mult))
                dve.tensor_tensor(part_, part_, turned, ALU.add).then_inc(s_roped, 1)
                dve.wait_ge(s_roped, count)

            dve.wait_ge(s_free, before(PROJ, "kv_a") + 3 + 2)
            rotate(Y[:, 2, :], swapped[0], 1)
            dve.wait_ge(s_kr, 1)
            chain.link(dve.tensor_tensor(KR[:, 1, :], Y[:, 2, :], KR[:, 0, :].bitcast(F32), ALU.subtract))
            add_squares("c_kv")
            invert("c_kv")
            make_scaled("c_kv", yc, vcol("kv_latent_g"), hl, zero, after=PANEL0["kv_b"])
            make_scaled("x_b", xc, preg(3), hl, adash(LAYER1 + SH1), after=PANEL0["q_a"], inv=rstd_x)
            add_squares("c_q")
            invert("c_q")
            make_scaled("c_q", lambda m: Y[:, 3 + m, :], vcol("q_latent_g"), hl, zero, after=PANEL0["q_b"])
            for m in range(4):
                dve.wait_ge(s_free, before(PROJ, "q_rope") + m + 3)
                rotate(X[:, m, :], swapped[m % 2], m + 2)
            dve.wait_ge(s_used, PANEL0["b_out"])
            dve.memset(QS[:].bitcast(F32), 0.0).then_inc(s_pad, 1)
            attention("mla", HEADS)
            make_plain("o_b", yc)
            add_squares("b")
            invert("b")
            residual("b", postg(2))
            add_squares("x_mlp1")
            invert("x_mlp1")
            make_scaled("x_mlp1", xc, preg(4), hl, adash(LAYER1 + SH2))
            feed_forward(*FFNS[2])
            add_squares("mlp1")
            invert("mlp1")
            residual("mlp1", postg(3))


def _panels(w, chunks=None):
    k, n = w.shape
    return w.reshape(k // P, P, n // P, P).transpose(2, 1, 0, 3).reshape(n // P, P, k)


def _value_panels(w):
    k, n = w.shape
    return w.reshape(k // (2 * P), 2, P, n // S, S).transpose(3, 0, 2, 1, 4).reshape(-1, P, D)


def _few(w, per_panel):
    k, n = w.shape
    a = w.reshape(k // P, P, n // (P * per_panel), per_panel, P).transpose(2, 1, 3, 0, 4)
    a = a.reshape(n // (P * per_panel), P, per_panel * k)
    out = np.zeros((a.shape[0], P, D), np.float32)
    out[:, :, :a.shape[2]] = a
    return out


def _ffn_panels(up, down, per):
    first = up.reshape(-1, 2 * per, P, D)
    second = down.reshape(-1, 2, P, D)
    out = [first[0]]
    for g in range(1, len(first)):
        out += [first[g], second[g - 1]]
    return np.concatenate(out + [second[-1]])


def _cols(v):
    return np.ascontiguousarray(v.reshape(-1, P).T)


def kernel(**inputs):
    import concourse.bacc as bacc
    from concourse.bass_utils import run_bass_kernel_spmd

    a = {k: np.asarray(v) for k, v in inputs.items()}
    w_in, a_in = a["w_in"][0], a["a_w_in_2"][0]
    gu = a["w_gate_up"][0]
    gate, up = _panels(gu[:, :DFF1]), _panels(gu[:, DFF1:])
    q_b = a["b_w_q_b_2"][0].reshape(384, HEADS, 192)
    kv_b = a["kv_w_b_2"].reshape(256, HEADS, 256)
    kv_a = a["kv_w_a_2"]
    panels = np.concatenate([
        _panels(np.concatenate([w_in[:, 0:1024], w_in[:, 1544:2568]], 1)),
        _value_panels(np.concatenate([w_in[:, 1024:1536], w_in[:, 2568:3080]], 1)),
        _panels(a["w_out"][0]),
        _panels(a["w_mem_kv"][0][:, :D]), _value_panels(a["w_mem_kv"][0][:, D:]),
        _panels(a["w_mem_q"][0]), _panels(a["w_mem_o"][0]),
        _ffn_panels(np.stack([gate, up], 1), a["w_down"][0].reshape(-1, P, D), 2),
        _panels(np.concatenate([a_in[:, 0:1024], a_in[:, 2064:3088]], 1)), _value_panels(a_in[:, 1024:2048]),
        _panels(a["a_w_out_2"][0]),
        _ffn_panels(_panels(a["mlp_w1_2"][0]), a["mlp_w2_2"][0].reshape(-1, P, D), 1),
        _panels(np.concatenate([kv_a, kv_a[:, 256:]], 1)),
        _few(kv_b[:, :, :P].reshape(256, D), 4), _value_panels(kv_b[:, :, P:].reshape(256, D)),
        _panels(a["b_w_q_a_2"][0]),
        _few(q_b[:, :, :P].reshape(384, D), 2), _few(q_b[:, :, P:].reshape(384, 512), 2),
        _panels(a["b_w_out_2"][0]),
        _ffn_panels(_panels(a["mlp_w1_2"][1]), a["mlp_w2_2"][1].reshape(-1, P, D), 1),
    ])
    ada = np.concatenate([
        w.reshape(KC, P, -1, D).transpose(2, 0, 1, 3).reshape(-1, P, D)
        for w in (a["ada_w_2"][0], a["kv_ada_w_2"], a["ada_w_2"][1])])
    wide = np.ones((P, 1), np.float32)
    vecs = np.concatenate([
        _cols(a["g_mix_pre"]), _cols(np.concatenate([a["g_fox_out"][0], a["g_chunk_out"][0]])),
        _cols(a["g_mix_post"]), _cols(a["g_mem_pre"]), _cols(a["g_mem_kv"]), _cols(a["g_mem_post"]),
        _cols(a["g_ffn_pre"]), _cols(a["g_ffn_post"]), _cols(a["norm_g_2"]),
        _cols(np.concatenate([a["ada_b_2"][0], a["kv_ada_b_2"], a["ada_b_2"][1]])), _cols(a["kv_norm_g_2"]),
        _cols(a["a_head_g_2"][0]), _cols(a["kv_latent_g_2"]), _cols(a["b_q_latent_g_2"]), _cols(a["c_2"]),
        np.zeros((P, 8), np.float32), np.broadcast_to(a["b_fgate"][0], (P, 8)),
        np.broadcast_to(a["a_gate_b_2"][0].reshape(16), (P, 16))], 1)
    i = np.arange(P)
    onehot = np.zeros((P, 8), np.float32)
    onehot[:8] = -np.eye(8)
    onehot[32:40] = -np.eye(8)
    causal = np.where(i[None, :] <= i[:, None], 0.0, NEG)
    freq = 10000.0 ** (-(i % 32).astype(np.float32) / np.float32(32))
    cons = np.concatenate([
        np.eye(P), np.ones((P, P)), causal, causal.T, i[:, None] <= np.arange(S)[None, :], onehot,
        freq[:, None], np.where(i % 64 < 32, -1.0, 1.0)[:, None]], 1).astype(np.float32)
    gates_w = np.concatenate([w_in[:, 1536:1544], a_in[:, 2048:2064]], 1).reshape(KC, P, 24).transpose(1, 0, 2)
    dist = i[:, None] + P - np.arange(2 * P)[None, :]
    tile = a["rel_bias"][0][:, np.clip(dist, 1 - CH, REL) + CH - 1]
    tile = np.where((i[:, None] // CH < (np.arange(2 * P)[None, :] - P) // CH)[None], np.float32(NEG), tile)
    bias = tile.transpose(1, 0, 2).reshape(P, 2 * D)
    pos = np.broadcast_to(a["positions_2"].reshape(1, S), (P, S))
    arrays = {"xT": a["x"][0].T, "memT": a["mem"][0].T, "panels": panels, "ada": ada, "vecs": vecs, "cons": cons,
              "gates_w": gates_w, "bias": bias, "pos": pos}
    arrays = {k: np.ascontiguousarray(v) for k, v in arrays.items()}
    nc = bacc.Bacc("TRN2", target_bir_lowering=False, num_devices=1)
    args = [nc.dram_tensor(k, v.shape, mybir.dt.from_np(v.dtype), kind="ExternalInput").ap() for k, v in arrays.items()]
    out = nc.dram_tensor("outT", (D, S), F32, kind="ExternalOutput").ap()
    program(nc, *args, out)
    r = run_bass_kernel_spmd(nc, [arrays], core_ids=[0])
    return np.ascontiguousarray(r.results[0]["outT"].T)[None]
```

```python
from contextlib import ExitStack, nullcontext

import numpy as np
import concourse.bass as bass
from concourse import mybir

F32 = mybir.dt.float32
F32R = mybir.dt.float32r
I32 = mybir.dt.int32
ALU = mybir.AluOpType
ACT = mybir.ActivationFunctionType
AX = mybir.AxisListType.X

P = 128
S = 512
D = 1024
KC = D // P
NT = S // P
MEM = 256
DFF1 = 2816
DFF2 = 4096
HEADS = 8
EPS = 1e-6
NEG = -1e30
REL = 128
CH = 64

PANELS = [("w_in", 24), ("mem_k", 8), ("w_out", 8), ("mem_v", 8), ("mem_q", 8), ("mem_o", 8), ("ffn", 3 * DFF1 // P),
          ("a_in", 24), ("a_out", 8), ("mlp0", 2 * DFF2 // P), ("kv_a", 3), ("kv_b", 4), ("q_a", 3), ("q_b", 6),
          ("b_out", 8), ("mlp1", 2 * DFF2 // P)]
PANEL0 = {}
_n = 0
for _name, _count in PANELS:
    PANEL0[_name] = _n
    _n += _count
NPANEL = _n
assert NPANEL % 2 == 0

PROJ = [("w_in", 16), ("mem_k", 8), ("w_out", 8), ("mem_q", 8), ("mem_o", 8), ("a_in", 16), ("a_out", 8),
        ("kv_a", 3), ("k_nope", 8), ("q_a", 3), ("q_nope", 8), ("q_rope", 4), ("b_out", 8)]
STATS = [("x", 8, D), ("mem", 8, D), ("fox", 4, 512), ("chunk", 4, 512), ("mix", 8, D), ("x_mem", 8, D),
         ("ca", 8, D), ("x_ffn", 8, D), ("ffn", 8, D), ("x_a", 8, D), ("a", 8, D), ("x_mlp0", 8, D), ("mlp0", 8, D), ("x_b", 8, D), ("c_kv", 2, 256), ("c_q", 3, 384),
         ("b", 8, D), ("x_mlp1", 8, D), ("mlp1", 8, D)]
MAKES = [("x", 8, 1), ("mem", 8, 1), ("o_fox", 4, 1), ("o_chunk", 4, 1), ("x_mem", 8, 1), ("o_mem", 8, 0), ("x_ffn", 8, 1),
         ("x_a", 8, 1), ("cells", 8, 0), ("x_mlp0", 8, 1), ("x_kv", 8, 1), ("c_kv", 2, 1), ("x_b", 8, 1),
         ("c_q", 3, 1), ("o_b", 8, 0), ("x_mlp1", 8, 1)]
MAKES_T = [(name, n * normed) for name, n, normed in MAKES]
TURN = 2 * np.pi
TURN_PARTS = (6.28125, float(np.float32(TURN - 6.28125)), float(TURN - 6.28125 - np.float32(TURN - 6.28125)))
PI_IN = 3.1415925
ROUND = 1.5 * 2 ** 23
RESID = ["mix", "ca", "ffn", "a", "mlp0", "b", "mlp1"]
FFNS = [("ffn", DFF1 // P // 2, True), ("mlp0", DFF2 // P // 2, False), ("mlp1", DFF2 // P // 2, False)]


VTILES = [("w_in", 8), ("mem", 4), ("a_in", 8), ("kv_b", 8)]
SUMMED_BY_PE = ["x_ffn", "x_a", "x_mlp0", "x_b", "x_mlp1"]
ADDS = [(name, 0 if name in SUMMED_BY_PE else n - 1) for name, n, _ in STATS]
SUMS = [(name, n if name in SUMMED_BY_PE else 1) for name, n, _ in STATS]
POOL_ADDS = (1, 3, 5)


def ff_up(name, g):
    size = 6 if name == "ffn" else 4
    return PANEL0[name] if isinstance(g, int) and g == 0 else g * size + (PANEL0[name] - 2)


def ff_down(name, g, last=False):
    size = 6 if name == "ffn" else 4
    return g * size + (PANEL0[name] + (size - 2 if last else 2 * size - 4))


def before(table, name, column=1):
    total = 0
    for row in table:
        if row[0] == name:
            return total
        total += row[column]
    raise KeyError(name)


def row(table, name):
    return [r for r in table if r[0] == name][0]


VEC = {}
_v = 0
for _name, _count in [("g_mix_pre", 8), ("g_out", 8), ("g_mix_post", 8), ("g_mem_pre", 8), ("g_mem_kv", 8),
                      ("g_mem_post", 8), ("g_ffn_pre", 8), ("g_ffn_post", 8), ("norm_g", 64), ("ada_b", 112),
                      ("kv_norm_g", 8), ("head_g", 8), ("kv_latent_g", 2), ("q_latent_g", 3),
                      ("zero", 8), ("b_f", 8), ("gate_b", 16)]:
    VEC[_name] = _v
    _v += _count
NVEC = _v
CON = {}
_c = 0
for _name, _count in [("ident", P), ("ones", P), ("mask", P), ("maskT", P), ("upper", S), ("minus_onehot", 8),
                      ("inv_freq", 1), ("rope_sign", 1)]:
    CON[_name] = _c
    _c += _count
NCON = _c
SH1, SC1, G1, SH2, SC2, G2, KVSH, KVSC = range(8)
LAYER1 = 8


class Chain:

    def __init__(self, eng, sem):
        self.eng, self.sem, self.n = eng, sem, 0

    def link(self, ins):
        ins.then_inc(self.sem, 1)
        self.n = self.n + 1
        self.eng.wait_ge(self.sem, self.n)


def program(nc, xT, memT, panels, ada, c, vecs, cons, gates_w, bias, pos, outT):
    ctx = ExitStack()
    with ctx:
        def sb(name, shape, dt=F32, where=ctx):
            return where.enter_context(nc.sbuf_tensor(name, shape, dt))

        def sem(name):
            return ctx.enter_context(nc.semaphore(name))

        x = sb("x", [P, KC, S])
        Y = sb("Y", [P, KC, S])
        stage = sb("stage", [P, 2, D])
        WH = sb("WH", [P, 2, D], F32R)
        WL = sb("WL", [P, 2, D], F32R)
        apiece = sb("apiece", [P, 2, D])
        cond = sb("cond", [P, D])
        con = sb("con", [P, NCON])
        vec = sb("vec", [P, NVEC])
        adac = sb("adac", [P, 112])
        pre_g = sb("pre_g", [P, 5, KC])
        post_g = sb("post_g", [P, 4, KC])
        identr = sb("identr", [P, P], F32R)
        onesr = sb("onesr", [P, P], F32R)
        maskr = sb("maskr", [P, P], F32R)
        maskTr = sb("maskTr", [P, P], F32R)
        wgate = sb("wgate", [P, KC, 24])
        wgateH = sb("wgateH", [P, KC, 24], F32R)
        wgateL = sb("wgateL", [P, KC, 24], F32R)
        stat = sb("stat", [P, 24])
        lf = sb("lf", [P, NT, 8])
        gi = sb("gi", [P, NT, 8])
        gs = sb("gs", [P, NT, 8])
        gz = sb("gz", [P, NT, 8])
        gw = sb("gw", [P, NT, 8])
        sq = sb("sq", [P, 2, S])
        acc = sb("acc", [P, S])
        logs = sb("logs", [P, S])
        rstd = sb("rstd", [P, S])
        eps = sb("eps", [P, 1])
        t = sb("t", [P, 2, S])
        region = ExitStack()
        QK = sb("QK", [P, 16, S], F32, region)
        V = sb("V", [P, NT, D], F32, region)
        X = sb("X", [P, 4, S], F32, region)
        part = ExitStack()
        H = sb("H", [P, KC, 2, S], F32R, part)
        HM = sb("HM", [P, KC, 2, MEM], F32R, part)
        part.close()
        part = ExitStack()
        QS = sb("QS", [P, 2, 2, 2, S], F32R, part)
        KS = sb("KS", [P, 2, 2, S], F32R, part)
        VS = sb("VS", [P, 2, 2, S], F32R, part)
        PT = sb("PT", [P, 2, NT, S], F32R, part)
        RB = sb("RB", [40, S], F32R, part)
        RBS = sb("RBS", [40, 2, S], F32R, part)
        part.close()
        part = ExitStack()
        sb("under_kr", [P, 24 * S], F32R, part)
        KR = sb("KR", [P, 2, S], F32R, part)
        part.close()
        region.close()
        region = ExitStack()
        HID = sb("HID", [P, 2, 2, 2, S], F32R, region)
        region.close()

        bank = [ctx.enter_context(nc.psum_tensor(f"bank{i}", [P, S], F32)) for i in range(8)]
        G, T, O = bank[0:2], bank[2:4], bank[4:6]
        ST, AD = bank[6], bank[7]

        ident = con[:, CON["ident"]:CON["ident"] + P]
        ones = con[:, CON["ones"]:CON["ones"] + P]
        upper = con[:, CON["upper"]:CON["upper"] + S]

        memf = V[:, 0:2, :].rearrange("p a (c t) -> p (a c) t", t=MEM)
        memK = QK[:, 8:12, :].rearrange("p a (c t) -> p (a c) t", t=MEM)
        QKf = QK[:].rearrange("p a b -> p (a b)")
        Xf = X[:].rearrange("p a b -> p (a b)")
        ropeF, ropeA, ropeB = apiece[:, 0, S:2 * S], apiece[:, 1, 0:S], apiece[:, 1, S:2 * S]
        swapped = [apiece[:, 0, 0:S], apiece[:, 0, S:2 * S]]
        rstd_x = apiece[:, 1, 0:S]
        gu = sq[:, 1, :]
        gsf = gs[:].rearrange("p a b -> p (a b)")
        cos, sin = cond[:, 0:S], cond[:, S:2 * S]
        half_rows = [slice(0, 64), slice(64, 128)]

        def col(name, m=0):
            return vec[:, VEC[name] + m:VEC[name] + m + 1]

        def await_x(eng, name, m):
            base = RESID.index(name)
            if m in POOL_ADDS:
                eng.wait_ge(s_resp, len(POOL_ADDS) * base + POOL_ADDS.index(m) + 1)
            else:
                by_vector = [c for c in range(KC) if c not in POOL_ADDS]
                eng.wait_ge(s_res, len(by_vector) * base + by_vector.index(m) + 1)

        s_const = sem("const_loaded")
        s_x = sem("x_loaded")
        s_mem = sem("mem_loaded")
        s_gw = sem("gate_weights_loaded")
        s_bias = sem("bias_loaded")
        s_pos = sem("positions_loaded")
        s_stage = [sem("panel0_loaded"), sem("panel1_loaded")]
        s_split = sem("panel_split")
        s_hisplit = sem("panel_high")
        s_used = sem("panel_used")
        s_piece = [sem("piece0_loaded"), sem("piece1_loaded")]
        s_pused = sem("piece_used")
        s_proj = sem("projected")
        s_free = sem("projection_bank_free")
        s_vev = sem("values_evacuated")
        s_sq = sem("squares")
        s_add = sem("squares_added")
        s_sum = sem("squares_summed")
        s_log = sem("mean_squares_log")
        s_rstd = sem("rstd_ready")
        s_t = sem("scaled")
        s_hi = sem("input_high")
        s_h = sem("input_split")
        s_hold = sem("waits_held")
        s_eps = sem("eps_set")
        s_wgh = sem("gate_weights_high")
        s_gz = sem("gate_magnitude")
        s_scan = sem("running_max")
        s_rbl = sem("rows_split")
        s_kr = sem("shared_keys_high")
        s_res = sem("residual_added")
        s_resp = sem("residual_added_by_pool")
        s_rt2 = sem("residual_scaled")
        s_dve = sem("vector_chain")
        s_act = sem("scalar_chain")
        s_cr = sem("consts_rounded")
        s_wg = sem("gate_weights_split")
        s_gl = sem("gate_logits")
        s_glr = sem("gate_logit_rows")
        s_gact = sem("gate_exp_ln")
        s_gate = sem("gates_ready")
        s_row = sem("gate_rows")
        s_rb = sem("rows_high")
        s_c = sem("condition_loaded")
        s_cond = sem("cond_ready")
        s_out = sem("out_stored")
        s_rope = sem("rope_angles")
        s_rsin = sem("rope_sines")
        s_roped = sem("rotated")
        att = {}
        for name in ("fox", "chunk", "mem", "mla"):
            att[name] = {k: sem(f"{name}_{k}") for k in (
                "qk_high", "qk_split", "v_high", "v_split", "scores", "max", "exp", "probs", "turned",
                "pt_high", "pt_split", "pv", "out", "recip")}
        s_pad = sem("queries_padded")
        cell = {k: sem(f"cell_{k}") for k in (
            "qk_high", "qk_split", "v_high", "v_split", "scores", "exp", "probs", "pt_high", "pt_split",
            "pv", "guard", "gexp", "den", "normed", "out", "square", "mean", "log", "root", "den_log", "den_inverse")}
        ff = {}
        for name, _, _ in FFNS:
            ff[name] = {k: sem(f"{name}_{k}") for k in ("act", "hidden", "high", "split", "down", "added")}

        block = ctx.enter_context(nc.Block())

        @block.sync
        def _(sp):
            sp.dma_start(con[:], cons).then_inc(s_const, 16)
            sp.dma_start(vec[:], vecs).then_inc(s_const, 16)
            sp.dma_start(x[:], xT.rearrange("(c p) t -> p c t", p=P)).then_inc(s_x, 16)

            sp.dma_start(cond[:], c).then_inc(s_c, 16)

            def load_panel(p, slot, first=False):
                if not first:
                    sp.wait_ge(s_split, p - 1)
                sp.dma_start(stage[:, slot, :], panels[p]).then_inc(s_stage[slot], 16)

            def load_piece(q, slot, first=False):
                if not first:
                    sp.wait_ge(s_pused, q - 1)
                sp.dma_start(apiece[:, slot, :], ada[q]).then_inc(s_piece[slot], 16)

            def with_pieces(p0, q0, n):
                with sp.Fori(0, n) as i:
                    for j in range(4):
                        load_panel(i * 4 + (p0 + j), j % 2)
                        load_piece(i * 8 + (q0 + 2 * j), 0)
                        load_piece(i * 8 + (q0 + 2 * j + 1), 1)

            def plain(p0, p1):
                if p1 - p0 >= 4:
                    with sp.Fori(0, (p1 - p0) // 2) as i:
                        for j in range(2):
                            load_panel(i * 2 + (p0 + j), j)
                else:
                    for p in range(p0, p1):
                        load_panel(p, p % 2)

            load_panel(0, 0, True)
            load_panel(1, 1, True)
            load_piece(0, 0, True)
            load_piece(1, 1, True)
            sp.dma_start(wgate[:], gates_w).then_inc(s_gw, 16)
            sp.dma_start(X[:].rearrange("p a b -> p (a b)"), bias).then_inc(s_bias, 16)
            for j in range(2, 4):
                load_panel(j, j % 2)
            for q in range(2, 8):
                load_piece(q, q % 2)
            with_pieces(4, 8, 5)
            load_panel(24, 0)
            load_panel(25, 1)
            sp.wait_ge(att["chunk"]["v_split"], HEADS)
            sp.dma_start(memf, memT.rearrange("(c p) t -> p c t", p=P)).then_inc(s_mem, 16)
            plain(26, PANEL0["mem_q"])
            with_pieces(PANEL0["mem_q"], 48, 2)
            plain(PANEL0["mem_o"], PANEL0["a_in"])
            with_pieces(PANEL0["a_in"], 64, 6)
            sp.wait_ge(s_pused, 112)
            sp.dma_start(apiece[:].bitcast(I32)[:, 0, 0:S], pos).then_inc(s_pos, 16)
            plain(PANEL0["a_out"], NPANEL)
            for m in range(KC):
                await_x(sp, "mlp1", m)
                sp.dma_start(outT[m * P:(m + 1) * P, :], x[:, m, :]).then_inc(s_out, 16)
            sp.wait_ge(s_out, 16 * KC)

        @block.gpsimd
        def _(pool):
            def split_low(p, slot):
                pool.wait_ge(s_hisplit, p + 1)
                pool.tensor_tensor(WL[:, slot, :], stage[:, slot, :], WH[:, slot, :].bitcast(F32),
                                   ALU.subtract).then_inc(s_split, 1)

            def split_lows(p0, p1):
                with pool.Fori(0, (p1 - p0) // 2) as i:
                    for slot in range(2):
                        split_low(i * 2 + (p0 + slot), slot)

            def residual(name):
                base = 8 * RESID.index(name)
                for m in POOL_ADDS:
                    pool.wait_ge(s_rt2, base + m + 1)
                    pool.tensor_tensor(x[:, m, :], x[:, m, :], Y[:, m, :], ALU.add).then_inc(s_resp, 1)

            done = 0
            for name, following in [("mix", "mem_v"), ("ca", "ffn"), ("ffn", "a_in"), ("a", "mlp0"),
                                    ("mlp0", "kv_a"), ("b", "mlp1"), ("mlp1", None)]:
                end = PANEL0[following] + 2 if following else NPANEL
                split_lows(done, end)
                residual(name)
                done = end

        @block.tensor
        def _(pe):
            def three(out, wh, wl, rh, rl, start, stop):
                pe.matmul(out, wh, rh, start=start, stop=False)
                pe.matmul(out, wh, rl, start=False, stop=False)
                return pe.matmul(out, wl, rh, start=False, stop=stop)

            def chunk_of(p, n, slot, src, width, fresh=None):
                pe.wait_ge(s_split, p + 1)
                pe.wait_ge(s_free, n + 1)
                for k in range(KC):
                    input_chunk(fresh, k)
                    last = three(G[slot][:, 0:width], WH[:, slot, k * P:(k + 1) * P],
                                 WL[:, slot, k * P:(k + 1) * P], src[:, k, 0, 0:width], src[:, k, 1, 0:width],
                                 k == 0, k == KC - 1)
                last.then_inc(s_used, 1)

            def project(name, count, fresh):
                p0, n0 = PANEL0[name], before(PROJ, name)
                for j in range(2):
                    chunk_of(p0 + j, n0 + j, j % 2, H, S, fresh if j == 0 else None)
                with pe.Fori(1, count // 2) as i:
                    for j in range(2):
                        chunk_of(i * 2 + (p0 + j), i * 2 + (n0 + j), j % 2, H, S)

            def value_panel(p, pp, tiles, src=H):
                slot = pp % 2
                pe.wait_ge(s_split, p + 1)
                for kk in range(2):
                    k = 2 * pp + kk
                    for tt in range(tiles):
                        last = three((T + O)[tt][:, :], src[:, k, 0, tt * P:(tt + 1) * P],
                                     src[:, k, 1, tt * P:(tt + 1) * P], WH[:, slot, kk * S:(kk + 1) * S],
                                     WL[:, slot, kk * S:(kk + 1) * S], k == 0, k == KC - 1)
                last.then_inc(s_used, 1)

            def values_half(p0, name, half, gates=None):
                pe.wait_ge(s_vev, half * NT + before(VTILES, name) + 1)
                for pp in range(4):
                    value_panel(p0 + half * 4 + pp, pp, NT)
                    if gates is not None and pp == 0:
                        turn_logits(*gates)

            def input_chunk(name, k):
                if name == "o":
                    pe.wait_ge(s_h, before(MAKES, "o_fox") + k + 1)
                elif name is not None:
                    pe.wait_ge(s_h, before(MAKES, name) + k + 1)

            def mean_square(name, width=S):
                at = [r[0] for r in STATS].index(name)
                if at:
                    pe.wait_ge(s_log, at)
                if name in SUMMED_BY_PE:
                    for m in range(KC):
                        pe.wait_ge(s_sq, before(STATS, name) + m + 1)
                        pe.matmul(ST[:, :], ones, sq[:, m % 2, :], start=m == 0, stop=m == KC - 1).then_inc(s_sum, 1)
                else:
                    pe.wait_ge(s_add, before(ADDS, name) + row(ADDS, name)[1])
                    pe.matmul(ST[:, 0:width], ones, acc[:, 0:width], start=True, stop=True).then_inc(s_sum, 1)

            def gate_logits(first, n):
                for k in range(KC):
                    last = three(ST[0:n, :], wgateH[:, k, first:first + n], wgateL[:, k, first:first + n],
                                 H[:, k, 0, :], H[:, k, 1, :], k == 0, k == KC - 1)
                last.then_inc(s_gl, 1)

            def turn_logits(mixer, n):
                pe.wait_ge(s_glr, mixer + 1)
                for tt in range(NT):
                    last = pe.transpose(AD[:, 16 * tt:16 * tt + n], t[0:n, 0, tt * P:(tt + 1) * P], ident[0:n, 0:n])
                last.then_inc(s_gl, 1)

            def cumulate(out, gate, stop=True):
                for st in range(NT):
                    last = pe.matmul(out[0:8, st * P:S], gate[:, st, :], upper[:, 0:S - st * P],
                                     start=st == 0, stop=stop and st == NT - 1, skip_group_check=True)
                return last

            def attention(name, heads, scores, turned_tiles, pv):
                sm = att[name]

                def score(n, slot, qb):
                    if qb == 0:
                        pe.wait_ge(sm["qk_split"], n + 1)
                    if not (isinstance(n, int) and n == 0 and qb < 2):
                        pe.wait_ge(sm["exp"], n * 4 + qb - 1)
                    scores(n, slot, qb, G[qb % 2]).then_inc(sm["scores"], 1)

                def turn(n, slot, qb):
                    pe.wait_ge(sm["probs"], n * 4 + qb + 1)
                    if not (isinstance(n, int) and n == 0 and qb < 2):
                        pe.wait_ge(sm["pt_split"], n * 4 + qb - 1)
                    for kb in range(turned_tiles(qb)):
                        last = pe.transpose(T[qb % 2][:, kb * P:(kb + 1) * P], t[:, qb % 2, kb * P:(kb + 1) * P], ident)
                    last.then_inc(sm["turned"], 1)

                def weigh(n, slot):
                    pe.wait_ge(sm["pt_split"], n * 4 + 4)
                    pe.wait_ge(sm["v_split"], n + 1)
                    pe.wait_ge(sm["out"], n + 1)
                    pv(n, slot).then_inc(sm["pv"], 1)

                def head(n, slot, prev):
                    score(n, slot, 0)
                    if prev:
                        turn(n - 1, 1 - slot, 3)
                    score(n, slot, 1)
                    if prev:
                        weigh(n - 1, 1 - slot)
                    turn(n, slot, 0)
                    score(n, slot, 2)
                    turn(n, slot, 1)
                    score(n, slot, 3)
                    turn(n, slot, 2)

                head(0, 0, False)
                with pe.Fori(0, (heads - 2) // 2) as i:
                    head(i * 2 + 1, 1, True)
                    head(i * 2 + 2, 0, True)
                head(heads - 1, 1, True)
                turn(heads - 1, 1, 3)
                weigh(heads - 1, 1)

            def qk(out, slot, part_, qb, kh, kl, width, start, stop):
                return three(out[:, 0:width], QS[:, slot, part_, 0, qb * P:(qb + 1) * P],
                             QS[:, slot, part_, 1, qb * P:(qb + 1) * P], kh, kl, start, stop)

            def causal_pv(n, slot):
                for kb in range(NT):
                    last = three(O[slot][:, kb * P:S], VS[:, slot, 0, kb * P:(kb + 1) * P],
                                 VS[:, slot, 1, kb * P:(kb + 1) * P], PT[:, 0, kb, kb * P:S], PT[:, 1, kb, kb * P:S],
                                 kb == 0, kb == NT - 1)
                return last

            def fox_scores(n, slot, qb, out):
                w = (qb + 1) * P
                qk(out, slot, 0, qb, KS[:, slot, 0, 0:w], KS[:, slot, 1, 0:w], w, True, False)
                pe.matmul(out[:, 0:w], onesr[0:40, :], RBS[:, slot, 0:w], start=False, stop=False)
                return pe.matmul(out[:, qb * P:w], identr[:, :], maskr[:, :], start=False, stop=True)

            def chunk_scores(n, slot, qb, out):
                w = (qb + 1) * P
                near = max(0, qb - 1) * P
                qk(out, slot, 0, qb, KS[:, slot, 0, 0:w], KS[:, slot, 1, 0:w], w, True, False)
                if near:
                    pe.matmul(out[:, 0:near], ident, Xf[:, bass.ds(n * 256, 1)].to_broadcast([P, near]),
                              start=False, stop=False)
                return pe.matmul(out[:, near:w], ident, Xf[:, bass.ds(n * 256 + (256 - (w - near)), w - near)],
                                 start=False, stop=True)

            def mem_scores(n, slot, qb, out):
                for c in range(2):
                    last = qk(out, slot, c, qb, KS[:, slot, 0, c * MEM:(c + 1) * MEM],
                              KS[:, slot, 1, c * MEM:(c + 1) * MEM], MEM, c == 0, c == 1)
                return last

            def mem_pv(n, slot):
                for dc in range(2):
                    for kb in range(2):
                        at = kb * MEM + dc * P
                        last = three(O[dc][:, :], VS[:, slot, 0, at:at + P], VS[:, slot, 1, at:at + P],
                                     PT[:, 0, kb, :], PT[:, 1, kb, :], kb == 0, kb == 1)
                return last

            def mla_scores(n, slot, qb, out):
                w = (qb + 1) * P
                qk(out, slot, 0, qb, KS[:, slot, 0, 0:w], KS[:, slot, 1, 0:w], w, True, False)
                qk(out, slot, 1, qb, KR[:, 0, 0:w], KR[:, 1, 0:w], w, False, False)
                return pe.matmul(out[:, qb * P:w], identr[:, :], maskr[:, :], start=False, stop=True)

            def feed_forward(name, groups, gated):
                sm = ff[name]
                banks = [G[0], G[1], ST, AD] if gated else [G[0], None, G[1], None]
                per = 2 if gated else 1

                def up(g, slot):
                    p = ff_up(name, g)
                    for j in range(2):
                        for u in range(per):
                            q = j * per + u
                            pe.wait_ge(s_split, p + (q + 1))
                            if not (isinstance(g, int) and g == 0):
                                pe.wait_ge(sm["hidden"], g * 2 + j - 1)
                            for k in range(KC):
                                if isinstance(g, int) and g == 0 and q == 0:
                                    input_chunk("x_" + name, k)
                                last = three(banks[2 * j + u][:, :], WH[:, q % 2, k * P:(k + 1) * P],
                                             WL[:, q % 2, k * P:(k + 1) * P], H[:, k, 0, :], H[:, k, 1, :],
                                             k == 0, k == KC - 1)
                            last.then_inc(s_used, 1)

                def down(g, slot, last_group=False):
                    p = ff_down(name, g, last_group)
                    pe.wait_ge(sm["split"], g * 2 + 2)
                    for m in range(KC):
                        half, at = m // 4, m % 4 * P
                        if m % 4 == 0:
                            pe.wait_ge(s_split, p + (half + 1))
                        pe.wait_ge(sm["added"], g * 8 + (m + 1))
                        for j in range(2):
                            last = three((T + O)[m % 4][:, :], WH[:, half, j * S + at:j * S + at + P],
                                         WL[:, half, j * S + at:j * S + at + P],
                                         HID[:, slot, j, 0, :], HID[:, slot, j, 1, :], j == 0, j == 1)
                        last.then_inc(s_used if m % 4 == 3 else sm["down"], 1)
                    if last_group:
                        mean_square(name)

                up(0, 0)
                with pe.Fori(0, (groups - 1) // 2) as i:
                    up(i * 2 + 1, 1)
                    down(i * 2, 0)
                    up(i * 2 + 2, 0)
                    down(i * 2 + 1, 1)
                if groups % 2 == 0:
                    up(groups - 1, 1)
                    down(groups - 2, 0)
                down(groups - 1, (groups - 1) % 2, True)

            def small_project(p0, n0, chunks, ks, per_panel, fresh=None):
                for c in range(chunks):
                    p, at = p0 + c // per_panel, c % per_panel
                    slot, n = p % 2, n0 + c
                    if at == 0:
                        pe.wait_ge(s_split, p + 1)
                    pe.wait_ge(s_free, n + 1)
                    for k in range(ks):
                        if c == 0:
                            input_chunk(fresh, k)
                        w = (at * ks + k) * P
                        last = three(G[n % 2][:, :], WH[:, slot, w:w + P], WL[:, slot, w:w + P],
                                     H[:, k, 0, :], H[:, k, 1, :], k == 0, k == ks - 1)
                    last.then_inc(s_used if at == per_panel - 1 or c == chunks - 1 else s_proj, 1)

            pe.wait_ge(s_const, 32)
            mean_square("x")
            project("w_in", 16, "x")
            pe.wait_ge(s_wg, 1)
            gate_logits(0, 8)
            values_half(PANEL0["w_in"] + 16, "w_in", 0, (0, 8))
            pe.wait_ge(s_gate, 1)
            cumulate(ST, lf).then_inc(s_row, 1)
            values_half(PANEL0["w_in"] + 16, "w_in", 1)
            pe.wait_ge(s_vev, 2 * NT + 1)
            pe.wait_ge(s_cr, 1)
            pe.wait_ge(s_rbl, 1)
            attention("fox", HEADS, fox_scores, lambda qb: qb + 1, causal_pv)
            pe.wait_ge(s_bias, 16)
            attention("chunk", HEADS, chunk_scores, lambda qb: qb + 1, causal_pv)
            mean_square("mem", MEM)
            for c in range(8):
                chunk_of(PANEL0["mem_k"] + c, before(PROJ, "mem_k") + c, c % 2, HM, MEM, "mem" if c == 0 else None)
                if c == 1:
                    mean_square("fox")
                if c == 3:
                    mean_square("chunk")
            project("w_out", 8, "o")
            for pp in range(8):
                if pp == 1:
                    mean_square("mix")
                if pp == 6:
                    mean_square("x_mem")
                if pp % 4 == 0:
                    pe.wait_ge(s_vev, before(VTILES, "mem") + pp // 4 * 2 + 1)
                value_panel(PANEL0["mem_v"] + pp, pp % 4, 2, HM)
            project("mem_q", 8, "x_mem")
            attention("mem", 4, mem_scores, lambda qb: 2, mem_pv)
            project("mem_o", 8, "o_mem")
            mean_square("ca")
            mean_square("x_ffn")
            feed_forward(*FFNS[0])
            mean_square("x_a")
            project("a_in", 16, "x_a")
            gate_logits(8, 16)
            values_half(PANEL0["a_in"] + 16, "a_in", 0, (1, 16))
            pe.wait_ge(s_gate, 2)
            pe.wait_ge(s_free, before(PROJ, "a_in") + 16 + 2)
            cumulate(G[0], gz, stop=False)
            for tt in range(NT):
                last = pe.matmul(G[0][0:8, tt * P:(tt + 1) * P], gi[:, tt, :], ident, start=False, stop=tt == NT - 1,
                                 skip_group_check=True)
            last.then_inc(s_row, 1)
            cumulate(G[1], lf).then_inc(s_row, 1)
            for tt in range(NT):
                for st in range(tt + 1):
                    pe.matmul(ST[:, tt * 8:tt * 8 + 8], upper[:, 0:P] if st == tt else ones, gz[:, st, :],
                              start=st == 0, stop=False)
                last = pe.matmul(ST[:, tt * 8:tt * 8 + 8], ident, gi[:, tt, :], start=False, stop=True)
            last.then_inc(s_row, 1)
            values_half(PANEL0["a_in"] + 16, "a_in", 1)
            pe.wait_ge(s_vev, before(VTILES, "kv_b") + 1)
            pe.wait_ge(s_rbl, 2)

            def cell_head(n, slot):
                pe.wait_ge(cell["qk_split"], n + 1)
                for kb in range(NT):
                    w = S - kb * P
                    if not (isinstance(n, int) and n == 0 and kb < 2):
                        pe.wait_ge(cell["probs"], n * 4 + kb - 1)
                    three(G[kb % 2][:, 0:w], KS[:, slot, 0, kb * P:(kb + 1) * P], KS[:, slot, 1, kb * P:(kb + 1) * P],
                          QS[:, slot, 0, 0, kb * P:S], QS[:, slot, 0, 1, kb * P:S], True, True)
                    pe.matmul(T[kb % 2][:, 0:w], onesr[0:40, :], RBS[:, slot, kb * P:S], start=True, stop=False)
                    pe.matmul(T[kb % 2][:, 0:P], identr[:, :], maskTr[:, :], start=False, stop=True)\
                        .then_inc(cell["scores"], 1)
                if not (isinstance(n, int) and n == 0):
                    pe.wait_ge(cell["out"], n)
                pe.matmul(AD[:, :], ones[0:8, :], cond[0:8, slot * S:(slot + 1) * S], start=True, stop=True).then_inc(cell["guard"], 1)
                pe.wait_ge(cell["v_split"], n + 1)
                for kb in range(NT):
                    pe.wait_ge(cell["pt_split"], n * 4 + kb + 1)
                    three(O[0][:, kb * P:S], VS[:, slot, 0, kb * P:(kb + 1) * P], VS[:, slot, 1, kb * P:(kb + 1) * P],
                          PT[:, 0, kb, kb * P:S], PT[:, 1, kb, kb * P:S], kb == 0, kb == NT - 1)
                    for hl in range(2):
                        last = pe.matmul(O[1][:, kb * P:S], onesr[:, :], PT[:, hl, kb, kb * P:S],
                                         start=kb == 0 and hl == 0, stop=kb == NT - 1 and hl == 1)
                last.then_inc(cell["pv"], 1)

            cell_head(0, 0)
            cell_head(1, 1)
            with pe.Fori(1, HEADS // 2) as i:
                cell_head(i * 2, 0)
                cell_head(i * 2 + 1, 1)
            for h in range(HEADS):
                pe.wait_ge(cell["square"], h + 1)
                if h:
                    pe.wait_ge(cell["log"], h)
                pe.matmul(ST[:, :], ones, sq[:, h % 2, :], start=True, stop=True).then_inc(cell["mean"], 1)
            project("a_out", 8, "cells")
            mean_square("a")
            mean_square("x_mlp0")
            feed_forward(*FFNS[1])
            mean_square("x_b")
            small_project(PANEL0["kv_a"], before(PROJ, "kv_a"), 3, 8, 1, "x_kv")
            mean_square("c_kv")
            small_project(PANEL0["kv_b"], before(PROJ, "k_nope"), 8, 2, 4, "c_kv")
            for half in range(2):
                p = PANEL0["kv_b"] + 2 + half
                pe.wait_ge(s_split, p + 1)
                pe.wait_ge(s_vev, before(VTILES, "kv_b") + half * NT + 1)
                for k in range(2):
                    for tt in range(NT):
                        last = three((T + O)[tt][:, :], H[:, k, 0, tt * P:(tt + 1) * P],
                                     H[:, k, 1, tt * P:(tt + 1) * P], WH[:, p % 2, k * S:(k + 1) * S],
                                     WL[:, p % 2, k * S:(k + 1) * S], k == 0, k == 1)
                last.then_inc(s_used, 1)
            small_project(PANEL0["q_a"], before(PROJ, "q_a"), 3, 8, 1, "x_b")
            mean_square("c_q")
            small_project(PANEL0["q_b"], before(PROJ, "q_nope"), 8, 3, 2, "c_q")
            small_project(PANEL0["q_b"] + 4, before(PROJ, "q_rope"), 4, 3, 2)
            pe.wait_ge(s_vev, before(VTILES, "kv_b") + 2 * NT + 1)
            attention("mla", HEADS, mla_scores, lambda qb: qb + 1, causal_pv)
            project("b_out", 8, "o_b")
            mean_square("b")
            mean_square("x_mlp1")
            feed_forward(*FFNS[2])

        def staged_qk(name, n, pair, slot):
            rows = half_rows[slot]
            if name == "fox":
                return [(QK[rows, pair, :], QS[rows, slot, 0, 0, :], QS[rows, slot, 0, 1, :], 0.125),
                        (QK[:, pair + 4, :], KS[:, slot, 0, :], KS[:, slot, 1, :], 1.0)]
            if name == "chunk":
                return [(QK[rows, pair + 8, :], QS[rows, slot, 0, 0, :], QS[rows, slot, 0, 1, :], 0.125),
                        (QK[:, pair + 12, :], KS[:, slot, 0, :], KS[:, slot, 1, :], 1.0)]
            if name == "mem":
                return [(QK[:, bass.ds(n * 2, 2), :], QS[:, slot, :, 0, :], QS[:, slot, :, 1, :], 256 ** -0.5),
                        (QKf[:, bass.ds(n * S + 8 * S, S)], KS[:, slot, 0, :], KS[:, slot, 1, :], 1.0)]
            return [(QK[:, n, :], QS[:, slot, 0, 0, :], QS[:, slot, 0, 1, :], 192 ** -0.5),
                    (X[rows, pair, :], QS[rows, slot, 1, 0, :], QS[rows, slot, 1, 1, :], 192 ** -0.5),
                    (QK[:, n + 8, :], KS[:, slot, 0, :], KS[:, slot, 1, :], 1.0)]

        def staged_v(name, n, pair, slot):
            if name == "mem":
                wide = dict(b=MEM)
                src = V[:, 2:4, bass.ds(n * MEM, MEM)]
            else:
                wide = dict(b=P)
                src = V[:, :, bass.ds(pair * P + (S if name == "chunk" else 0), P) if name in ("fox", "chunk")
                        else bass.ds(n * P, P)]
            return [(src, VS[:, slot, 0, :].rearrange("p (a b) -> p a b", **wide),
                     VS[:, slot, 1, :].rearrange("p (a b) -> p a b", **wide), 1.0)]

        def cell_qk(n, pair, slot):
            rows = half_rows[slot]
            return [(QK[rows, pair, :], QS[rows, slot, 0, 0, :], QS[rows, slot, 0, 1, :], 0.125),
                    (QK[:, pair + 4, :], KS[:, slot, 0, :], KS[:, slot, 1, :], 1.0)]

        def keys_of(name, qb):
            return MEM if name == "mem" else (qb + 1) * P

        value_banks = [T[0], T[1], O[0], O[1]]

        @block.scalar
        def _(act):
            def hold():
                act.sem_inc(s_hold, 1)

            def panel_high(p, slot):
                if isinstance(p, int) and p >= NPANEL:
                    return
                act.wait_ge(s_stage[slot], p * 8 + (16 - 8 * slot))
                act.activation(WH[:, slot, :], stage[:, slot, :], ACT.Copy).then_inc(s_hisplit, 1)

            def used(p, slot):
                act.wait_ge(s_used, p + 1)
                panel_high(p + 2, slot)

            def square(name, m, source, width=S):
                if m == 0 and name != "x":
                    act.wait_ge(s_sum, before(SUMS, name))
                table, counter = (SUMS, s_sum) if name in SUMMED_BY_PE else (ADDS, s_add)
                if before(table, name) + max(m - 1, 0):
                    act.wait_ge(counter, before(table, name) + max(m - 1, 0))
                act.activation(sq[:, m % 2, 0:width], source, ACT.Square).then_inc(s_sq, 1)

            def squares(name, source, ready, width=S):
                for m in range(row(STATS, name)[1]):
                    ready(m)
                    square(name, m, source(m), width)

            def load_ln_exp():
                act.preload_act_table_set("natural_log_exp_and_others")

            def root(name, width=S):
                at = [r[0] for r in STATS].index(name)
                act.wait_ge(s_sum, before(SUMS, name) + row(SUMS, name)[1])
                act.activation(logs[:, 0:width], ST[:, 0:width], ACT.Ln, bias=eps[:, :],
                               scale=1.0 / row(STATS, name)[2]).then_inc(s_log, 1)
                act.wait_ge(s_log, at + 1)
                act.activation(rstd[:, 0:width], logs[:, 0:width], ACT.Exp, scale=-0.5).then_inc(s_rstd, 1)

            def high_chunk(name, m, source, dest, shift=None):
                if row(MAKES, name)[2]:
                    act.wait_ge(s_t, before(MAKES_T, name) + m + 1)
                    act.activation(dest(m), source(m), ACT.Identity, bias=shift(m))\
                        .then_inc(s_hi, 1)
                else:
                    act.activation(dest(m), source(m), ACT.Copy).then_inc(s_hi, 1)

            def high(name, source, dest, shift=None):
                for m in range(row(MAKES, name)[1]):
                    high_chunk(name, m, source, dest, shift)

            def evacuate(name, count, dest, first=0, func=ACT.Copy):
                p0 = PANEL0[name] + first
                with act.Fori(0, count // 2) as i:
                    for j in range(2):
                        used(i * 2 + (p0 + j), j)
                        hold()
                        act.activation(dest(i * 2 + j), G[j][:, :], func).then_inc(s_free, 1)

            def evacuate_squares(name, stat_name):
                for c in range(KC):
                    used(PANEL0[name] + c, c % 2)
                    square(stat_name, c, G[c % 2][:, :])
                    act.activation(Y[:, c, :], G[c % 2][:, :], ACT.Copy).then_inc(s_free, 1)
                    if name == "a_out" and c == 3:
                        act.wait_ge(s_rope, 1)
                        act.activation(sin, ropeA, ACT.Sin, scale=con[:, CON["rope_sign"]:CON["rope_sign"] + 1])\
                            .then_inc(s_rsin, 1)
                        act.activation(cos, ropeB, ACT.Sin).then_inc(s_rsin, 1)
                        load_ln_exp()

            def evacuate_half(p0, half, mixer=None):
                for pp in range(4):
                    if mixer is not None and pp == 0:
                        log_of_gates(mixer)
                    used(p0 + half * 4 + pp, pp % 2)
                for tt in range(NT):
                    act.activation(V[:, tt, half * S:(half + 1) * S], value_banks[tt][:, :], ACT.Copy)\
                        .then_inc(s_vev, 1)

            def evacuated(name):
                act.wait_ge(s_free, before(PROJ, name) + row(PROJ, name)[1] + 2)

            def attention(name, heads, out_of):
                sm = att[name]
                act.sem_inc(sm["out"], 1)

                def stage_qk(n, pair, slot, early=False):
                    if not early:
                        act.wait_ge(sm["scores"], n * 4 - 4)
                    hold()
                    for source, hi, _, scale in staged_qk(name, n, pair, slot):
                        last = act.activation(hi, source, ACT.Copy, scale=scale)
                    last.then_inc(sm["qk_high"], 1)

                def stage_v(n, pair, slot, early=False):
                    if not early:
                        act.wait_ge(sm["pv"], n - 1)
                    hold()
                    for source, hi, _, _ in staged_v(name, n, pair, slot):
                        act.activation(hi, source, ACT.Copy).then_inc(sm["v_high"], 1)

                def exp(n, qb):
                    if not (isinstance(n, int) and n == 0 and qb < 2):
                        act.wait_ge(sm["turned"], n * 4 + qb - 1)
                    act.wait_ge(sm["max"], n * 4 + qb + 1)
                    w = keys_of(name, qb)
                    act.activation(t[:, qb % 2, 0:w], G[qb % 2][:, 0:w], ACT.Exp, bias=stat[:, qb:qb + 1],
                                   accum_out=stat[:, 4 + qb:5 + qb]).then_inc(sm["exp"], 1)

                def pt_high(n, qb):
                    act.wait_ge(sm["turned"], n * 4 + qb + 1)
                    if qb == 0 and not (isinstance(n, int) and n == 0):
                        act.wait_ge(sm["pv"], n)
                    w = keys_of(name, qb)
                    act.activation(PT[:, 0, 0:w // P, qb * P:(qb + 1) * P],
                                   T[qb % 2][:, 0:w].rearrange("p (k q) -> p k q", q=P), ACT.Copy)\
                        .then_inc(sm["pt_high"], 1)

                def out(n, pair, slot):
                    act.wait_ge(sm["pv"], n + 1)
                    hold()
                    for dest, source in out_of(n, pair, slot):
                        last = act.activation(dest, source, ACT.Copy)
                    last.then_inc(sm["out"], 1)

                def head(n, pair, slot, prev, nxt, prev_pair, next_pair):
                    early = isinstance(n, int) and n == 0
                    exp(n, 0)
                    if prev:
                        pt_high(n - 1, 3)
                    if nxt:
                        stage_qk(n + 1, next_pair, 1 - slot, early)
                    exp(n, 1)
                    if prev:
                        out(n - 1, prev_pair, 1 - slot)
                    if nxt:
                        stage_v(n + 1, next_pair, 1 - slot, early)
                    pt_high(n, 0)
                    exp(n, 2)
                    pt_high(n, 1)
                    exp(n, 3)
                    pt_high(n, 2)

                stage_qk(0, 0, 0, True)
                stage_v(0, 0, 0, True)
                head(0, 0, 0, False, True, None, 0)
                with act.Fori(0, (heads - 2) // 2) as i:
                    head(i * 2 + 1, i, 1, True, True, i, i + 1)
                    head(i * 2 + 2, i + 1, 0, True, True, i, i + 1)
                head(heads - 1, heads // 2 - 1, 1, True, False, heads // 2 - 1, None)
                pt_high(heads - 1, 3)
                out(heads - 1, heads // 2 - 1, 1)

            def half_out(base):
                return lambda n, pair, slot: [(Y[half_rows[slot], pair + base, :], O[slot][half_rows[slot], :])]

            def feed_forward(name, groups, gated):
                sm = ff[name]
                banks = [G[0], None, ST, None] if gated else [G[0], None, G[1], None]
                per = 2 if gated else 1
                def through(g, slot):
                    p = ff_up(name, g)
                    for j in range(2):
                        used(p + j * per, (j * per) % 2)
                        if not (isinstance(g, int) and g == 0):
                            act.wait_ge(sm["split"], g * 2 + j - 1)
                        act.activation(t[:, j, :], banks[2 * j][:, :], ACT.Silu if gated else ACT.Relu)\
                            .then_inc(sm["act"], 1)
                        if gated:
                            used(p + (j * per + 1), 1)
                        act.wait_ge(sm["hidden"], g * 2 + j + 1)
                        act.activation(HID[:, slot, j, 0, :], t[:, j, :], ACT.Copy).then_inc(sm["high"], 1)

                def down(g, last=False):
                    p = ff_down(name, g, last)
                    used(p, 0)
                    used(p + 1, 1)

                through(0, 0)
                with act.Fori(0, (groups - 1) // 2) as i:
                    through(i * 2 + 1, 1)
                    down(i * 2)
                    through(i * 2 + 2, 0)
                    down(i * 2 + 1)
                if groups % 2 == 0:
                    through(groups - 1, 1)
                    down(groups - 2)
                if gated:
                    load_ln_exp()
                for m in range(KC):
                    if m % 4 == 0:
                        used_panel = ff_down(name, groups - 1, True) + m // 4
                    act.wait_ge(sm["added"], groups * 8 + m - 3)
                    square(name, m, Y[:, m, :])
                    if m % 4 == 3:
                        used(used_panel, m // 4)

            def after_residual(name):
                return lambda m: await_x(act, name, m)

            def once(sem_, value):
                return lambda m: act.wait_ge(sem_, value)

            def xc(m):
                return x[:, m, :]

            def yc(m):
                return Y[:, m, :]

            def hh(m):
                return H[:, m, 0, :]

            def logit_rows(mixer, n):
                act.wait_ge(s_gl, 2 * mixer + 1)
                act.activation(t[0:n, 0, :], ST[0:n, :], ACT.Copy).then_inc(s_glr, 1)

            def log_of_gates(mixer):
                act.wait_ge(s_gz, mixer + 1)
                act.activation(gw[:], gw[:], ACT.Exp).then_inc(s_gact, 1)
                act.wait_ge(s_gact, 2 * mixer + 1)
                act.activation(gw[:], gw[:], ACT.Ln, bias=1.0).then_inc(s_gact, 1)

            act.wait_ge(s_const, 32)
            act.wait_ge(s_eps, 1)
            act.activation(identr[:], ident, ACT.Copy).then_inc(s_free, 1)
            act.activation(onesr[:], ones, ACT.Copy).then_inc(s_free, 1)
            act.activation(maskr[:], con[:, CON["mask"]:CON["mask"] + P], ACT.Copy).then_inc(s_vev, 1)
            act.activation(maskTr[:], con[:, CON["maskT"]:CON["maskT"] + P], ACT.Copy).then_inc(s_cr, 1)
            act.wait_ge(s_c, 16)
            act.activation(cond[:], cond[:], ACT.Silu).then_inc(s_cond, 1)
            load_ln_exp()
            squares("x", xc, once(s_x, 16))
            panel_high(0, 0)
            panel_high(1, 1)
            root("x")
            high("x", yc, hh, lambda m: col("zero"))
            act.wait_ge(s_gw, 16)
            act.activation(wgateH[:], wgate[:], ACT.Copy).then_inc(s_wgh, 1)
            evacuate("w_in", 16, lambda c: QK[:, c, :])
            logit_rows(0, 8)
            evacuate_half(PANEL0["w_in"] + 16, 0, 0)
            act.wait_ge(s_row, 1)
            act.wait_ge(s_pad, 1)
            act.activation(RB[0:8, :], ST[0:8, :], ACT.Copy).then_inc(s_rb, 1)
            evacuate_half(PANEL0["w_in"] + 16, 1)
            act.wait_ge(s_pad, 2)
            attention("fox", HEADS, half_out(0))
            attention("chunk", HEADS, half_out(4))
            act.wait_ge(att["chunk"]["out"], HEADS + 1)
            squares("mem", lambda m: memf[:, m, :], once(s_mem, 16), MEM)
            root("mem", MEM)
            high("mem", lambda m: memf[:, m, :], lambda m: HM[:, m, 0, :], lambda m: col("zero"))
            for c in range(8):
                used(PANEL0["mem_k"] + c, c % 2)
                act.activation(memK[:, c, :], G[c % 2][:, 0:MEM], ACT.Copy).then_inc(s_free, 1)
                if c == 0:
                    squares("fox", yc, lambda m: None)
                if c == 1:
                    root("fox")
                    high("o_fox", yc, hh, lambda m: col("zero"))
                    squares("chunk", lambda m: yc(m + 4), lambda m: None)
                if c == 3:
                    root("chunk")
                    high("o_chunk", lambda m: yc(4 + m), lambda m: hh(4 + m), lambda m: col("zero"))
            evacuate_squares("w_out", "mix")
            for pp in range(8):
                used(PANEL0["mem_v"] + pp, pp % 2)
                if pp == 0:
                    root("mix")
                if 1 <= pp <= 4:
                    for m in (2 * pp - 2, 2 * pp - 1):
                        await_x(act, "mix", m)
                        square("x_mem", m, xc(m))
                if pp % 4 == 3:
                    for tt in range(2):
                        act.activation(V[:, 2 + tt, pp // 4 * S:pp // 4 * S + S], value_banks[tt][:, :], ACT.Copy)\
                            .then_inc(s_vev, 1)
                if pp == 5:
                    root("x_mem")
            high("x_mem", yc, hh, lambda m: col("zero"))
            evacuate("mem_q", 8, lambda c: QK[:, c, :])
            evacuated("mem_q")
            attention("mem", 4, lambda n, pair, slot: [(Y[:, n * 2 + c, :], O[c][:, :]) for c in range(2)])
            act.wait_ge(att["mem"]["out"], 5)
            high("o_mem", yc, hh)
            evacuate_squares("mem_o", "ca")
            root("ca")
            squares("x_ffn", xc, after_residual("ca"))
            root("x_ffn")
            high("x_ffn", yc, hh, lambda m: col("zero"))
            feed_forward(*FFNS[0])
            root("ffn")
            squares("x_a", xc, after_residual("ffn"))
            root("x_a")
            high("x_a", yc, hh, lambda m: adac[:, SH1 * 8 + m:SH1 * 8 + m + 1])
            evacuate("a_in", 8, lambda c: QK[:, c, :])
            evacuate("a_in", 8, lambda c: QK[:, c + 8, :], first=8, func=ACT.Sigmoid)
            load_ln_exp()
            logit_rows(1, 16)
            evacuate_half(PANEL0["a_in"] + 16, 0, 1)
            act.wait_ge(s_scan, 1)
            act.activation(RB[0:8, :], t[0:8, 0, :], ACT.Copy).then_inc(s_rb, 1)
            evacuate_half(PANEL0["a_in"] + 16, 1)
            act.wait_ge(s_pad, 3)

            def cell_stage(n, pair, slot, early=False):
                if not early:
                    act.wait_ge(cell["scores"], n * 4 - 4)
                hold()
                for source, hi, _, scale in cell_qk(n, pair, slot):
                    last = act.activation(hi, source, ACT.Copy, scale=scale)
                last.then_inc(cell["qk_high"], 1)

            def cell_stage_v(n, slot, early=False):
                if not early:
                    act.wait_ge(cell["pv"], n - 1)
                hold()
                for source, hi, _, _ in staged_v("cell", n, None, slot):
                    act.activation(hi, source, ACT.Copy).then_inc(cell["v_high"], 1)

            def cell_head(n, pair, slot, nxt=True):
                zero = isinstance(n, int) and n == 0

                def weight(kb):
                    if not (zero and kb < 2):
                        act.wait_ge(cell["probs"], n * 4 + kb - 1)
                    act.wait_ge(cell["scores"], n * 4 + kb + 1)
                    hold()
                    act.activation(sq[:, kb % 2, 0:S - kb * P], T[kb % 2][:, 0:S - kb * P], ACT.Exp,
                                   bias=gsf[:, bass.ds(n + kb * 8, 1)]).then_inc(cell["exp"], 1)

                def pt_high(kb):
                    if kb == 0 and not zero:
                        act.wait_ge(cell["pv"], n)
                    act.wait_ge(cell["probs"], n * 4 + kb + 1)
                    act.activation(PT[:, 0, kb, kb * P:S], t[:, kb % 2, 0:S - kb * P], ACT.Copy)\
                        .then_inc(cell["pt_high"], 1)

                weight(0)
                weight(1)
                pt_high(0)
                if nxt:
                    cell_stage(n + 1, pair if slot == 0 else pair + 1, 1 - slot, zero)
                weight(2)
                pt_high(1)
                weight(3)
                pt_high(2)
                if nxt:
                    cell_stage_v(n + 1, 1 - slot, zero)
                pt_high(3)
                act.wait_ge(cell["guard"], n + 1)
                if not zero:
                    act.wait_ge(cell["out"], n)
                act.activation(X[:, 0, :], AD[:, :], ACT.Exp).then_inc(cell["gexp"], 1)
                act.wait_ge(cell["den"], n * 2 + 2)
                act.activation(X[:, 1, :], X[:, 1, :], ACT.Ln).then_inc(cell["den_log"], 1)
                act.wait_ge(cell["den_log"], n + 1)
                act.activation(X[:, 1, :], X[:, 1, :], ACT.Exp, scale=-1.0).then_inc(cell["den_inverse"], 1)

            cell_stage(0, 0, 0, True)
            cell_stage_v(0, 0, True)
            cell_head(0, 0, 0)
            with act.Fori(0, (HEADS - 2) // 2) as i:
                cell_head(i * 2 + 1, i, 1)
                cell_head(i * 2 + 2, i + 1, 0)
            cell_head(HEADS - 1, HEADS // 2 - 1, 1, False)
            act.wait_ge(cell["out"], HEADS)

            def cell_square(h):
                if h >= 2:
                    act.wait_ge(cell["mean"], h - 1)
                act.activation(sq[:, h % 2, :], Y[:, h, :], ACT.Square).then_inc(cell["square"], 1)

            cell_square(0)
            for h in range(HEADS):
                if h + 1 < HEADS:
                    cell_square(h + 1)
                act.wait_ge(cell["mean"], h + 1)
                if h >= 2:
                    act.wait_ge(cell["normed"], h - 1)
                act.activation(X[:, h % 2, :], ST[:, :], ACT.Ln, bias=eps[:, :], scale=1.0 / P)\
                    .then_inc(cell["log"], 1)
                act.wait_ge(cell["log"], h + 1)
                act.activation(X[:, h % 2, :], X[:, h % 2, :], ACT.Exp, scale=-0.5).then_inc(cell["root"], 1)
                if h:
                    act.wait_ge(cell["normed"], h)
                    high_chunk("cells", h - 1, yc, hh)
            act.wait_ge(cell["normed"], HEADS)
            high_chunk("cells", HEADS - 1, yc, hh)
            evacuate_squares("a_out", "a")
            root("a")
            squares("x_mlp0", xc, after_residual("a"))
            root("x_mlp0")
            high("x_mlp0", yc, hh, lambda m: adac[:, SH2 * 8 + m:SH2 * 8 + m + 1])
            feed_forward(*FFNS[1])
            root("mlp0")
            squares("x_b", xc, after_residual("mlp0"))
            root("x_b")
            high("x_kv", yc, hh, lambda m: adac[:, KVSH * 8 + m:KVSH * 8 + m + 1])

            def evacuate_small(p0, name, chunks, per_panel, proj0, dest, swap=None):
                n0, passed = before(PROJ, name), 0
                for c in range(chunks):
                    if c % per_panel == per_panel - 1 or c == chunks - 1:
                        p = p0 + c // per_panel
                        used(p, p % 2)
                    else:
                        passed += 1
                        act.wait_ge(s_proj, proj0 + passed)
                    last = act.activation(dest(c), G[(n0 + c) % 2][:, :], ACT.Copy)
                    turned = swap(c) if swap else None
                    if turned is not None:
                        for b in range(4):
                            r = b ^ 1
                            last = act.activation(turned[32 * r:32 * r + 32, :],
                                                  G[(n0 + c) % 2][32 * b:32 * b + 32, :], ACT.Copy)
                    last.then_inc(s_free, 1)

            act.wait_ge(s_rsin, 2)
            evacuate_small(PANEL0["kv_a"], "kv_a", 3, 1, 0, yc, lambda c: swapped[0] if c == 2 else None)
            evacuated("kv_a")
            squares("c_kv", yc, lambda m: None)
            act.wait_ge(s_roped, 1)
            act.activation(KR[:, 0, :], Y[:, 2, :], ACT.Copy).then_inc(s_kr, 1)
            root("c_kv")
            high("c_kv", yc, hh, lambda m: col("zero"))
            evacuate_small(PANEL0["kv_b"], "k_nope", 8, 4, 0, lambda c: QK[:, 8 + c, :])
            for half in range(2):
                used(PANEL0["kv_b"] + 2 + half, (PANEL0["kv_b"] + half) % 2)
                for tt in range(NT):
                    act.activation(V[:, tt, half * S:(half + 1) * S], value_banks[tt][:, :], ACT.Copy)\
                        .then_inc(s_vev, 1)
            high("x_b", yc, hh, lambda m: adac[:, (LAYER1 + SH1) * 8 + m:(LAYER1 + SH1) * 8 + m + 1])
            evacuate_small(PANEL0["q_a"], "q_a", 3, 1, 0, lambda c: Y[:, 3 + c, :])
            evacuated("q_a")
            squares("c_q", lambda m: Y[:, 3 + m, :], lambda m: None)
            root("c_q")
            high("c_q", lambda m: yc(3 + m), hh, lambda m: col("zero"))
            evacuate_small(PANEL0["q_b"], "q_nope", 8, 2, 6, lambda c: QK[:, c, :])

            def swap_q(c):
                if c >= 2:
                    act.wait_ge(s_roped, c)
                return swapped[c % 2]

            evacuate_small(PANEL0["q_b"] + 4, "q_rope", 4, 2, 10, lambda c: X[:, c, :], swap_q)
            act.wait_ge(s_roped, 5)
            act.wait_ge(s_pad, 4)
            attention("mla", HEADS, lambda n, pair, slot: [(Y[:, n, :], O[slot][:, :])])
            act.wait_ge(att["mla"]["out"], HEADS + 1)
            high("o_b", yc, hh)
            evacuate_squares("b_out", "b")
            root("b")
            squares("x_mlp1", xc, after_residual("b"))
            root("x_mlp1")
            high("x_mlp1", yc, hh, lambda m: adac[:, (LAYER1 + SH2) * 8 + m:(LAYER1 + SH2) * 8 + m + 1])
            feed_forward(*FFNS[2])
            root("mlp1")

        @block.vector
        def _(dve):
            chain = Chain(dve, s_dve)

            def low(out, source, hi, scale=1.0):
                return dve.scalar_tensor_tensor(out, source, scale, hi.bitcast(F32), ALU.mult, ALU.subtract)

            def add_square(name, m, width=S):
                at = [r[0] for r in STATS].index(name)
                if m == 1 and at:
                    dve.wait_ge(s_sum, before(SUMS, name))
                dve.wait_ge(s_sq, before(STATS, name) + m + 1)
                first = sq[:, 0, 0:width] if m == 1 else acc[:, 0:width]
                dve.tensor_tensor(acc[:, 0:width], first, sq[:, m % 2, 0:width], ALU.add).then_inc(s_add, 1)
                dve.wait_ge(s_add, before(ADDS, name) + m)

            def await_rstd(name, width=S):
                if name not in SUMMED_BY_PE and name not in ff:
                    for m in range(1, row(STATS, name)[1]):
                        add_square(name, m, width)
                dve.wait_ge(s_rstd, [r[0] for r in STATS].index(name) + 1)

            def make_scaled(name, source, gain, dest, shift, after=0, width=S, inv=None, work=None):
                _, count, _ = row(MAKES, name)
                h0, t0 = before(MAKES, name), before(MAKES_T, name)
                scale_by = rstd if inv is None else inv
                work = work or yc
                if after:
                    dve.wait_ge(s_used, after)

                def lows(m):
                    dve.wait_ge(s_hi, h0 + m + 1)
                    dve.scalar_tensor_tensor(dest(m), work(m), shift(m), dest_hi(m, name), ALU.add, ALU.subtract)\
                        .then_inc(s_h, 1)

                for m in range(count):
                    dve.scalar_tensor_tensor(work(m), source(m), gain(m), scale_by[:, 0:width],
                                             ALU.mult, ALU.mult).then_inc(s_t, 1)
                    if m >= 2:
                        lows(m - 2)
                for m in range(max(count - 2, 0), count):
                    lows(m)
                dve.wait_ge(s_h, h0 + count)

            def dest_hi(m, name):
                if name == "mem":
                    return HM[:, m, 0, :].bitcast(F32)
                return H[:, m + 4 if name == "o_chunk" else m, 0, :].bitcast(F32)

            def hl(m):
                return H[:, m, 1, :]

            def plain_low(name, m, source):
                dve.wait_ge(s_hi, before(MAKES, name) + m + 1)
                dve.tensor_tensor(H[:, m, 1, :], source(m), H[:, m, 0, :].bitcast(F32), ALU.subtract)\
                    .then_inc(s_h, 1)

            def make_plain(name, source):
                _, count, _ = row(MAKES, name)
                for m in range(count):
                    plain_low(name, m, source)
                dve.wait_ge(s_h, before(MAKES, name) + count)

            def residual(name, gain):
                base = 8 * RESID.index(name)

                def add(m):
                    if m not in POOL_ADDS:
                        dve.wait_ge(s_rt2, base + m + 1)
                        dve.tensor_tensor(x[:, m, :], x[:, m, :], Y[:, m, :], ALU.add).then_inc(s_res, 1)

                for m in range(KC):
                    dve.scalar_tensor_tensor(Y[:, m, :], Y[:, m, :], gain(m), rstd[:, :], ALU.mult, ALU.mult)\
                        .then_inc(s_rt2, 1)
                    if m:
                        add(m - 1)
                add(KC - 1)
                for m in range(KC):
                    await_x(dve, name, m)

            def adaptive(g0, n):
                with dve.Fori(0, n) if n > 1 else nullcontext(0) as i:
                    for k in range(KC):
                        dve.wait_ge(s_piece[k % 2], i * 64 + 16 * (4 * g0 + k // 2 + 1))
                        dve.scalar_tensor_tensor(apiece[:, k % 2, :], apiece[:, k % 2, :], 1.0, cond[:], ALU.mult,
                                                 ALU.mult, accum_out=adac[:, bass.ds(i * 8 + (g0 * 8 + k), 1)])\
                            .then_inc(s_pused, 1)
                dve.wait_ge(s_pused, 8 * (g0 + n))
                chain.link(dve.tensor_tensor(adac[:, 8 * g0:8 * (g0 + n)], adac[:, 8 * g0:8 * (g0 + n)],
                                             vec[:, VEC["ada_b"] + 8 * g0:VEC["ada_b"] + 8 * (g0 + n)], ALU.add))

            def one_plus(dest, scale_group, gain_col):
                chain.link(dve.scalar_tensor_tensor(dest, adac[:, scale_group * 8:scale_group * 8 + 8], 1.0,
                                                    vec[:, gain_col:gain_col + 8], ALU.add, ALU.mult))

            def gated(dest, gate_group, gain_col):
                chain.link(dve.tensor_tensor(dest, adac[:, gate_group * 8:gate_group * 8 + 8],
                                             vec[:, gain_col:gain_col + 8], ALU.mult))

            def norm_col(layer, which):
                return VEC["norm_g"] + (layer * 4 + which) * 8

            def gains(layer, group0):
                one_plus(pre_g[:, 3 * layer, :], group0 + SC1, norm_col(layer, 0))
                one_plus(pre_g[:, 3 * layer + 1, :], group0 + SC2, norm_col(layer, 2))
                gated(post_g[:, 2 * layer, :], group0 + G1, norm_col(layer, 1))
                gated(post_g[:, 2 * layer + 1, :], group0 + G2, norm_col(layer, 3))

            def log_gates(mixer, first, bias_col):
                for tt in range(NT):
                    chain.link(dve.tensor_tensor(gz[:, tt, :], AD[:, 16 * tt + first:16 * tt + first + 8],
                                                 vec[:, bias_col:bias_col + 8], ALU.add))
                dve.scalar_tensor_tensor(gw[:], gz[:], -1.0, gz[:], ALU.mult, ALU.min).then_inc(s_gz, 1)
                dve.wait_ge(s_gact, 2 * mixer + 2)
                chain.link(dve.scalar_tensor_tensor(lf[:], gz[:], 0.0, gw[:], ALU.min, ALU.subtract))

            def select_rows(dest, source, n):
                rows = source.shape[0]
                return dve.tensor_scalar(dest, source, con[0:rows, bass.ds(n + CON["minus_onehot"], 1)], None, ALU.mult)

            def clear_other_rows(panels_used, part_):
                dve.wait_ge(s_used, panels_used)
                dve.memset(QS[half_rows[1], 0, part_, :, :].bitcast(F32), 0.0)
                dve.memset(QS[half_rows[0], 1, part_, :, :].bitcast(F32), 0.0).then_inc(s_pad, 1)

            def attention(name, heads):
                sm = att[name]

                def stage_qk(n, pair, slot):
                    dve.wait_ge(sm["qk_high"], n + 1)
                    if name == "fox":
                        select_rows(RBS[:, slot, :], RB[:].bitcast(F32), n)
                    for source, hi, lo, scale in staged_qk(name, n, pair, slot):
                        last = low(lo, source, hi, scale)
                    last.then_inc(sm["qk_split"], 1)

                def stage_v(n, pair, slot):
                    dve.wait_ge(sm["v_high"], n + 1)
                    for source, hi, lo, _ in staged_v(name, n, pair, slot):
                        dve.tensor_tensor(lo, source, hi.bitcast(F32), ALU.subtract).then_inc(sm["v_split"], 1)

                def maximum(n, qb):
                    w = keys_of(name, qb)
                    dve.wait_ge(sm["scores"], n * 4 + qb + 1)
                    dve.tensor_reduce(stat[:, qb:qb + 1], G[qb % 2][:, 0:w], AX, ALU.max, negate=True)\
                        .then_inc(sm["max"], 1)

                def scale(n, qb):
                    w = keys_of(name, qb)
                    dve.wait_ge(sm["exp"], n * 4 + qb + 1)
                    dve.reciprocal(stat[:, 8 + qb:9 + qb], stat[:, 4 + qb:5 + qb]).then_inc(sm["recip"], 1)
                    dve.wait_ge(sm["recip"], n * 4 + qb + 1)
                    dve.tensor_scalar(t[:, qb % 2, 0:w], t[:, qb % 2, 0:w], stat[:, 8 + qb:9 + qb], None, ALU.mult)\
                        .then_inc(sm["probs"], 1)

                def pt_low(n, qb):
                    w = keys_of(name, qb)
                    dve.wait_ge(sm["pt_high"], n * 4 + qb + 1)
                    dve.tensor_tensor(PT[:, 1, 0:w // P, qb * P:(qb + 1) * P],
                                      T[qb % 2][:, 0:w].rearrange("p (k q) -> p k q", q=P),
                                      PT[:, 0, 0:w // P, qb * P:(qb + 1) * P].bitcast(F32), ALU.subtract)\
                        .then_inc(sm["pt_split"], 1)

                def head(n, slot, prev, nxt, next_pair):
                    maximum(n, 0)
                    if prev:
                        pt_low(n - 1, 3)
                    scale(n, 0)
                    maximum(n, 1)
                    if nxt:
                        stage_qk(n + 1, next_pair, 1 - slot)
                    scale(n, 1)
                    if nxt:
                        stage_v(n + 1, next_pair, 1 - slot)
                    pt_low(n, 0)
                    maximum(n, 2)
                    scale(n, 2)
                    pt_low(n, 1)
                    maximum(n, 3)
                    scale(n, 3)
                    pt_low(n, 2)

                stage_qk(0, 0, 0)
                stage_v(0, 0, 0)
                head(0, 0, False, True, 0)
                with dve.Fori(0, (heads - 2) // 2) as i:
                    head(i * 2 + 1, 1, True, True, i + 1)
                    head(i * 2 + 2, 0, True, True, i + 1)
                head(heads - 1, 1, True, False, None)
                pt_low(heads - 1, 3)

            def feed_forward(name, groups, gated_):
                sm = ff[name]
                up_banks = [G[1], AD] if gated_ else [G[0], G[1]]
                per = 2 if gated_ else 1
                dve.memset(Y[:], 0.0).then_inc(sm["added"], 4)
                dve.wait_ge(sm["added"], 4)

                def hidden(g, slot):
                    p = ff_up(name, g)
                    for j in range(2):
                        dve.wait_ge(sm["act"], g * 2 + j + 1)
                        if gated_:
                            dve.wait_ge(s_used, p + (2 * j + 2))
                            ins = dve.tensor_tensor(t[:, j, :], up_banks[j][:, :], t[:, j, :], ALU.mult)
                        else:
                            ins = dve.scalar_tensor_tensor(t[:, j, :], up_banks[j][:, :], 0.0, t[:, j, :],
                                                           ALU.max, ALU.mult)
                        ins.then_inc(sm["hidden"], 1)
                        dve.wait_ge(sm["high"], g * 2 + j + 1)
                        dve.tensor_tensor(HID[:, slot, j, 1, :], t[:, j, :], HID[:, slot, j, 0, :].bitcast(F32),
                                          ALU.subtract).then_inc(sm["split"], 1)

                def add(g, last_group=False):
                    p = ff_down(name, g, last_group)
                    for m in range(KC):
                        if m % 4 < 3:
                            dve.wait_ge(sm["down"], g * 6 + (m - m // 4 + 1))
                        else:
                            dve.wait_ge(s_used, p + (m // 4 + 1))
                        dve.tensor_tensor(Y[:, m, :], (T + O)[m % 4][:, :], Y[:, m, :], ALU.add)\
                            .then_inc(sm["added"], 1)
                        if last_group and m >= 2:
                            add_square(name, m - 1)
                    if last_group:
                        add_square(name, KC - 1)

                hidden(0, 0)
                with dve.Fori(0, (groups - 1) // 2) as i:
                    hidden(i * 2 + 1, 1)
                    add(i * 2)
                    hidden(i * 2 + 2, 0)
                    add(i * 2 + 1)
                if groups % 2 == 0:
                    hidden(groups - 1, 1)
                    add(groups - 2)
                add(groups - 1, True)
                dve.wait_ge(sm["added"], groups * 8 + 4)

            def vcol(name):
                return lambda m: col(name, m)

            def adash(group):
                return lambda m: adac[:, group * 8 + m:group * 8 + m + 1]

            def preg(i):
                return lambda m: pre_g[:, i, m:m + 1]

            def postg(i):
                return lambda m: post_g[:, i, m:m + 1]

            def xc(m):
                return x[:, m, :]

            def yc(m):
                return Y[:, m, :]

            def zero(m):
                return col("zero")

            dve.memset(eps[:], EPS).then_inc(s_eps, 1)
            dve.wait_ge(s_const, 32)
            await_rstd("x")
            make_scaled("x", xc, vcol("g_mix_pre"), hl, zero)
            dve.memset(RB[:].bitcast(F32), 0.0).then_inc(s_pad, 1)
            dve.wait_ge(s_wgh, 1)
            dve.tensor_tensor(wgateL[:], wgate[:], wgateH[:].bitcast(F32), ALU.subtract).then_inc(s_wg, 1)
            dve.wait_ge(s_cond, 1)
            adaptive(0, 4)
            dve.wait_ge(s_gl, 2)
            log_gates(0, 0, VEC["b_f"])
            dve.tensor_copy(gs[:], lf[:]).then_inc(s_gate, 1)
            adaptive(4, 1)
            dve.wait_ge(s_rb, 1)
            dve.tensor_tensor(RB[32:40, :], ST[0:8, :], RB[0:8, :].bitcast(F32), ALU.subtract).then_inc(s_rbl, 1)
            adaptive(5, 1)
            gains(0, 0)
            dve.wait_ge(s_rbl, 1)
            clear_other_rows(PANEL0["w_in"] + 24, 0)
            attention("fox", HEADS)
            attention("chunk", HEADS)
            await_rstd("mem", MEM)
            make_scaled("mem", lambda m: memf[:, m, :], vcol("g_mem_kv"), lambda m: HM[:, m, 1, :], zero, width=MEM,
                        work=lambda m: memf[:, m, :])
            await_rstd("fox")
            make_scaled("o_fox", yc, vcol("g_out"), hl, zero)
            await_rstd("chunk")
            make_scaled("o_chunk", lambda m: yc(4 + m), lambda m: col("g_out", 4 + m), lambda m: hl(4 + m), zero,
                        work=lambda m: yc(4 + m))
            await_rstd("mix")
            residual("mix", vcol("g_mix_post"))
            await_rstd("x_mem")
            make_scaled("x_mem", xc, vcol("g_mem_pre"), hl, zero)
            adaptive(6, 2)
            one_plus(pre_g[:, 2, :], KVSC, VEC["kv_norm_g"])
            dve.wait_ge(s_used, PANEL0["mem_o"])
            attention("mem", 4)
            make_plain("o_mem", yc)
            await_rstd("ca")
            residual("ca", vcol("g_mem_post"))
            await_rstd("x_ffn")
            make_scaled("x_ffn", xc, vcol("g_ffn_pre"), hl, zero)
            feed_forward(*FFNS[0])
            await_rstd("ffn")
            residual("ffn", vcol("g_ffn_post"))
            await_rstd("x_a")
            make_scaled("x_a", xc, preg(0), hl, adash(SH1))
            adaptive(8, 4)
            dve.wait_ge(s_gl, 4)
            for tt in range(NT):
                chain.link(dve.tensor_tensor(gi[:, tt, :], AD[:, 16 * tt:16 * tt + 8],
                                             vec[:, VEC["gate_b"]:VEC["gate_b"] + 8], ALU.add))
            log_gates(1, 8, VEC["gate_b"] + 8)
            dve.tensor_scalar(gz[:], lf[:], -1.0, None, ALU.mult).then_inc(s_gate, 1)
            adaptive(12, 1)
            dve.wait_ge(s_row, 4)
            dve.tensor_copy(gu[0:8, :], G[0][0:8, :]).then_inc(s_dve, 1)
            chain.n += 1
            dve.wait_ge(s_dve, chain.n)
            dve.tensor_tensor_scan(t[0:8, 0, :], gu[0:8, :], gu[0:8, :], 0.0, ALU.max, ALU.max).then_inc(s_scan, 1)
            dve.wait_ge(s_scan, 1)
            chain.link(dve.tensor_tensor(X[0:8, 2, :], G[1][0:8, :], t[0:8, 0, :], ALU.add))
            chain.link(dve.tensor_copy(gs[:], ST[:, 0:8 * NT].rearrange("p (a b) -> p a b", b=8)))
            dve.wait_ge(s_rb, 2)
            dve.tensor_tensor(RB[32:40, :], t[0:8, 0, :], RB[0:8, :].bitcast(F32), ALU.subtract).then_inc(s_rbl, 1)
            adaptive(13, 1)
            gains(1, LAYER1)
            dve.wait_ge(s_rbl, 2)
            clear_other_rows(PANEL0["a_in"] + 24, 0)

            def cell_stage(n, pair, slot):
                dve.wait_ge(cell["qk_high"], n + 1)
                select_rows(RBS[:, slot, :], RB[:].bitcast(F32), n)
                select_rows(cond[0:8, slot * S:(slot + 1) * S], X[0:8, 2, :], n)
                for source, hi, lo, scale in cell_qk(n, pair, slot):
                    last = low(lo, source, hi, scale)
                last.then_inc(cell["qk_split"], 1)

            def cell_stage_v(n, slot):
                dve.wait_ge(cell["v_high"], n + 1)
                for source, hi, lo, _ in staged_v("cell", n, None, slot):
                    dve.tensor_tensor(lo, source, hi.bitcast(F32), ALU.subtract).then_inc(cell["v_split"], 1)

            def cell_head(n, pair, slot, nxt=True):
                def weigh(kb):
                    dve.wait_ge(cell["exp"], n * 4 + kb + 1)
                    if not (isinstance(n, int) and n == 0 and kb < 2):
                        dve.wait_ge(cell["pt_split"], n * 4 + kb - 1)
                    dve.tensor_tensor(t[:, kb % 2, 0:S - kb * P], G[kb % 2][:, 0:S - kb * P],
                                      sq[:, kb % 2, 0:S - kb * P], ALU.mult).then_inc(cell["probs"], 1)

                def pt_low(kb):
                    dve.wait_ge(cell["pt_high"], n * 4 + kb + 1)
                    dve.tensor_tensor(PT[:, 1, kb, kb * P:S], t[:, kb % 2, 0:S - kb * P],
                                      PT[:, 0, kb, kb * P:S].bitcast(F32), ALU.subtract).then_inc(cell["pt_split"], 1)

                weigh(0)
                weigh(1)
                pt_low(0)
                if nxt:
                    cell_stage(n + 1, pair if slot == 0 else pair + 1, 1 - slot)
                weigh(2)
                pt_low(1)
                weigh(3)
                pt_low(2)
                if nxt:
                    cell_stage_v(n + 1, 1 - slot)
                pt_low(3)
                dve.wait_ge(cell["gexp"], n + 1)
                dve.wait_ge(cell["pv"], n + 1)
                dve.tensor_tensor(X[:, 1, :], O[1][:, :], X[:, 0, :], ALU.max).then_inc(cell["den"], 1)
                dve.wait_ge(cell["den"], n * 2 + 1)
                dve.scalar_tensor_tensor(X[:, 1, :], O[1][:, :], -1.0, X[:, 1, :], ALU.mult, ALU.max)\
                    .then_inc(cell["den"], 1)
                dve.wait_ge(cell["den_inverse"], n + 1)
                dve.tensor_tensor(Y[:, n, :], O[0][:, :], X[:, 1, :], ALU.mult).then_inc(cell["out"], 1)

            cell_stage(0, 0, 0)
            cell_stage_v(0, 0)
            cell_head(0, 0, 0)
            with dve.Fori(0, (HEADS - 2) // 2) as i:
                cell_head(i * 2 + 1, i, 1)
                cell_head(i * 2 + 2, i + 1, 0)
            cell_head(HEADS - 1, HEADS // 2 - 1, 1, False)
            dve.wait_ge(cell["out"], HEADS)
            for h in range(HEADS):
                dve.wait_ge(cell["root"], h + 1)
                chain.link(dve.scalar_tensor_tensor(Y[:, h, :], Y[:, h, :], col("head_g", h), X[:, h % 2, :],
                                                    ALU.mult, ALU.mult))
                dve.tensor_tensor(Y[:, h, :], Y[:, h, :], QK[:, 8 + h, :], ALU.mult).then_inc(cell["normed"], 1)
                dve.wait_ge(cell["normed"], h + 1)
                if h:
                    plain_low("cells", h - 1, yc)
            plain_low("cells", HEADS - 1, yc)
            dve.wait_ge(s_h, before(MAKES, "cells") + HEADS)
            dve.wait_ge(s_pos, 16)
            chain.link(dve.tensor_copy(ropeF, apiece[:].bitcast(I32)[:, 0, 0:S]))
            chain.link(dve.tensor_scalar(ropeA, ropeF, con[:, CON["inv_freq"]:CON["inv_freq"] + 1], None, ALU.mult))
            chain.link(dve.tensor_scalar(ropeB, ropeA, 1.0 / TURN, ROUND, ALU.mult, ALU.add))
            chain.link(dve.tensor_scalar(ropeB, ropeB, ROUND, None, ALU.subtract))
            for part_of_turn in TURN_PARTS:
                chain.link(dve.scalar_tensor_tensor(ropeA, ropeB, -part_of_turn, ropeA, ALU.mult, ALU.add))
            chain.link(dve.tensor_scalar(ropeA, ropeA, PI_IN, -PI_IN, ALU.min, ALU.max))
            chain.link(dve.scalar_tensor_tensor(ropeB, ropeA, -1.0, ropeA, ALU.mult, ALU.min))
            dve.tensor_scalar(ropeB, ropeB, float(TURN / 4), None, ALU.add).then_inc(s_rope, 1)
            await_rstd("a")
            residual("a", postg(0))
            await_rstd("x_mlp0")
            make_scaled("x_mlp0", xc, preg(1), hl, adash(SH2))
            feed_forward(*FFNS[1])
            await_rstd("mlp0")
            residual("mlp0", postg(1))
            await_rstd("x_b")
            chain.link(dve.tensor_copy(rstd_x, rstd[:]))
            make_scaled("x_kv", xc, preg(2), hl, adash(KVSH))

            def rotate(part_, turned, count):
                chain.link(dve.tensor_tensor(part_, part_, cos, ALU.mult))
                chain.link(dve.tensor_tensor(turned, turned, sin, ALU.mult))
                dve.tensor_tensor(part_, part_, turned, ALU.add).then_inc(s_roped, 1)
                dve.wait_ge(s_roped, count)

            dve.wait_ge(s_free, before(PROJ, "kv_a") + 3 + 2)
            rotate(Y[:, 2, :], swapped[0], 1)
            dve.wait_ge(s_kr, 1)
            chain.link(dve.tensor_tensor(KR[:, 1, :], Y[:, 2, :], KR[:, 0, :].bitcast(F32), ALU.subtract))
            await_rstd("c_kv")
            make_scaled("c_kv", yc, vcol("kv_latent_g"), hl, zero, after=PANEL0["kv_b"])
            make_scaled("x_b", xc, preg(3), hl, adash(LAYER1 + SH1), after=PANEL0["q_a"], inv=rstd_x)
            await_rstd("c_q")
            make_scaled("c_q", lambda m: yc(3 + m), vcol("q_latent_g"), hl, zero, after=PANEL0["q_b"],
                        work=lambda m: yc(3 + m))
            for m in range(4):
                dve.wait_ge(s_free, before(PROJ, "q_rope") + m + 3)
                rotate(X[:, m, :], swapped[m % 2], m + 2)
            clear_other_rows(PANEL0["b_out"], 1)
            attention("mla", HEADS)
            make_plain("o_b", yc)
            await_rstd("b")
            residual("b", postg(2))
            await_rstd("x_mlp1")
            make_scaled("x_mlp1", xc, preg(4), hl, adash(LAYER1 + SH2))
            feed_forward(*FFNS[2])
            await_rstd("mlp1")
            residual("mlp1", postg(3))


def _panels(w, chunks=None):
    k, n = w.shape
    return w.reshape(k // P, P, n // P, P).transpose(2, 1, 0, 3).reshape(n // P, P, k)


def _value_panels(w):
    k, n = w.shape
    return w.reshape(k // (2 * P), 2, P, n // S, S).transpose(3, 0, 2, 1, 4).reshape(-1, P, D)


def _few(w, per_panel):
    k, n = w.shape
    a = w.reshape(k // P, P, n // (P * per_panel), per_panel, P).transpose(2, 1, 3, 0, 4)
    a = a.reshape(n // (P * per_panel), P, per_panel * k)
    out = np.zeros((a.shape[0], P, D), np.float32)
    out[:, :, :a.shape[2]] = a
    return out


def _ffn_panels(up, down, per):
    first = up.reshape(-1, 2 * per, P, D)
    second = down.reshape(-1, 2, P, 2, S).transpose(0, 3, 2, 1, 4).reshape(-1, 2, P, D)
    out = [first[0]]
    for g in range(1, len(first)):
        out += [first[g], second[g - 1]]
    return np.concatenate(out + [second[-1]])


def _cols(v):
    return np.ascontiguousarray(v.reshape(-1, P).T)


def kernel(**inputs):
    import concourse.bacc as bacc
    from concourse.bass_utils import run_bass_kernel_spmd

    a = {k: np.asarray(v) for k, v in inputs.items()}
    w_in, a_in = a["w_in"][0], a["a_w_in_2"][0]
    gu = a["w_gate_up"][0]
    gate, up = _panels(gu[:, :DFF1]), _panels(gu[:, DFF1:])
    q_b = a["b_w_q_b_2"][0].reshape(384, HEADS, 192)
    kv_b = a["kv_w_b_2"].reshape(256, HEADS, 256)
    kv_a = a["kv_w_a_2"]
    panels = np.concatenate([
        _panels(np.concatenate([w_in[:, 0:1024], w_in[:, 1544:2568]], 1)),
        _value_panels(np.concatenate([w_in[:, 1024:1536], w_in[:, 2568:3080]], 1)),
        _panels(a["w_mem_kv"][0][:, :D]), _panels(a["w_out"][0]), _value_panels(a["w_mem_kv"][0][:, D:]),
        _panels(a["w_mem_q"][0]), _panels(a["w_mem_o"][0]),
        _ffn_panels(np.stack([gate, up], 1), a["w_down"][0].reshape(-1, P, D), 2),
        _panels(np.concatenate([a_in[:, 0:1024], a_in[:, 2064:3088]], 1)), _value_panels(a_in[:, 1024:2048]),
        _panels(a["a_w_out_2"][0]),
        _ffn_panels(_panels(a["mlp_w1_2"][0]), a["mlp_w2_2"][0].reshape(-1, P, D), 1),
        _panels(np.concatenate([kv_a, kv_a[:, 256:]], 1)),
        _few(kv_b[:, :, :P].reshape(256, D), 4), _value_panels(kv_b[:, :, P:].reshape(256, D)),
        _panels(a["b_w_q_a_2"][0]),
        _few(q_b[:, :, :P].reshape(384, D), 2), _few(q_b[:, :, P:].reshape(384, 512), 2),
        _panels(a["b_w_out_2"][0]),
        _ffn_panels(_panels(a["mlp_w1_2"][1]), a["mlp_w2_2"][1].reshape(-1, P, D), 1),
    ])
    ada = np.concatenate([
        w.T.reshape(-1, P, D)
        for w in (a["ada_w_2"][0], a["kv_ada_w_2"], a["ada_w_2"][1])])
    vecs = np.concatenate([
        _cols(a["g_mix_pre"]), _cols(np.concatenate([a["g_fox_out"][0], a["g_chunk_out"][0]])),
        _cols(a["g_mix_post"]), _cols(a["g_mem_pre"]), _cols(a["g_mem_kv"]), _cols(a["g_mem_post"]),
        _cols(a["g_ffn_pre"]), _cols(a["g_ffn_post"]), _cols(a["norm_g_2"]),
        _cols(np.concatenate([a["ada_b_2"][0], a["kv_ada_b_2"], a["ada_b_2"][1]])), _cols(a["kv_norm_g_2"]),
        _cols(a["a_head_g_2"][0]), _cols(a["kv_latent_g_2"]), _cols(a["b_q_latent_g_2"]),
        np.zeros((P, 8), np.float32), np.broadcast_to(a["b_fgate"][0], (P, 8)),
        np.broadcast_to(a["a_gate_b_2"][0].reshape(16), (P, 16))], 1)
    i = np.arange(P)
    onehot = np.zeros((P, 8), np.float32)
    onehot[:8] = -np.eye(8)
    onehot[32:40] = -np.eye(8)
    causal = np.where(i[None, :] <= i[:, None], 0.0, NEG)
    freq = 10000.0 ** (-(i % 32).astype(np.float32) / np.float32(32))
    cons = np.concatenate([
        np.eye(P), np.ones((P, P)), causal, causal.T, i[:, None] <= np.arange(S)[None, :], onehot,
        freq[:, None], np.where(i % 64 < 32, -1.0, 1.0)[:, None]], 1).astype(np.float32)
    gates_w = np.concatenate([w_in[:, 1536:1544], a_in[:, 2048:2064]], 1).reshape(KC, P, 24).transpose(1, 0, 2)
    dist = i[:, None] + P - np.arange(2 * P)[None, :]
    tile = a["rel_bias"][0][:, np.clip(dist, 1 - CH, REL) + CH - 1]
    tile = np.where((i[:, None] // CH < (np.arange(2 * P)[None, :] - P) // CH)[None], np.float32(NEG), tile)
    bias = tile.transpose(1, 0, 2).reshape(P, 2 * D)
    pos = np.broadcast_to(a["positions_2"].reshape(1, S), (P, S))
    arrays = {"xT": a["x"][0].T, "memT": a["mem"][0].T, "panels": panels, "ada": ada, "c": np.broadcast_to(a["c_2"], (P, D)), "vecs": vecs, "cons": cons,
              "gates_w": gates_w, "bias": bias, "pos": pos}
    arrays = {k: np.ascontiguousarray(v) for k, v in arrays.items()}
    nc = bacc.Bacc("TRN2", target_bir_lowering=False, num_devices=1)
    args = [nc.dram_tensor(k, v.shape, mybir.dt.from_np(v.dtype), kind="ExternalInput").ap() for k, v in arrays.items()]
    out = nc.dram_tensor("outT", (D, S), F32, kind="ExternalOutput").ap()
    program(nc, *args, out)
    r = run_bass_kernel_spmd(nc, [arrays], core_ids=[0])
    return np.ascontiguousarray(r.results[0]["outT"].T)[None]
```

```python
from contextlib import ExitStack, nullcontext

import numpy as np
import concourse.bass as bass
from concourse import mybir

F32 = mybir.dt.float32
F32R = mybir.dt.float32r
I32 = mybir.dt.int32
ALU = mybir.AluOpType
ACT = mybir.ActivationFunctionType
AX = mybir.AxisListType.X

P = 128
S = 512
D = 1024
KC = D // P
NT = S // P
MEM = 256
DFF1 = 2816
DFF2 = 4096
HEADS = 8
EPS = 1e-6
NEG = -1e30
REL = 128
CH = 64

PANELS = [("w_in", 24), ("mem_k", 8), ("w_out", 8), ("mem_v", 8), ("mem_q", 8), ("mem_o", 8), ("ffn", 3 * DFF1 // P),
          ("a_in", 24), ("a_out", 8), ("mlp0", 2 * DFF2 // P), ("kv_a", 3), ("q_a", 3), ("kv_b", 4), ("q_b", 6),
          ("b_out", 8), ("mlp1", 2 * DFF2 // P)]
PANEL0 = {}
_n = 0
for _name, _count in PANELS:
    PANEL0[_name] = _n
    _n += _count
NPANEL = _n
assert NPANEL % 2 == 0

PROJ = [("w_in", 16), ("mem_k", 8), ("w_out", 8), ("mem_q", 8), ("mem_o", 8), ("a_in", 16), ("a_out", 8),
        ("kv_a", 3), ("q_a", 3), ("k_nope", 8), ("q_nope", 8), ("q_rope", 4), ("b_out", 8)]
STATS = [("x", 8, D), ("mem", 8, D), ("fox", 4, 512), ("chunk", 4, 512), ("mix", 8, D), ("x_mem", 8, D),
         ("ca", 8, D), ("x_ffn", 8, D), ("ffn", 8, D), ("x_a", 8, D), ("a", 8, D), ("x_mlp0", 8, D), ("mlp0", 8, D), ("x_b", 8, D), ("c_kv", 2, 256), ("c_q", 3, 384),
         ("b", 8, D), ("x_mlp1", 8, D), ("mlp1", 8, D)]
MAKES = [("x", 8, 1), ("mem", 8, 1), ("o_fox", 4, 1), ("o_chunk", 4, 1), ("x_mem", 8, 1), ("o_mem", 8, 0), ("x_ffn", 8, 1),
         ("x_a", 8, 1), ("cells", 8, 0), ("x_mlp0", 8, 1), ("x_kv", 8, 1), ("x_b", 8, 1), ("c_kv", 2, 1),
         ("c_q", 3, 1), ("o_b", 8, 0), ("x_mlp1", 8, 1)]
MAKES_T = [(name, n * normed) for name, n, normed in MAKES]
TURN = 2 * np.pi
TURN_PARTS = (6.28125, float(np.float32(TURN - 6.28125)), float(TURN - 6.28125 - np.float32(TURN - 6.28125)))
PI_IN = 3.1415925
ROUND = 1.5 * 2 ** 23
RESID = ["mix", "ca", "ffn", "a", "mlp0", "b", "mlp1"]
FFNS = [("ffn", DFF1 // P // 2, True), ("mlp0", DFF2 // P // 2, False), ("mlp1", DFF2 // P // 2, False)]


VTILES = [("w_in", 8), ("mem", 4), ("a_in", 8), ("kv_b", 8)]
SUMMED_BY_PE = ["x", "x_ffn", "x_a", "x_mlp0", "x_b", "x_mlp1"]
ADDS = [(name, 0 if name in SUMMED_BY_PE else n - 1) for name, n, _ in STATS]
SUMS = [(name, n if name in SUMMED_BY_PE else 1) for name, n, _ in STATS]
POOL_ADDS = (1, 3, 5)


def ff_up(name, g):
    size = 6 if name == "ffn" else 4
    return PANEL0[name] if isinstance(g, int) and g == 0 else g * size + (PANEL0[name] - 2)


def ff_down(name, g, last=False):
    size = 6 if name == "ffn" else 4
    return g * size + (PANEL0[name] + (size - 2 if last else 2 * size - 4))


def before(table, name, column=1):
    total = 0
    for row in table:
        if row[0] == name:
            return total
        total += row[column]
    raise KeyError(name)


def row(table, name):
    return [r for r in table if r[0] == name][0]


VEC = {}
_v = 0
for _name, _count in [("g_mix_pre", 8), ("g_out", 8), ("g_mix_post", 8), ("g_mem_pre", 8), ("g_mem_kv", 8),
                      ("g_mem_post", 8), ("g_ffn_pre", 8), ("g_ffn_post", 8), ("norm_g", 64), ("ada_b", 112),
                      ("kv_norm_g", 8), ("head_g", 8), ("kv_latent_g", 2), ("q_latent_g", 3),
                      ("zero", 8), ("b_f", 8), ("gate_b", 16)]:
    VEC[_name] = _v
    _v += _count
NVEC = _v
CON = {}
_c = 0
for _name, _count in [("ident", P), ("ones", P), ("mask", P), ("maskT", P), ("upper", S), ("minus_onehot", 8),
                      ("inv_freq", 1), ("rope_sign", 1)]:
    CON[_name] = _c
    _c += _count
NCON = _c
SH1, SC1, G1, SH2, SC2, G2, KVSH, KVSC = range(8)
LAYER1 = 8


class Chain:

    def __init__(self, eng, sem):
        self.eng, self.sem, self.n = eng, sem, 0

    def link(self, ins):
        ins.then_inc(self.sem, 1)
        self.n = self.n + 1
        self.eng.wait_ge(self.sem, self.n)


def program(nc, xT, memT, panels, ada, c, vecs, cons, gates_w, bias, pos, outT):
    ctx = ExitStack()
    with ctx:
        def sb(name, shape, dt=F32, where=ctx):
            return where.enter_context(nc.sbuf_tensor(name, shape, dt))

        def sem(name):
            return ctx.enter_context(nc.semaphore(name))

        x = sb("x", [P, KC, S])
        Y = sb("Y", [P, KC, S])
        stage = sb("stage", [P, 2, D])
        WH = sb("WH", [P, 2, D], F32R)
        WL = sb("WL", [P, 2, D], F32R)
        apiece = sb("apiece", [P, 2, D])
        cond = sb("cond", [P, D])
        con = sb("con", [P, NCON])
        vec = sb("vec", [P, NVEC])
        adac = sb("adac", [P, 112])
        pre_g = sb("pre_g", [P, 5, KC])
        post_g = sb("post_g", [P, 4, KC])
        identr = sb("identr", [P, P], F32R)
        onesr = sb("onesr", [P, P], F32R)
        maskr = sb("maskr", [P, P], F32R)
        maskTr = sb("maskTr", [P, P], F32R)
        wgate = sb("wgate", [P, KC, 24])
        wgateH = sb("wgateH", [P, KC, 24], F32R)
        wgateL = sb("wgateL", [P, KC, 24], F32R)
        stat = sb("stat", [P, 24])
        lf = sb("lf", [P, NT, 8])
        gi = sb("gi", [P, NT, 8])
        gs = sb("gs", [P, NT, 8])
        gz = sb("gz", [P, NT, 8])
        gw = sb("gw", [P, NT, 8])
        sq = sb("sq", [P, 2, S])
        acc = sb("acc", [P, S])
        logs = sb("logs", [P, S])
        rstd = sb("rstd", [P, S])
        eps = sb("eps", [P, 1])
        t = sb("t", [P, 2, S])
        region = ExitStack()
        QK = sb("QK", [P, 16, S], F32, region)
        V = sb("V", [P, NT, D], F32, region)
        X = sb("X", [P, 4, S], F32, region)
        part = ExitStack()
        H = sb("H", [P, KC, 2, S], F32R, part)
        HM = sb("HM", [P, KC, 2, MEM], F32R, part)
        part.close()
        part = ExitStack()
        QS = sb("QS", [P, 2, 2, 2, S], F32R, part)
        KS = sb("KS", [P, 2, 2, S], F32R, part)
        VS = sb("VS", [P, 2, 2, S], F32R, part)
        PT = sb("PT", [P, 2, NT, S], F32R, part)
        RB = sb("RB", [40, S], F32R, part)
        RBS = sb("RBS", [40, 2, S], F32R, part)
        part.close()
        part = ExitStack()
        sb("under_hc", [P, KC * 2 * S], F32R, part)
        HC = sb("HC", [P, 2, 2, S], F32R, part)
        part.close()
        part = ExitStack()
        sb("under_kr", [P, 24 * S], F32R, part)
        KR = sb("KR", [P, 2, S], F32R, part)
        part.close()
        region.close()
        region = ExitStack()
        HID = sb("HID", [P, 2, 2, 2, S], F32R, region)
        region.close()

        bank = [ctx.enter_context(nc.psum_tensor(f"bank{i}", [P, S], F32)) for i in range(8)]
        G, T, O = bank[0:2], bank[2:4], bank[4:6]
        ST, AD = bank[6], bank[7]

        ident = con[:, CON["ident"]:CON["ident"] + P]
        ones = con[:, CON["ones"]:CON["ones"] + P]
        upper = con[:, CON["upper"]:CON["upper"] + S]

        memf = V[:, 0:2, :].rearrange("p a (c t) -> p (a c) t", t=MEM)
        memK = QK[:, 8:12, :].rearrange("p a (c t) -> p (a c) t", t=MEM)
        QKf = QK[:].rearrange("p a b -> p (a b)")
        Xf = X[:].rearrange("p a b -> p (a b)")
        ropeF, ropeA, ropeB = apiece[:, 0, S:2 * S], apiece[:, 1, 0:S], apiece[:, 1, S:2 * S]
        swapped = [apiece[:, 0, 0:S], apiece[:, 0, S:2 * S]]
        gu = sq[:, 1, :]
        gsf = gs[:].rearrange("p a b -> p (a b)")
        cos, sin = cond[:, 0:S], cond[:, S:2 * S]
        score_bank = [G[0], G[1], ST, AD]
        prob = [t[:, 0, :], t[:, 1, :], sq[:, 0, :], sq[:, 1, :]]
        half_rows = [slice(0, 64), slice(64, 128)]

        def col(name, m=0):
            return vec[:, VEC[name] + m:VEC[name] + m + 1]

        def await_x(eng, name, m):
            base = RESID.index(name)
            if m in POOL_ADDS:
                eng.wait_ge(s_resp, len(POOL_ADDS) * base + POOL_ADDS.index(m) + 1)
            else:
                by_vector = [c for c in range(KC) if c not in POOL_ADDS]
                eng.wait_ge(s_res, len(by_vector) * base + by_vector.index(m) + 1)

        def attention_rounds(eng, heads, start, round_, end):
            def around(n, i=None):
                def head(k):
                    return (k, k // 2, k % 2) if i is None else (i * 2 + k, i + k // 2, k % 2)
                there = [head(n + d) if i is not None or 0 <= n + d < heads else None for d in (-1, 0, 1, 2)]
                round_(*there)

            start()
            around(0)
            if heads > 4:
                with eng.Fori(0, (heads - 4) // 2) as i:
                    around(1, i)
                    around(2, i)
            for n in range(heads - 3, heads):
                around(n)
            end()

        s_const = sem("const_loaded")
        s_x = sem("x_loaded")
        s_x2 = sem("x_rest_loaded")
        s_mem = sem("mem_loaded")
        s_gw = sem("gate_weights_loaded")
        s_bias = sem("bias_loaded")
        s_pos = sem("positions_loaded")
        s_stage = [sem("panel0_loaded"), sem("panel1_loaded")]
        s_split = sem("panel_split")
        s_hisplit = sem("panel_high")
        s_used = sem("panel_used")
        s_piece = [sem("piece0_loaded"), sem("piece1_loaded")]
        s_pused = sem("piece_used")
        s_proj = sem("projected")
        s_free = sem("projection_bank_free")
        s_vev = sem("values_evacuated")
        s_sq = sem("squares")
        s_add = sem("squares_added")
        s_sum = sem("squares_summed")
        s_log = sem("mean_squares_log")
        s_rstd = sem("rstd_ready")
        s_t = sem("scaled")
        s_hi = sem("input_high")
        s_h = sem("input_split")
        s_hold = sem("waits_held")
        s_phold = sem("pool_waits_held")
        s_eps = sem("eps_set")
        s_wgh = sem("gate_weights_high")
        s_gz = sem("gate_magnitude")
        s_scan = sem("running_max")
        s_rbl = sem("rows_split")
        s_kr = sem("shared_keys_high")
        s_res = sem("residual_added")
        s_resp = sem("residual_added_by_pool")
        s_rt2 = sem("residual_scaled")
        s_dve = sem("vector_chain")
        s_act = sem("scalar_chain")
        s_cr = sem("consts_rounded")
        s_wg = sem("gate_weights_split")
        s_gl = sem("gate_logits")
        s_glr = sem("gate_logit_rows")
        s_gact = sem("gate_exp_ln")
        s_gate = sem("gates_ready")
        s_row = sem("gate_rows")
        s_rb = sem("rows_high")
        s_c = sem("condition_loaded")
        s_cond = sem("cond_ready")
        s_out = sem("out_stored")
        s_rope = sem("rope_angles")
        s_rsin = sem("rope_sines")
        s_roped = sem("rotated")
        att = {}
        for name in ("fox", "chunk", "mem", "mla"):
            att[name] = {k: sem(f"{name}_{k}") for k in (
                "qk_high", "qk_split", "v_high", "v_split", "scores", "max", "exp", "probs", "turned",
                "pt_high", "pt_split", "pv", "out", "recip", "side")}
        s_pad = sem("queries_padded")
        cell = {k: sem(f"cell_{k}") for k in (
            "qk_high", "qk_split", "v_high", "v_split", "scores", "exp", "probs", "pt_high", "pt_split",
            "pv", "side", "guard", "gexp", "den", "normed", "out", "square", "mean", "log", "root", "den_log", "den_inverse")}
        ff = {}
        for name, _, _ in FFNS:
            ff[name] = {k: sem(f"{name}_{k}") for k in ("act", "hidden", "high", "split", "down", "added")}

        block = ctx.enter_context(nc.Block())

        def staged_qk(name, n, pair, slot):
            if name == "mem":
                return [(QK[:, bass.ds(n * 2, 2), :], QS[:, slot, :, 0, :], QS[:, slot, :, 1, :]),
                        (QKf[:, bass.ds(n * S + 8 * S, S)], KS[:, slot, 0, :], KS[:, slot, 1, :])]
            rows = half_rows[slot]
            if name == "mla":
                return [(QK[:, n, :], QS[:, slot, 0, 0, :], QS[:, slot, 0, 1, :]),
                        (X[rows, pair, :], QS[rows, slot, 1, 0, :], QS[rows, slot, 1, 1, :]),
                        (QK[:, n + 8, :], KS[:, slot, 0, :], KS[:, slot, 1, :])]
            first = 8 if name == "chunk" else 0
            return [(QK[rows, pair + first, :], QS[rows, slot, 0, 0, :], QS[rows, slot, 0, 1, :]),
                    (QK[:, pair + (first + 4), :], KS[:, slot, 0, :], KS[:, slot, 1, :])]

        def by_vector(name):
            return 1 if name in ("mem", "mla") else 0

        def staged_v(name, n, pair, slot):
            wide = dict(b=MEM if name == "mem" else P)
            if name == "mem":
                src = V[:, 2:4, bass.ds(n * MEM, MEM)]
            elif name in ("fox", "chunk"):
                src = V[:, :, bass.ds(pair * P + (S if name == "chunk" else 0), P)]
            else:
                src = V[:, :, bass.ds(n * P, P)]
            return (src, VS[:, slot, 0, :].rearrange("p (a b) -> p a b", **wide),
                    VS[:, slot, 1, :].rearrange("p (a b) -> p a b", **wide))

        def keys_of(name, qb):
            return MEM if name == "mem" else (qb + 1) * P

        value_banks = [T[0], T[1], O[0], O[1]]

        @block.sync
        def _(sp):
            sp.dma_start(x[:, 0:4, :], xT[0:4 * P, :].rearrange("(c p) t -> p c t", p=P)).then_inc(s_x, 16)
            sp.dma_start(con[:], cons).then_inc(s_const, 16)
            sp.dma_start(x[:, 4:8, :], xT[4 * P:8 * P, :].rearrange("(c p) t -> p c t", p=P)).then_inc(s_x2, 16)
            sp.dma_start(vec[:], vecs).then_inc(s_const, 16)

            def load_panel(p, slot, first=False):
                if not first:
                    sp.wait_ge(s_split, p - 1)
                sp.dma_start(stage[:, slot, :], panels[p]).then_inc(s_stage[slot], 16)

            def load_piece(q, slot, first=False):
                if not first:
                    sp.wait_ge(s_pused, q - 1)
                sp.dma_start(apiece[:, slot, :], ada[q]).then_inc(s_piece[slot], 16)

            def start_pieces(p0, q0):
                for j in range(4):
                    load_panel(p0 + j, j % 2, p0 + j < 2)
                    if j in (0, 1):
                        load_piece(q0 + j, j, q0 == 0)

            def with_pieces(p0, q0, n):
                with sp.Fori(0, n) as i:
                    for j in range(4):
                        load_panel(i * 4 + (p0 + j), j % 2)
                        load_piece(i * 8 + (q0 + 2 * j), 0)
                        load_piece(i * 8 + (q0 + 2 * j + 1), 1)

            def end_pieces(p0, q0, panels):
                for j in range(max(panels, 3)):
                    if j < panels:
                        load_panel(p0 + j, j % 2)
                    if j < 3:
                        load_piece(q0 + 2 * j, 0)
                        load_piece(q0 + 2 * j + 1, 1)

            def plain(p0, p1):
                if p1 - p0 >= 4:
                    with sp.Fori(0, (p1 - p0) // 2) as i:
                        for j in range(2):
                            load_panel(i * 2 + (p0 + j), j)
                else:
                    for p in range(p0, p1):
                        load_panel(p, p % 2)

            sp.dma_start(cond[:], c).then_inc(s_c, 16)
            sp.dma_start(wgate[:], gates_w).then_inc(s_gw, 16)
            start_pieces(0, 0)
            with_pieces(4, 2, 4)
            end_pieces(20, 34, 6)
            sp.dma_start(X[:].rearrange("p a b -> p (a b)"), bias).then_inc(s_bias, 16)
            sp.wait_ge(att["chunk"]["v_split"], HEADS)
            sp.dma_start(memf, memT.rearrange("(c p) t -> p c t", p=P)).then_inc(s_mem, 16)
            plain(26, PANEL0["ffn"])
            p0, q0 = PANEL0["ffn"], 40
            plain(p0, p0 + 12)
            load_piece(q0, 0)
            load_piece(q0 + 1, 1)
            with sp.Fori(0, 4) as i:
                for half in range(2):
                    for j in range(6):
                        load_panel(i * 12 + (p0 + 12 + 6 * half + j), j % 2)
                        if j < 4:
                            load_piece(i * 8 + (q0 + 2 + 4 * half + j), j % 2)
            for j in range(6):
                load_panel(p0 + 60 + j, j % 2)
                if j < 4:
                    load_piece(q0 + 34 + j, j % 2)
            load_piece(q0 + 38, 0)
            load_piece(q0 + 39, 1)
            plain(p0 + 66, p0 + 68)
            p0, q0 = PANEL0["a_in"], 80
            plain(p0 + 2, p0 + 4)
            load_piece(q0, 0)
            load_piece(q0 + 1, 1)
            with_pieces(p0 + 4, q0 + 2, 3)
            plain(p0 + 16, p0 + 18)
            end_pieces(p0 + 18, q0 + 26, 6)
            sp.wait_ge(s_pused, 112)
            sp.dma_start(apiece[:].bitcast(I32)[:, 0, 0:S], pos).then_inc(s_pos, 16)
            plain(PANEL0["a_out"], NPANEL)
            for m in range(KC):
                await_x(sp, "mlp1", m)
                sp.dma_start(outT[m * P:(m + 1) * P, :], x[:, m, :]).then_inc(s_out, 16)
            sp.wait_ge(s_out, 16 * KC)

        @block.gpsimd
        def _(pool):
            def split_low(p, slot):
                pool.wait_ge(s_hisplit, p + 1)
                pool.tensor_tensor(WL[:, slot, :], stage[:, slot, :], WH[:, slot, :].bitcast(F32),
                                   ALU.subtract).then_inc(s_split, 1)

            def split_lows(p0, p1):
                with pool.Fori(0, (p1 - p0) // 2) as i:
                    for slot in range(2):
                        split_low(i * 2 + (p0 + slot), slot)

            def residual(name):
                base = 8 * RESID.index(name)
                for m in POOL_ADDS:
                    pool.wait_ge(s_rt2, base + m + 1)
                    pool.tensor_tensor(x[:, m, :], x[:, m, :], Y[:, m, :], ALU.add).then_inc(s_resp, 1)

            def low_qk(name, sm, head):
                n, pair, slot = head
                pool.wait_ge(sm["qk_high"], n + 1)
                pool.sem_inc(s_phold, 1)
                for k, (source, hi, lo) in enumerate(staged_qk(name, n, pair, slot)):
                    if k != by_vector(name):
                        last = pool.tensor_tensor(lo, source, hi.bitcast(F32), ALU.subtract)
                last.then_inc(sm["qk_split"], 1)

            def low_v(name, sm, head):
                n, pair, slot = head
                pool.wait_ge(sm["v_high"], n + 1)
                pool.sem_inc(s_phold, 1)
                source, hi, lo = staged_v(name, n, pair, slot)
                pool.tensor_tensor(lo, source, hi.bitcast(F32), ALU.subtract).then_inc(sm["v_split"], 1)

            def attention(name, heads):
                sm = att[name]
                low_qk(name, sm, (0, 0, 0))
                low_v(name, sm, (0, 0, 0))
                low_qk(name, sm, (1, 0, 1))
                with pool.Fori(0, heads // 2 - 1) as i:
                    low_v(name, sm, (i * 2 + 1, i, 1))
                    low_qk(name, sm, (i * 2 + 2, i + 1, 0))
                    low_v(name, sm, (i * 2 + 2, i + 1, 0))
                    low_qk(name, sm, (i * 2 + 3, i + 1, 1))
                low_v(name, sm, (heads - 1, heads // 2 - 1, 1))

            def cells():
                low_qk("cell", cell, (0, 0, 0))
                low_v("cell", cell, (0, 0, 0))
                with pool.Fori(0, HEADS // 2 - 1) as i:
                    for head in ((i * 2 + 1, i, 1), (i * 2 + 2, i + 1, 0)):
                        low_qk("cell", cell, head)
                        low_v("cell", cell, head)
                low_qk("cell", cell, (HEADS - 1, HEADS // 2 - 1, 1))
                low_v("cell", cell, (HEADS - 1, HEADS // 2 - 1, 1))

            split_lows(0, PANEL0["mem_k"] + 2)
            attention("fox", HEADS)
            attention("chunk", HEADS)
            split_lows(PANEL0["mem_k"] + 2, PANEL0["mem_v"] + 2)
            residual("mix")
            split_lows(PANEL0["mem_v"] + 2, PANEL0["mem_o"] + 2)
            attention("mem", 4)
            split_lows(PANEL0["mem_o"] + 2, PANEL0["ffn"] + 2)
            residual("ca")
            split_lows(PANEL0["ffn"] + 2, PANEL0["a_in"] + 2)
            residual("ffn")
            split_lows(PANEL0["a_in"] + 2, PANEL0["a_out"] + 2)
            cells()
            split_lows(PANEL0["a_out"] + 2, PANEL0["mlp0"] + 2)
            residual("a")
            split_lows(PANEL0["mlp0"] + 2, PANEL0["kv_a"] + 2)
            residual("mlp0")
            split_lows(PANEL0["kv_a"] + 2, PANEL0["b_out"] + 2)
            attention("mla", HEADS)
            split_lows(PANEL0["b_out"] + 2, PANEL0["mlp1"] + 2)
            residual("b")
            split_lows(PANEL0["mlp1"] + 2, NPANEL)
            residual("mlp1")

        @block.tensor
        def _(pe):
            def three(out, wh, wl, rh, rl, start, stop):
                pe.matmul(out, wh, rh, start=start, stop=False)
                pe.matmul(out, wh, rl, start=False, stop=False)
                return pe.matmul(out, wl, rh, start=False, stop=stop)

            def chunk_of(p, n, slot, src, width, fresh=None):
                pe.wait_ge(s_split, p + 1)
                pe.wait_ge(s_free, n + 1)
                for k in range(KC):
                    input_chunk(fresh, k)
                    last = three(G[slot][:, 0:width], WH[:, slot, k * P:(k + 1) * P],
                                 WL[:, slot, k * P:(k + 1) * P], src[:, k, 0, 0:width], src[:, k, 1, 0:width],
                                 k == 0, k == KC - 1)
                last.then_inc(s_used, 1)

            def project(name, count, fresh):
                p0, n0 = PANEL0[name], before(PROJ, name)
                for j in range(2):
                    chunk_of(p0 + j, n0 + j, j % 2, H, S, fresh if j == 0 else None)
                with pe.Fori(1, count // 2) as i:
                    for j in range(2):
                        chunk_of(i * 2 + (p0 + j), i * 2 + (n0 + j), j % 2, H, S)

            def value_panel(p, pp, tiles, src=H):
                slot = pp % 2
                pe.wait_ge(s_split, p + 1)
                for kk in range(2):
                    k = 2 * pp + kk
                    for tt in range(tiles):
                        last = three((T + O)[tt][:, :], src[:, k, 0, tt * P:(tt + 1) * P],
                                     src[:, k, 1, tt * P:(tt + 1) * P], WH[:, slot, kk * S:(kk + 1) * S],
                                     WL[:, slot, kk * S:(kk + 1) * S], k == 0, k == KC - 1)
                last.then_inc(s_used, 1)

            def values_half(p0, name, half, gates=None):
                pe.wait_ge(s_vev, half * NT + before(VTILES, name) + 1)
                for pp in range(4):
                    value_panel(p0 + half * 4 + pp, pp, NT)
                    if gates is not None and pp == 0:
                        turn_logits(*gates)

            def input_chunk(name, k):
                if name == "o":
                    pe.wait_ge(s_h, before(MAKES, "o_fox") + k + 1)
                elif name is not None:
                    pe.wait_ge(s_h, before(MAKES, name) + k + 1)

            def mean_square(name, width=S):
                at = [r[0] for r in STATS].index(name)
                if at:
                    pe.wait_ge(s_log, at)
                if name in SUMMED_BY_PE:
                    for m in range(KC):
                        pe.wait_ge(s_sq, before(STATS, name) + m + 1)
                        pe.matmul(ST[:, :], ones, sq[:, m % 2, :], start=m == 0, stop=m == KC - 1).then_inc(s_sum, 1)
                else:
                    pe.wait_ge(s_add, before(ADDS, name) + row(ADDS, name)[1])
                    pe.matmul(ST[:, 0:width], ones, acc[:, 0:width], start=True, stop=True).then_inc(s_sum, 1)

            def gate_logits(first, n):
                for k in range(KC):
                    last = three(ST[0:n, :], wgateH[:, k, first:first + n], wgateL[:, k, first:first + n],
                                 H[:, k, 0, :], H[:, k, 1, :], k == 0, k == KC - 1)
                last.then_inc(s_gl, 1)

            def turn_logits(mixer, n):
                pe.wait_ge(s_glr, mixer + 1)
                for tt in range(NT):
                    last = pe.transpose(AD[:, 16 * tt:16 * tt + n], t[0:n, 0, tt * P:(tt + 1) * P], ident[0:n, 0:n])
                last.then_inc(s_gl, 1)

            def cumulate(out, gate, stop=True):
                for st in range(NT):
                    last = pe.matmul(out[0:8, st * P:S], gate[:, st, :], upper[:, 0:S - st * P],
                                     start=st == 0, stop=stop and st == NT - 1, skip_group_check=True)
                return last

            def attention(name, heads, scores, turned_tiles, pv):
                sm = att[name]

                def score(head, qb):
                    n, _, slot = head
                    if qb == 0:
                        pe.wait_ge(sm["qk_split"], n + 1)
                        pe.wait_ge(sm["side"], n + 1)
                    if not (isinstance(n, int) and n == 0):
                        pe.wait_ge(sm["exp"], n * 4 + (qb - 3))
                    scores(n, slot, qb, score_bank[qb]).then_inc(sm["scores"], 1)

                def turn(head, qb):
                    n = head[0]
                    pe.wait_ge(sm["probs"], n * 4 + (qb + 1))
                    if not (isinstance(n, int) and n == 0 and qb < 2):
                        pe.wait_ge(sm["pt_split"], n * 4 + (qb - 1))
                    for kb in range(turned_tiles(qb)):
                        last = pe.transpose(T[qb % 2][:, kb * P:(kb + 1) * P], prob[qb][:, kb * P:(kb + 1) * P], ident)
                    last.then_inc(sm["turned"], 1)

                def weigh(head):
                    n, _, slot = head
                    pe.wait_ge(sm["pt_split"], n * 4 + 4)
                    pe.wait_ge(sm["v_split"], n + 1)
                    pe.wait_ge(sm["out"], n + 1)
                    pv(n, slot).then_inc(sm["pv"], 1)

                def start():
                    for qb in range(NT):
                        score((0, 0, 0), qb)

                def round_(prev, now, nxt, _):
                    for qb in range(NT):
                        turn(now, qb)
                        if nxt:
                            score(nxt, qb)
                        if qb == 0 and prev:
                            weigh(prev)

                attention_rounds(pe, heads, start, round_, lambda: weigh((heads - 1, None, (heads - 1) % 2)))

            def qk(out, slot, part_, qb, kh, kl, width, start, stop):
                return three(out[:, 0:width], QS[:, slot, part_, 0, qb * P:(qb + 1) * P],
                             QS[:, slot, part_, 1, qb * P:(qb + 1) * P], kh, kl, start, stop)

            def causal_pv(n, slot):
                for kb in range(NT):
                    last = three(O[slot][:, kb * P:S], VS[:, slot, 0, kb * P:(kb + 1) * P],
                                 VS[:, slot, 1, kb * P:(kb + 1) * P], PT[:, 0, kb, kb * P:S], PT[:, 1, kb, kb * P:S],
                                 kb == 0, kb == NT - 1)
                return last

            def fox_scores(n, slot, qb, out):
                w = (qb + 1) * P
                qk(out, slot, 0, qb, KS[:, slot, 0, 0:w], KS[:, slot, 1, 0:w], w, True, False)
                pe.matmul(out[:, 0:w], onesr[0:40, :], RBS[:, slot, 0:w], start=False, stop=False)
                return pe.matmul(out[:, qb * P:w], identr[:, :], maskr[:, :], start=False, stop=True)

            def chunk_scores(n, slot, qb, out):
                w = (qb + 1) * P
                near = max(0, qb - 1) * P
                qk(out, slot, 0, qb, KS[:, slot, 0, 0:w], KS[:, slot, 1, 0:w], w, True, False)
                if near:
                    pe.matmul(out[:, 0:near], ident, Xf[:, bass.ds(n * 256, 1)].to_broadcast([P, near]),
                              start=False, stop=False)
                return pe.matmul(out[:, near:w], ident, Xf[:, bass.ds(n * 256 + (256 - (w - near)), w - near)],
                                 start=False, stop=True)

            def mem_scores(n, slot, qb, out):
                for c in range(2):
                    last = qk(out, slot, c, qb, KS[:, slot, 0, c * MEM:(c + 1) * MEM],
                              KS[:, slot, 1, c * MEM:(c + 1) * MEM], MEM, c == 0, c == 1)
                return last

            def mem_pv(n, slot):
                for dc in range(2):
                    for kb in range(2):
                        at = kb * MEM + dc * P
                        last = three(O[dc][:, :], VS[:, slot, 0, at:at + P], VS[:, slot, 1, at:at + P],
                                     PT[:, 0, kb, :], PT[:, 1, kb, :], kb == 0, kb == 1)
                return last

            def mla_scores(n, slot, qb, out):
                w = (qb + 1) * P
                qk(out, slot, 0, qb, KS[:, slot, 0, 0:w], KS[:, slot, 1, 0:w], w, True, False)
                qk(out, slot, 1, qb, KR[:, 0, 0:w], KR[:, 1, 0:w], w, False, False)
                return pe.matmul(out[:, qb * P:w], identr[:, :], maskr[:, :], start=False, stop=True)

            def feed_forward(name, groups, gated):
                sm = ff[name]
                banks = [G[0], G[1], ST, AD] if gated else [G[0], None, G[1], None]
                per = 2 if gated else 1

                def up(g, slot):
                    p = ff_up(name, g)
                    for j in range(2):
                        for u in range(per):
                            q = j * per + u
                            pe.wait_ge(s_split, p + (q + 1))
                            if not (isinstance(g, int) and g == 0):
                                pe.wait_ge(sm["hidden"], g * 2 + j - 1)
                            for k in range(KC):
                                if isinstance(g, int) and g == 0 and q == 0:
                                    input_chunk("x_" + name, k)
                                last = three(banks[2 * j + u][:, :], WH[:, q % 2, k * P:(k + 1) * P],
                                             WL[:, q % 2, k * P:(k + 1) * P], H[:, k, 0, :], H[:, k, 1, :],
                                             k == 0, k == KC - 1)
                            last.then_inc(s_used, 1)

                def down(g, slot, last_group=False):
                    p = ff_down(name, g, last_group)
                    pe.wait_ge(sm["split"], g * 2 + 2)
                    for m in range(KC):
                        half, at = m // 4, m % 4 * P
                        if m % 4 == 0:
                            pe.wait_ge(s_split, p + (half + 1))
                        pe.wait_ge(sm["added"], g * 8 + (m + 1))
                        for j in range(2):
                            last = three((T + O)[m % 4][:, :], WH[:, half, j * S + at:j * S + at + P],
                                         WL[:, half, j * S + at:j * S + at + P],
                                         HID[:, slot, j, 0, :], HID[:, slot, j, 1, :], j == 0, j == 1)
                        last.then_inc(s_used if m % 4 == 3 else sm["down"], 1)
                    if last_group:
                        mean_square(name)

                up(0, 0)
                with pe.Fori(0, (groups - 1) // 2) as i:
                    up(i * 2 + 1, 1)
                    down(i * 2, 0)
                    up(i * 2 + 2, 0)
                    down(i * 2 + 1, 1)
                if groups % 2 == 0:
                    up(groups - 1, 1)
                    down(groups - 2, 0)
                down(groups - 1, (groups - 1) % 2, True)

            def small_project(p0, n0, chunks, ks, per_panel, fresh=None, src=H, after_chunk=None):
                for c in range(chunks):
                    p, at = p0 + c // per_panel, c % per_panel
                    slot, n = p % 2, n0 + c
                    if at == 0:
                        pe.wait_ge(s_split, p + 1)
                    pe.wait_ge(s_free, n + 1)
                    for k in range(ks):
                        if c == 0:
                            input_chunk(fresh, k)
                        w = (at * ks + k) * P
                        last = three(G[n % 2][:, :], WH[:, slot, w:w + P], WL[:, slot, w:w + P],
                                     src[:, k, 0, :], src[:, k, 1, :], k == 0, k == ks - 1)
                    last.then_inc(s_used if at == per_panel - 1 or c == chunks - 1 else s_proj, 1)
                    if after_chunk and c == after_chunk[0]:
                        mean_square(after_chunk[1])

            pe.wait_ge(s_const, 32)
            mean_square("x")
            project("w_in", 16, "x")
            pe.wait_ge(s_wg, 1)
            gate_logits(0, 8)
            values_half(PANEL0["w_in"] + 16, "w_in", 0, (0, 8))
            pe.wait_ge(s_gate, 1)
            cumulate(ST, lf).then_inc(s_row, 1)
            values_half(PANEL0["w_in"] + 16, "w_in", 1)
            pe.wait_ge(s_vev, 2 * NT + 1)
            pe.wait_ge(s_cr, 1)
            pe.wait_ge(s_rbl, 1)
            attention("fox", HEADS, fox_scores, lambda qb: qb + 1, causal_pv)
            pe.wait_ge(s_bias, 16)
            attention("chunk", HEADS, chunk_scores, lambda qb: qb + 1, causal_pv)
            mean_square("mem", MEM)
            for c in range(8):
                chunk_of(PANEL0["mem_k"] + c, before(PROJ, "mem_k") + c, c % 2, HM, MEM, "mem" if c == 0 else None)
                if c == 1:
                    mean_square("fox")
                if c == 3:
                    mean_square("chunk")
            project("w_out", 8, "o")
            for pp in range(8):
                if pp == 1:
                    mean_square("mix")
                if pp == 6:
                    mean_square("x_mem")
                if pp % 4 == 0:
                    pe.wait_ge(s_vev, before(VTILES, "mem") + pp // 4 * 2 + 1)
                value_panel(PANEL0["mem_v"] + pp, pp % 4, 2, HM)
            project("mem_q", 8, "x_mem")
            attention("mem", 4, mem_scores, lambda qb: 2, mem_pv)
            project("mem_o", 8, "o_mem")
            mean_square("ca")
            mean_square("x_ffn")
            feed_forward(*FFNS[0])
            mean_square("x_a")
            project("a_in", 16, "x_a")
            gate_logits(8, 16)
            values_half(PANEL0["a_in"] + 16, "a_in", 0, (1, 16))
            pe.wait_ge(s_gate, 2)
            pe.wait_ge(s_free, before(PROJ, "a_in") + 16 + 2)
            cumulate(G[0], gz, stop=False)
            for tt in range(NT):
                last = pe.matmul(G[0][0:8, tt * P:(tt + 1) * P], gi[:, tt, :], ident, start=False, stop=tt == NT - 1,
                                 skip_group_check=True)
            last.then_inc(s_row, 1)
            cumulate(G[1], lf).then_inc(s_row, 1)
            for tt in range(NT):
                for st in range(tt + 1):
                    pe.matmul(ST[:, tt * 8:tt * 8 + 8], upper[:, 0:P] if st == tt else ones, gz[:, st, :],
                              start=st == 0, stop=False)
                last = pe.matmul(ST[:, tt * 8:tt * 8 + 8], ident, gi[:, tt, :], start=False, stop=True)
            last.then_inc(s_row, 1)
            values_half(PANEL0["a_in"] + 16, "a_in", 1)
            pe.wait_ge(s_vev, before(VTILES, "kv_b") + 1)
            pe.wait_ge(s_rbl, 2)

            def cell_head(n, slot):
                pe.wait_ge(cell["qk_split"], n + 1)
                pe.wait_ge(cell["side"], n + 1)
                for kb in range(NT):
                    w = S - kb * P
                    if not (isinstance(n, int) and n == 0 and kb < 2):
                        pe.wait_ge(cell["probs"], n * 4 + kb - 1)
                    three(G[kb % 2][:, 0:w], KS[:, slot, 0, kb * P:(kb + 1) * P], KS[:, slot, 1, kb * P:(kb + 1) * P],
                          QS[:, slot, 0, 0, kb * P:S], QS[:, slot, 0, 1, kb * P:S], True, True)
                    pe.matmul(T[kb % 2][:, 0:w], onesr[0:40, :], RBS[:, slot, kb * P:S], start=True, stop=False)
                    pe.matmul(T[kb % 2][:, 0:P], identr[:, :], maskTr[:, :], start=False, stop=True)\
                        .then_inc(cell["scores"], 1)
                if not (isinstance(n, int) and n == 0):
                    pe.wait_ge(cell["out"], n)
                pe.matmul(AD[:, :], ones[0:8, :], cond[0:8, slot * S:(slot + 1) * S], start=True, stop=True).then_inc(cell["guard"], 1)
                pe.wait_ge(cell["v_split"], n + 1)
                for kb in range(NT):
                    pe.wait_ge(cell["pt_split"], n * 4 + kb + 1)
                    three(O[0][:, kb * P:S], VS[:, slot, 0, kb * P:(kb + 1) * P], VS[:, slot, 1, kb * P:(kb + 1) * P],
                          PT[:, 0, kb, kb * P:S], PT[:, 1, kb, kb * P:S], kb == 0, kb == NT - 1)
                    for hl in range(2):
                        last = pe.matmul(O[1][:, kb * P:S], onesr[:, :], PT[:, hl, kb, kb * P:S],
                                         start=kb == 0 and hl == 0, stop=kb == NT - 1 and hl == 1)
                last.then_inc(cell["pv"], 1)

            cell_head(0, 0)
            cell_head(1, 1)
            with pe.Fori(1, HEADS // 2) as i:
                cell_head(i * 2, 0)
                cell_head(i * 2 + 1, 1)
            for h in range(HEADS):
                pe.wait_ge(cell["square"], h + 1)
                if h:
                    pe.wait_ge(cell["log"], h)
                pe.matmul(ST[:, :], ones, sq[:, h % 2, :], start=True, stop=True).then_inc(cell["mean"], 1)
            project("a_out", 8, "cells")
            mean_square("a")
            mean_square("x_mlp0")
            feed_forward(*FFNS[1])
            mean_square("x_b")
            small_project(PANEL0["kv_a"], before(PROJ, "kv_a"), 3, 8, 1, "x_kv")
            small_project(PANEL0["q_a"], before(PROJ, "q_a"), 3, 8, 1, "x_b", after_chunk=(0, "c_kv"))
            small_project(PANEL0["kv_b"], before(PROJ, "k_nope"), 8, 2, 4, "c_kv", HC, (3, "c_q"))
            for half in range(2):
                p = PANEL0["kv_b"] + 2 + half
                pe.wait_ge(s_split, p + 1)
                pe.wait_ge(s_vev, before(VTILES, "kv_b") + half * NT + 1)
                for k in range(2):
                    for tt in range(NT):
                        last = three((T + O)[tt][:, :], HC[:, k, 0, tt * P:(tt + 1) * P],
                                     HC[:, k, 1, tt * P:(tt + 1) * P], WH[:, p % 2, k * S:(k + 1) * S],
                                     WL[:, p % 2, k * S:(k + 1) * S], k == 0, k == 1)
                last.then_inc(s_used, 1)
            small_project(PANEL0["q_b"], before(PROJ, "q_nope"), 8, 3, 2, "c_q")
            small_project(PANEL0["q_b"] + 4, before(PROJ, "q_rope"), 4, 3, 2)
            pe.wait_ge(s_vev, before(VTILES, "kv_b") + 2 * NT + 1)
            attention("mla", HEADS, mla_scores, lambda qb: qb + 1, causal_pv)
            project("b_out", 8, "o_b")
            mean_square("b")
            mean_square("x_mlp1")
            feed_forward(*FFNS[2])

        @block.scalar
        def _(act):
            def hold():
                act.sem_inc(s_hold, 1)

            def panel_high(p, slot):
                if isinstance(p, int) and p >= NPANEL:
                    return
                act.wait_ge(s_stage[slot], p * 8 + (16 - 8 * slot))
                act.activation(WH[:, slot, :], stage[:, slot, :], ACT.Copy).then_inc(s_hisplit, 1)

            def used(p, slot):
                act.wait_ge(s_used, p + 1)
                panel_high(p + 2, slot)

            def square(name, m, source, width=S):
                if m == 0 and name != "x":
                    act.wait_ge(s_sum, before(SUMS, name))
                table, counter = (SUMS, s_sum) if name in SUMMED_BY_PE else (ADDS, s_add)
                if before(table, name) + max(m - 1, 0):
                    act.wait_ge(counter, before(table, name) + max(m - 1, 0))
                act.activation(sq[:, m % 2, 0:width], source, ACT.Square).then_inc(s_sq, 1)

            def squares(name, source, ready, width=S):
                for m in range(row(STATS, name)[1]):
                    ready(m)
                    square(name, m, source(m), width)

            def load_ln_exp():
                act.preload_act_table_set("natural_log_exp_and_others")

            def root(name, width=S):
                at = [r[0] for r in STATS].index(name)
                act.wait_ge(s_sum, before(SUMS, name) + row(SUMS, name)[1])
                act.activation(logs[:, 0:width], ST[:, 0:width], ACT.Ln, bias=eps[:, :],
                               scale=1.0 / row(STATS, name)[2]).then_inc(s_log, 1)
                act.wait_ge(s_log, at + 1)
                act.activation(rstd[:, 0:width], logs[:, 0:width], ACT.Exp, scale=-0.5).then_inc(s_rstd, 1)

            def high_chunk(name, m, source, dest, shift=None):
                if row(MAKES, name)[2]:
                    act.wait_ge(s_t, before(MAKES_T, name) + m + 1)
                    act.activation(dest(m), source(m), ACT.Identity, bias=shift(m))\
                        .then_inc(s_hi, 1)
                else:
                    act.activation(dest(m), source(m), ACT.Copy).then_inc(s_hi, 1)

            def high(name, source, dest, shift=None):
                for m in range(row(MAKES, name)[1]):
                    high_chunk(name, m, source, dest, shift)

            def evacuate(name, count, dest, first=0, func=ACT.Copy, scale=1.0):
                p0 = PANEL0[name] + first
                with act.Fori(0, count // 2) as i:
                    for j in range(2):
                        used(i * 2 + (p0 + j), j)
                        hold()
                        act.activation(dest(i * 2 + j), G[j][:, :], func, scale=scale).then_inc(s_free, 1)

            def evacuate_squares(name, stat_name):
                for c in range(KC):
                    used(PANEL0[name] + c, c % 2)
                    square(stat_name, c, G[c % 2][:, :])
                    act.activation(Y[:, c, :], G[c % 2][:, :], ACT.Copy).then_inc(s_free, 1)
                    if name == "a_out" and c == 3:
                        act.wait_ge(s_rope, 1)
                        act.activation(sin, ropeA, ACT.Sin, scale=con[:, CON["rope_sign"]:CON["rope_sign"] + 1])\
                            .then_inc(s_rsin, 1)
                        act.activation(cos, ropeB, ACT.Sin).then_inc(s_rsin, 1)
                        load_ln_exp()

            def evacuate_half(p0, half, mixer=None):
                for pp in range(4):
                    used(p0 + half * 4 + pp, pp % 2)
                    if mixer is not None and pp == 0:
                        log_of_gates(mixer)
                for tt in range(NT):
                    act.activation(V[:, tt, half * S:(half + 1) * S], value_banks[tt][:, :], ACT.Copy)\
                        .then_inc(s_vev, 1)

            def evacuated(name):
                act.wait_ge(s_free, before(PROJ, name) + row(PROJ, name)[1] + 2)

            def attention(name, heads, out_of):
                sm = att[name]
                act.sem_inc(sm["out"], 1)

                def stage_qk(n, pair, slot, early=False):
                    if not early:
                        act.wait_ge(sm["scores"], n * 4 - 4)
                    hold()
                    for source, hi, _ in staged_qk(name, n, pair, slot):
                        last = act.activation(hi, source, ACT.Copy)
                    last.then_inc(sm["qk_high"], 1)

                def stage_v(n, pair, slot, early=False):
                    if not early:
                        act.wait_ge(sm["pv"], n - 1)
                    hold()
                    source, hi, _ = staged_v(name, n, pair, slot)
                    act.activation(hi, source, ACT.Copy).then_inc(sm["v_high"], 1)

                def exp(head, qb):
                    n = head[0]
                    if not (isinstance(n, int) and n == 0):
                        act.wait_ge(sm["turned"], n * 4 + (qb - 3))
                    act.wait_ge(sm["max"], n * 4 + (qb + 1))
                    w = keys_of(name, qb)
                    act.activation(prob[qb][:, 0:w], score_bank[qb][:, 0:w], ACT.Exp, bias=stat[:, qb:qb + 1],
                                   accum_out=stat[:, 4 + qb:5 + qb]).then_inc(sm["exp"], 1)

                def pt_high(head, qb):
                    n = head[0]
                    act.wait_ge(sm["turned"], n * 4 + (qb + 1))
                    if qb == 0 and not (isinstance(n, int) and n == 0):
                        act.wait_ge(sm["pv"], n)
                    w = keys_of(name, qb)
                    act.activation(PT[:, 0, 0:w // P, qb * P:(qb + 1) * P],
                                   T[qb % 2][:, 0:w].rearrange("p (k q) -> p k q", q=P), ACT.Copy)\
                        .then_inc(sm["pt_high"], 1)

                def out(head):
                    n, pair, slot = head
                    act.wait_ge(sm["pv"], n + 1)
                    hold()
                    for dest, source in out_of(n, pair, slot):
                        last = act.activation(dest, source, ACT.Copy)
                    last.then_inc(sm["out"], 1)

                def start():
                    stage_qk(0, 0, 0, True)
                    for qb in range(NT):
                        exp((0, 0, 0), qb)
                        if qb == 0:
                            stage_v(0, 0, 0, True)
                        if qb == 1:
                            stage_qk(1, 0, 1, True)

                def round_(prev, now, nxt, after):
                    if nxt:
                        exp(nxt, 0)
                    if prev:
                        out(prev)
                    pt_high(now, 0)
                    if nxt:
                        stage_v(*nxt, early=not prev)
                    pt_high(now, 1)
                    if nxt:
                        exp(nxt, 1)
                    if after:
                        stage_qk(*after)
                    for qb in (2, 3):
                        pt_high(now, qb)
                        if nxt:
                            exp(nxt, qb)

                attention_rounds(act, heads, start, round_, lambda: out((heads - 1, heads // 2 - 1, 1)))

            def half_out(base):
                return lambda n, pair, slot: [(Y[half_rows[slot], pair + base, :], O[slot][half_rows[slot], :])]

            def feed_forward(name, groups, gated):
                sm = ff[name]
                banks = [G[0], None, ST, None] if gated else [G[0], None, G[1], None]
                per = 2 if gated else 1
                def through(g, slot):
                    p = ff_up(name, g)
                    for j in range(2):
                        used(p + j * per, (j * per) % 2)
                        if not (isinstance(g, int) and g == 0):
                            act.wait_ge(sm["split"], g * 2 + j - 1)
                        act.activation(t[:, j, :], banks[2 * j][:, :], ACT.Silu if gated else ACT.Relu)\
                            .then_inc(sm["act"], 1)
                        if gated:
                            used(p + (j * per + 1), 1)
                        act.wait_ge(sm["hidden"], g * 2 + j + 1)
                        act.activation(HID[:, slot, j, 0, :], t[:, j, :], ACT.Copy).then_inc(sm["high"], 1)

                def down(g, last=False):
                    p = ff_down(name, g, last)
                    used(p, 0)
                    used(p + 1, 1)

                through(0, 0)
                with act.Fori(0, (groups - 1) // 2) as i:
                    through(i * 2 + 1, 1)
                    down(i * 2)
                    through(i * 2 + 2, 0)
                    down(i * 2 + 1)
                if groups % 2 == 0:
                    through(groups - 1, 1)
                    down(groups - 2)
                if gated:
                    load_ln_exp()
                for m in range(KC):
                    if m % 4 == 0:
                        used_panel = ff_down(name, groups - 1, True) + m // 4
                    act.wait_ge(sm["added"], groups * 8 + m - 3)
                    square(name, m, Y[:, m, :])
                    if m % 4 == 3:
                        used(used_panel, m // 4)

            def after_residual(name):
                return lambda m: await_x(act, name, m)

            def once(sem_, value):
                return lambda m: act.wait_ge(sem_, value)

            def xc(m):
                return x[:, m, :]

            def yc(m):
                return Y[:, m, :]

            def hh(m):
                return H[:, m, 0, :]

            def logit_rows(mixer, n):
                act.wait_ge(s_gl, 2 * mixer + 1)
                act.activation(t[0:n, 0, :], ST[0:n, :], ACT.Copy).then_inc(s_glr, 1)

            def log_of_gates(mixer):
                act.wait_ge(s_gz, mixer + 1)
                act.activation(gw[:], gw[:], ACT.Exp).then_inc(s_gact, 1)
                act.wait_ge(s_gact, 2 * mixer + 1)
                act.activation(gw[:], gw[:], ACT.Ln, bias=1.0).then_inc(s_gact, 1)

            load_ln_exp()
            act.sem_inc(s_free, 2)
            act.sem_inc(s_vev, 1)
            act.wait_ge(s_eps, 1)
            squares("x", xc, lambda m: act.wait_ge(s_x if m < 4 else s_x2, 16))
            panel_high(0, 0)
            panel_high(1, 1)
            root("x")
            act.wait_ge(s_const, 32)
            high("x", yc, hh, lambda m: col("zero"))
            act.activation(identr[:], ident, ACT.Copy)
            act.activation(onesr[:], ones, ACT.Copy)
            act.activation(maskr[:], con[:, CON["mask"]:CON["mask"] + P], ACT.Copy)
            act.activation(maskTr[:], con[:, CON["maskT"]:CON["maskT"] + P], ACT.Copy).then_inc(s_cr, 1)
            act.wait_ge(s_c, 16)
            act.activation(cond[:], cond[:], ACT.Silu).then_inc(s_cond, 1)
            load_ln_exp()
            act.wait_ge(s_gw, 16)
            act.activation(wgateH[:], wgate[:], ACT.Copy).then_inc(s_wgh, 1)
            for first in (0, 8):
                evacuate("w_in", 4, lambda c: QK[:, c + first, :], first=first, scale=64 ** -0.5)
                evacuate("w_in", 4, lambda c: QK[:, c + (first + 4), :], first=first + 4)
            logit_rows(0, 8)
            evacuate_half(PANEL0["w_in"] + 16, 0, 0)
            act.wait_ge(s_row, 1)
            act.wait_ge(s_pad, 1)
            act.activation(RB[0:8, :], ST[0:8, :], ACT.Copy).then_inc(s_rb, 1)
            evacuate_half(PANEL0["w_in"] + 16, 1)
            act.wait_ge(s_pad, 2)
            attention("fox", HEADS, half_out(0))
            attention("chunk", HEADS, half_out(4))
            act.wait_ge(att["chunk"]["out"], HEADS + 1)
            squares("mem", lambda m: memf[:, m, :], once(s_mem, 16), MEM)
            root("mem", MEM)
            high("mem", lambda m: memf[:, m, :], lambda m: HM[:, m, 0, :], lambda m: col("zero"))
            for c in range(8):
                used(PANEL0["mem_k"] + c, c % 2)
                act.activation(memK[:, c, :], G[c % 2][:, 0:MEM], ACT.Copy).then_inc(s_free, 1)
                if c == 0:
                    squares("fox", yc, lambda m: None)
                if c == 1:
                    root("fox")
                    high("o_fox", yc, hh, lambda m: col("zero"))
                    squares("chunk", lambda m: yc(m + 4), lambda m: None)
                if c == 3:
                    root("chunk")
                    high("o_chunk", lambda m: yc(4 + m), lambda m: hh(4 + m), lambda m: col("zero"))
            evacuate_squares("w_out", "mix")
            for pp in range(8):
                used(PANEL0["mem_v"] + pp, pp % 2)
                if pp == 0:
                    root("mix")
                if 1 <= pp <= 4:
                    for m in (2 * pp - 2, 2 * pp - 1):
                        await_x(act, "mix", m)
                        square("x_mem", m, xc(m))
                if pp % 4 == 3:
                    for tt in range(2):
                        act.activation(V[:, 2 + tt, pp // 4 * S:pp // 4 * S + S], value_banks[tt][:, :], ACT.Copy)\
                            .then_inc(s_vev, 1)
                if pp == 5:
                    root("x_mem")
            high("x_mem", yc, hh, lambda m: col("zero"))
            evacuate("mem_q", 8, lambda c: QK[:, c, :], scale=256 ** -0.5)
            evacuated("mem_q")
            attention("mem", 4, lambda n, pair, slot: [(Y[:, n * 2 + c, :], O[c][:, :]) for c in range(2)])
            act.wait_ge(att["mem"]["out"], 5)
            high("o_mem", yc, hh)
            evacuate_squares("mem_o", "ca")
            root("ca")
            squares("x_ffn", xc, after_residual("ca"))
            root("x_ffn")
            high("x_ffn", yc, hh, lambda m: col("zero"))
            feed_forward(*FFNS[0])
            root("ffn")
            squares("x_a", xc, after_residual("ffn"))
            root("x_a")
            high("x_a", yc, hh, lambda m: adac[:, SH1 * 8 + m:SH1 * 8 + m + 1])
            evacuate("a_in", 4, lambda c: QK[:, c, :], scale=64 ** -0.5)
            evacuate("a_in", 4, lambda c: QK[:, c + 4, :], first=4)
            evacuate("a_in", 8, lambda c: QK[:, c + 8, :], first=8, func=ACT.Sigmoid)
            load_ln_exp()
            logit_rows(1, 16)
            evacuate_half(PANEL0["a_in"] + 16, 0, 1)
            act.wait_ge(s_scan, 1)
            act.activation(RB[0:8, :], t[0:8, 0, :], ACT.Copy).then_inc(s_rb, 1)
            evacuate_half(PANEL0["a_in"] + 16, 1)
            act.wait_ge(s_pad, 3)

            def cell_stage(n, pair, slot, early=False):
                if not early:
                    act.wait_ge(cell["scores"], n * 4 - 4)
                hold()
                for source, hi, _ in staged_qk("cell", n, pair, slot):
                    last = act.activation(hi, source, ACT.Copy)
                last.then_inc(cell["qk_high"], 1)

            def cell_stage_v(n, slot, early=False):
                if not early:
                    act.wait_ge(cell["pv"], n - 1)
                hold()
                source, hi, _ = staged_v("cell", n, None, slot)
                act.activation(hi, source, ACT.Copy).then_inc(cell["v_high"], 1)

            def cell_head(n, pair, slot, nxt=True):
                zero = isinstance(n, int) and n == 0

                def weight(kb):
                    if not (zero and kb < 2):
                        act.wait_ge(cell["probs"], n * 4 + kb - 1)
                    act.wait_ge(cell["scores"], n * 4 + kb + 1)
                    hold()
                    act.activation(sq[:, kb % 2, 0:S - kb * P], T[kb % 2][:, 0:S - kb * P], ACT.Exp,
                                   bias=gsf[:, bass.ds(n + kb * 8, 1)]).then_inc(cell["exp"], 1)

                def pt_high(kb):
                    if kb == 0 and not zero:
                        act.wait_ge(cell["pv"], n)
                    act.wait_ge(cell["probs"], n * 4 + kb + 1)
                    act.activation(PT[:, 0, kb, kb * P:S], t[:, kb % 2, 0:S - kb * P], ACT.Copy)\
                        .then_inc(cell["pt_high"], 1)

                weight(0)
                weight(1)
                pt_high(0)
                if nxt:
                    cell_stage(n + 1, pair if slot == 0 else pair + 1, 1 - slot, zero)
                weight(2)
                pt_high(1)
                weight(3)
                pt_high(2)
                if nxt:
                    cell_stage_v(n + 1, 1 - slot, zero)
                pt_high(3)
                act.wait_ge(cell["guard"], n + 1)
                if not zero:
                    act.wait_ge(cell["out"], n)
                act.activation(X[:, 0, :], AD[:, :], ACT.Exp).then_inc(cell["gexp"], 1)
                act.wait_ge(cell["den"], n * 2 + 2)
                act.activation(X[:, 1, :], X[:, 1, :], ACT.Ln).then_inc(cell["den_log"], 1)
                act.wait_ge(cell["den_log"], n + 1)
                act.activation(X[:, 1, :], X[:, 1, :], ACT.Exp, scale=-1.0).then_inc(cell["den_inverse"], 1)

            cell_stage(0, 0, 0, True)
            cell_stage_v(0, 0, True)
            cell_head(0, 0, 0)
            with act.Fori(0, (HEADS - 2) // 2) as i:
                cell_head(i * 2 + 1, i, 1)
                cell_head(i * 2 + 2, i + 1, 0)
            cell_head(HEADS - 1, HEADS // 2 - 1, 1, False)
            act.wait_ge(cell["out"], HEADS)

            def cell_square(h):
                if h >= 2:
                    act.wait_ge(cell["mean"], h - 1)
                act.activation(sq[:, h % 2, :], Y[:, h, :], ACT.Square).then_inc(cell["square"], 1)

            cell_square(0)
            for h in range(HEADS):
                if h + 1 < HEADS:
                    cell_square(h + 1)
                act.wait_ge(cell["mean"], h + 1)
                if h >= 2:
                    act.wait_ge(cell["normed"], h - 1)
                act.activation(X[:, h % 2, :], ST[:, :], ACT.Ln, bias=eps[:, :], scale=1.0 / P)\
                    .then_inc(cell["log"], 1)
                act.wait_ge(cell["log"], h + 1)
                act.activation(X[:, h % 2, :], X[:, h % 2, :], ACT.Exp, scale=-0.5).then_inc(cell["root"], 1)
                if h:
                    act.wait_ge(cell["normed"], h)
                    high_chunk("cells", h - 1, yc, hh)
            act.wait_ge(cell["normed"], HEADS)
            high_chunk("cells", HEADS - 1, yc, hh)
            evacuate_squares("a_out", "a")
            root("a")
            squares("x_mlp0", xc, after_residual("a"))
            root("x_mlp0")
            high("x_mlp0", yc, hh, lambda m: adac[:, SH2 * 8 + m:SH2 * 8 + m + 1])
            feed_forward(*FFNS[1])
            root("mlp0")
            squares("x_b", xc, after_residual("mlp0"))
            root("x_b")
            high("x_kv", yc, hh, lambda m: adac[:, KVSH * 8 + m:KVSH * 8 + m + 1])

            def evacuate_small(p0, name, chunks, per_panel, proj0, dest, swap=None, scale=1.0,
                               after=None):
                n0, passed = before(PROJ, name), 0
                for c in range(chunks):
                    if c % per_panel == per_panel - 1 or c == chunks - 1:
                        p = p0 + c // per_panel
                        used(p, p % 2)
                    else:
                        passed += 1
                        act.wait_ge(s_proj, proj0 + passed)
                    last = act.activation(dest(c), G[(n0 + c) % 2][:, :], ACT.Copy, scale=scale)
                    turned = swap(c) if swap else None
                    if turned is not None:
                        for b in range(4):
                            r = b ^ 1
                            last = act.activation(turned[32 * r:32 * r + 32, :],
                                                  G[(n0 + c) % 2][32 * b:32 * b + 32, :], ACT.Copy, scale=scale)
                    last.then_inc(s_free, 1)
                    if after:
                        after(c)

            act.wait_ge(s_rsin, 2)
            evacuate_small(PANEL0["kv_a"], "kv_a", 3, 1, 0, yc, lambda c: swapped[0] if c == 2 else None)
            high("x_b", lambda m: QK[:, m, :], hh, lambda m: adac[:, (LAYER1 + SH1) * 8 + m:(LAYER1 + SH1) * 8 + m + 1])
            evacuated("kv_a")
            squares("c_kv", yc, lambda m: None)

            def between_q_a(c):
                if c == 0:
                    act.wait_ge(s_roped, 1)
                    act.activation(KR[:, 0, :], Y[:, 2, :], ACT.Copy).then_inc(s_kr, 1)
                    root("c_kv")
                if c == 1:
                    high("c_kv", yc, lambda m: HC[:, m, 0, :], lambda m: col("zero"))

            evacuate_small(PANEL0["q_a"], "q_a", 3, 1, 0, lambda c: Y[:, 3 + c, :], after=between_q_a)
            evacuated("q_a")
            squares("c_q", lambda m: Y[:, 3 + m, :], lambda m: None)

            def between_k_nope(c):
                if c == 4:
                    root("c_q")
                if c == 6:
                    high("c_q", lambda m: yc(3 + m), hh, lambda m: col("zero"))

            evacuate_small(PANEL0["kv_b"], "k_nope", 8, 4, 0, lambda c: QK[:, 8 + c, :], after=between_k_nope)
            for half in range(2):
                used(PANEL0["kv_b"] + 2 + half, (PANEL0["kv_b"] + half) % 2)
                for tt in range(NT):
                    act.activation(V[:, tt, half * S:(half + 1) * S], value_banks[tt][:, :], ACT.Copy)\
                        .then_inc(s_vev, 1)
            evacuate_small(PANEL0["q_b"], "q_nope", 8, 2, 6, lambda c: QK[:, c, :], scale=192 ** -0.5)

            def swap_q(c):
                if c >= 2:
                    act.wait_ge(s_roped, c)
                return swapped[c % 2]

            evacuate_small(PANEL0["q_b"] + 4, "q_rope", 4, 2, 10, lambda c: X[:, c, :], swap_q, 192 ** -0.5)
            act.wait_ge(s_roped, 5)
            act.wait_ge(s_pad, 4)
            attention("mla", HEADS, lambda n, pair, slot: [(Y[:, n, :], O[slot][:, :])])
            act.wait_ge(att["mla"]["out"], HEADS + 1)
            high("o_b", yc, hh)
            evacuate_squares("b_out", "b")
            root("b")
            squares("x_mlp1", xc, after_residual("b"))
            root("x_mlp1")
            high("x_mlp1", yc, hh, lambda m: adac[:, (LAYER1 + SH2) * 8 + m:(LAYER1 + SH2) * 8 + m + 1])
            feed_forward(*FFNS[2])
            root("mlp1")

        @block.vector
        def _(dve):
            chain = Chain(dve, s_dve)

            def low(out, source, hi, scale=1.0):
                return dve.scalar_tensor_tensor(out, source, scale, hi.bitcast(F32), ALU.mult, ALU.subtract)

            def add_square(name, m, width=S):
                at = [r[0] for r in STATS].index(name)
                if m == 1 and at:
                    dve.wait_ge(s_sum, before(SUMS, name))
                dve.wait_ge(s_sq, before(STATS, name) + m + 1)
                first = sq[:, 0, 0:width] if m == 1 else acc[:, 0:width]
                dve.tensor_tensor(acc[:, 0:width], first, sq[:, m % 2, 0:width], ALU.add).then_inc(s_add, 1)
                dve.wait_ge(s_add, before(ADDS, name) + m)

            def await_rstd(name, width=S):
                if name not in SUMMED_BY_PE and name not in ff:
                    for m in range(1, row(STATS, name)[1]):
                        add_square(name, m, width)
                dve.wait_ge(s_rstd, [r[0] for r in STATS].index(name) + 1)

            def make_scaled(name, source, gain, dest, shift, width=S, work=None):
                _, count, _ = row(MAKES, name)
                h0, t0 = before(MAKES, name), before(MAKES_T, name)
                work = work or yc

                def lows(m):
                    dve.wait_ge(s_hi, h0 + m + 1)
                    dve.scalar_tensor_tensor(dest(m), work(m), shift(m), dest_hi(m, name), ALU.add, ALU.subtract)\
                        .then_inc(s_h, 1)

                for m in range(count):
                    dve.scalar_tensor_tensor(work(m), source(m), gain(m), rstd[:, 0:width],
                                             ALU.mult, ALU.mult).then_inc(s_t, 1)
                    if m >= 2:
                        lows(m - 2)
                for m in range(max(count - 2, 0), count):
                    lows(m)
                dve.wait_ge(s_h, h0 + count)

            def dest_hi(m, name):
                if name == "mem":
                    return HM[:, m, 0, :].bitcast(F32)
                if name == "c_kv":
                    return HC[:, m, 0, :].bitcast(F32)
                return H[:, m + 4 if name == "o_chunk" else m, 0, :].bitcast(F32)

            def hl(m):
                return H[:, m, 1, :]

            def plain_low(name, m, source):
                dve.wait_ge(s_hi, before(MAKES, name) + m + 1)
                dve.tensor_tensor(H[:, m, 1, :], source(m), H[:, m, 0, :].bitcast(F32), ALU.subtract)\
                    .then_inc(s_h, 1)

            def make_plain(name, source):
                _, count, _ = row(MAKES, name)
                for m in range(count):
                    plain_low(name, m, source)
                dve.wait_ge(s_h, before(MAKES, name) + count)

            def residual(name, gain):
                base = 8 * RESID.index(name)

                def add(m):
                    if m not in POOL_ADDS:
                        dve.wait_ge(s_rt2, base + m + 1)
                        dve.tensor_tensor(x[:, m, :], x[:, m, :], Y[:, m, :], ALU.add).then_inc(s_res, 1)

                for m in range(KC):
                    dve.scalar_tensor_tensor(Y[:, m, :], Y[:, m, :], gain(m), rstd[:, :], ALU.mult, ALU.mult)\
                        .then_inc(s_rt2, 1)
                    if m:
                        add(m - 1)
                add(KC - 1)
                for m in range(KC):
                    await_x(dve, name, m)

            def piece(k, landed, column):
                dve.wait_ge(s_piece[k % 2], landed)
                dve.scalar_tensor_tensor(apiece[:, k % 2, :], apiece[:, k % 2, :], 1.0, cond[:], ALU.mult,
                                         ALU.mult, accum_out=adac[:, column]).then_inc(s_pused, 1)

            def add_bias(g0, n):
                dve.wait_ge(s_pused, 8 * (g0 + n))
                chain.link(dve.tensor_tensor(adac[:, 8 * g0:8 * (g0 + n)], adac[:, 8 * g0:8 * (g0 + n)],
                                             vec[:, VEC["ada_b"] + 8 * g0:VEC["ada_b"] + 8 * (g0 + n)], ALU.add))

            def adaptive(g0, n):
                with dve.Fori(0, n) if n > 1 else nullcontext(0) as i:
                    for k in range(KC):
                        piece(k, i * 64 + 16 * (4 * g0 + k // 2 + 1), bass.ds(i * 8 + (g0 * 8 + k), 1))
                add_bias(g0, n)

            def one_plus(dest, scale_group, gain_col):
                chain.link(dve.scalar_tensor_tensor(dest, adac[:, scale_group * 8:scale_group * 8 + 8], 1.0,
                                                    vec[:, gain_col:gain_col + 8], ALU.add, ALU.mult))

            def gated(dest, gate_group, gain_col):
                chain.link(dve.tensor_tensor(dest, adac[:, gate_group * 8:gate_group * 8 + 8],
                                             vec[:, gain_col:gain_col + 8], ALU.mult))

            def norm_col(layer, which):
                return VEC["norm_g"] + (layer * 4 + which) * 8

            def gains(layer, group0):
                one_plus(pre_g[:, 3 * layer, :], group0 + SC1, norm_col(layer, 0))
                one_plus(pre_g[:, 3 * layer + 1, :], group0 + SC2, norm_col(layer, 2))
                gated(post_g[:, 2 * layer, :], group0 + G1, norm_col(layer, 1))
                gated(post_g[:, 2 * layer + 1, :], group0 + G2, norm_col(layer, 3))

            def log_gates(mixer, first, bias_col):
                for tt in range(NT):
                    chain.link(dve.tensor_tensor(gz[:, tt, :], AD[:, 16 * tt + first:16 * tt + first + 8],
                                                 vec[:, bias_col:bias_col + 8], ALU.add))
                dve.scalar_tensor_tensor(gw[:], gz[:], -1.0, gz[:], ALU.mult, ALU.min).then_inc(s_gz, 1)
                dve.wait_ge(s_gact, 2 * mixer + 2)
                chain.link(dve.scalar_tensor_tensor(lf[:], gz[:], 0.0, gw[:], ALU.min, ALU.subtract))

            def select_rows(dest, source, n):
                rows = source.shape[0]
                return dve.tensor_scalar(dest, source, con[0:rows, bass.ds(n + CON["minus_onehot"], 1)], None, ALU.mult)

            def clear_other_rows(panels_used, part_):
                dve.wait_ge(s_used, panels_used)
                dve.memset(QS[half_rows[1], 0, part_, :, :].bitcast(F32), 0.0)
                dve.memset(QS[half_rows[0], 1, part_, :, :].bitcast(F32), 0.0).then_inc(s_pad, 1)

            def low_half(name, head):
                source, hi, lo = staged_qk(name, *head)[by_vector(name)]
                return dve.tensor_tensor(lo, source, hi.bitcast(F32), ALU.subtract)

            def attention(name, heads):
                sm = att[name]

                def rows(head):
                    dve.wait_ge(sm["qk_high"], head[0] + 1)
                    if name == "fox":
                        select_rows(RBS[:, head[2], :], RB[:].bitcast(F32), head[0])
                    low_half(name, head).then_inc(sm["side"], 1)

                def maximum(head, qb):
                    w = keys_of(name, qb)
                    dve.wait_ge(sm["scores"], head[0] * 4 + (qb + 1))
                    dve.tensor_reduce(stat[:, qb:qb + 1], score_bank[qb][:, 0:w], AX, ALU.max, negate=True)\
                        .then_inc(sm["max"], 1)

                def scale(head, qb):
                    n, w = head[0], keys_of(name, qb)
                    dve.wait_ge(sm["exp"], n * 4 + (qb + 1))
                    dve.reciprocal(stat[:, 8 + qb:9 + qb], stat[:, 4 + qb:5 + qb]).then_inc(sm["recip"], 1)
                    dve.wait_ge(sm["recip"], n * 4 + (qb + 1))
                    dve.tensor_scalar(prob[qb][:, 0:w], prob[qb][:, 0:w], stat[:, 8 + qb:9 + qb], None, ALU.mult)\
                        .then_inc(sm["probs"], 1)

                def pt_low(head, qb):
                    w = keys_of(name, qb)
                    dve.wait_ge(sm["pt_high"], head[0] * 4 + (qb + 1))
                    dve.tensor_tensor(PT[:, 1, 0:w // P, qb * P:(qb + 1) * P],
                                      T[qb % 2][:, 0:w].rearrange("p (k q) -> p k q", q=P),
                                      PT[:, 0, 0:w // P, qb * P:(qb + 1) * P].bitcast(F32), ALU.subtract)\
                        .then_inc(sm["pt_split"], 1)

                def start():
                    rows((0, 0, 0))
                    for qb in range(NT):
                        maximum((0, 0, 0), qb)
                        scale((0, 0, 0), qb)
                        if qb == 2:
                            rows((1, 0, 1))

                def round_(prev, now, nxt, after):
                    if nxt:
                        maximum(nxt, 0)
                        scale(nxt, 0)
                    pt_low(now, 0)
                    if nxt:
                        maximum(nxt, 1)
                    pt_low(now, 1)
                    if nxt:
                        scale(nxt, 1)
                    if after:
                        rows(after)
                    for qb in (2, 3):
                        if nxt:
                            maximum(nxt, qb)
                        pt_low(now, qb)
                        if nxt:
                            scale(nxt, qb)

                attention_rounds(dve, heads, start, round_, lambda: None)

            def feed_forward(name, groups, gated_, adaptive_group=None):
                def pieces(i, half):
                    if adaptive_group is not None:
                        for k in range(4 * half, 4 * half + 4):
                            piece(k, i * 64 + 16 * (4 * adaptive_group + k // 2 + 1),
                                  bass.ds(i * 8 + (adaptive_group * 8 + k), 1))

                sm = ff[name]
                up_banks = [G[1], AD] if gated_ else [G[0], G[1]]
                per = 2 if gated_ else 1
                dve.memset(Y[:], 0.0).then_inc(sm["added"], 4)
                dve.wait_ge(sm["added"], 4)

                def hidden(g, slot):
                    p = ff_up(name, g)
                    for j in range(2):
                        dve.wait_ge(sm["act"], g * 2 + j + 1)
                        if gated_:
                            dve.wait_ge(s_used, p + (2 * j + 2))
                            ins = dve.tensor_tensor(t[:, j, :], up_banks[j][:, :], t[:, j, :], ALU.mult)
                        else:
                            ins = dve.scalar_tensor_tensor(t[:, j, :], up_banks[j][:, :], 0.0, t[:, j, :],
                                                           ALU.max, ALU.mult)
                        ins.then_inc(sm["hidden"], 1)
                        dve.wait_ge(sm["high"], g * 2 + j + 1)
                        dve.tensor_tensor(HID[:, slot, j, 1, :], t[:, j, :], HID[:, slot, j, 0, :].bitcast(F32),
                                          ALU.subtract).then_inc(sm["split"], 1)

                def add(g, last_group=False):
                    p = ff_down(name, g, last_group)
                    for m in range(KC):
                        if m % 4 < 3:
                            dve.wait_ge(sm["down"], g * 6 + (m - m // 4 + 1))
                        else:
                            dve.wait_ge(s_used, p + (m // 4 + 1))
                        dve.tensor_tensor(Y[:, m, :], (T + O)[m % 4][:, :], Y[:, m, :], ALU.add)\
                            .then_inc(sm["added"], 1)
                        if last_group and m >= 2:
                            add_square(name, m - 1)
                    if last_group:
                        add_square(name, KC - 1)

                hidden(0, 0)
                with dve.Fori(0, (groups - 1) // 2) as i:
                    hidden(i * 2 + 1, 1)
                    add(i * 2)
                    pieces(i, 0)
                    hidden(i * 2 + 2, 0)
                    add(i * 2 + 1)
                    pieces(i, 1)
                if groups % 2 == 0:
                    hidden(groups - 1, 1)
                    add(groups - 2)
                add(groups - 1, True)
                dve.wait_ge(sm["added"], groups * 8 + 4)

            def vcol(name):
                return lambda m: col(name, m)

            def adash(group):
                return lambda m: adac[:, group * 8 + m:group * 8 + m + 1]

            def preg(i):
                return lambda m: pre_g[:, i, m:m + 1]

            def postg(i):
                return lambda m: post_g[:, i, m:m + 1]

            def xc(m):
                return x[:, m, :]

            def yc(m):
                return Y[:, m, :]

            def zero(m):
                return col("zero")

            dve.memset(eps[:], EPS).then_inc(s_eps, 1)
            dve.wait_ge(s_const, 32)
            await_rstd("x")
            make_scaled("x", xc, vcol("g_mix_pre"), hl, zero)
            dve.memset(RB[:].bitcast(F32), 0.0).then_inc(s_pad, 1)
            dve.wait_ge(s_wgh, 1)
            dve.tensor_tensor(wgateL[:], wgate[:], wgateH[:].bitcast(F32), ALU.subtract).then_inc(s_wg, 1)
            dve.wait_ge(s_cond, 1)
            adaptive(0, 4)
            dve.wait_ge(s_gl, 2)
            log_gates(0, 0, VEC["b_f"])
            dve.tensor_copy(gs[:], lf[:]).then_inc(s_gate, 1)
            adaptive(4, 1)
            dve.wait_ge(s_rb, 1)
            dve.tensor_tensor(RB[32:40, :], ST[0:8, :], RB[0:8, :].bitcast(F32), ALU.subtract).then_inc(s_rbl, 1)
            dve.wait_ge(s_rbl, 1)
            clear_other_rows(PANEL0["w_in"] + 24, 0)
            attention("fox", HEADS)
            attention("chunk", HEADS)
            await_rstd("mem", MEM)
            make_scaled("mem", lambda m: memf[:, m, :], vcol("g_mem_kv"), lambda m: HM[:, m, 1, :], zero, width=MEM,
                        work=lambda m: memf[:, m, :])
            await_rstd("fox")
            make_scaled("o_fox", yc, vcol("g_out"), hl, zero)
            await_rstd("chunk")
            make_scaled("o_chunk", lambda m: yc(4 + m), lambda m: col("g_out", 4 + m), lambda m: hl(4 + m), zero,
                        work=lambda m: yc(4 + m))
            await_rstd("mix")
            residual("mix", vcol("g_mix_post"))
            await_rstd("x_mem")
            make_scaled("x_mem", xc, vcol("g_mem_pre"), hl, zero)
            dve.wait_ge(s_used, PANEL0["mem_o"])
            attention("mem", 4)
            make_plain("o_mem", yc)
            await_rstd("ca")
            residual("ca", vcol("g_mem_post"))
            await_rstd("x_ffn")
            make_scaled("x_ffn", xc, vcol("g_ffn_pre"), hl, zero)
            feed_forward(*FFNS[0], adaptive_group=5)
            add_bias(5, 5)
            gains(0, 0)
            one_plus(pre_g[:, 2, :], KVSC, VEC["kv_norm_g"])
            await_rstd("ffn")
            residual("ffn", vcol("g_ffn_post"))
            await_rstd("x_a")
            make_scaled("x_a", xc, preg(0), hl, adash(SH1))
            adaptive(10, 3)
            dve.wait_ge(s_gl, 4)
            for tt in range(NT):
                chain.link(dve.tensor_tensor(gi[:, tt, :], AD[:, 16 * tt:16 * tt + 8],
                                             vec[:, VEC["gate_b"]:VEC["gate_b"] + 8], ALU.add))
            log_gates(1, 8, VEC["gate_b"] + 8)
            dve.tensor_scalar(gz[:], lf[:], -1.0, None, ALU.mult).then_inc(s_gate, 1)
            adaptive(13, 1)
            gains(1, LAYER1)
            dve.wait_ge(s_row, 4)
            dve.tensor_copy(gu[0:8, :], G[0][0:8, :]).then_inc(s_dve, 1)
            chain.n += 1
            dve.wait_ge(s_dve, chain.n)
            dve.tensor_tensor_scan(t[0:8, 0, :], gu[0:8, :], gu[0:8, :], 0.0, ALU.max, ALU.max).then_inc(s_scan, 1)
            dve.wait_ge(s_scan, 1)
            chain.link(dve.tensor_tensor(X[0:8, 2, :], G[1][0:8, :], t[0:8, 0, :], ALU.add))
            chain.link(dve.tensor_copy(gs[:], ST[:, 0:8 * NT].rearrange("p (a b) -> p a b", b=8)))
            dve.wait_ge(s_rb, 2)
            dve.tensor_tensor(RB[32:40, :], t[0:8, 0, :], RB[0:8, :].bitcast(F32), ALU.subtract).then_inc(s_rbl, 1)
            dve.wait_ge(s_rbl, 2)
            clear_other_rows(PANEL0["a_in"] + 24, 0)

            def cell_rows(n, pair, slot):
                dve.wait_ge(cell["qk_high"], n + 1)
                select_rows(RBS[:, slot, :], RB[:].bitcast(F32), n)
                select_rows(cond[0:8, slot * S:(slot + 1) * S], X[0:8, 2, :], n)
                low_half("cell", (n, pair, slot)).then_inc(cell["side"], 1)

            def cell_head(n, pair, slot, nxt=True):
                def weigh(kb):
                    dve.wait_ge(cell["exp"], n * 4 + kb + 1)
                    if not (isinstance(n, int) and n == 0 and kb < 2):
                        dve.wait_ge(cell["pt_split"], n * 4 + kb - 1)
                    dve.tensor_tensor(t[:, kb % 2, 0:S - kb * P], G[kb % 2][:, 0:S - kb * P],
                                      sq[:, kb % 2, 0:S - kb * P], ALU.mult).then_inc(cell["probs"], 1)

                def pt_low(kb):
                    dve.wait_ge(cell["pt_high"], n * 4 + kb + 1)
                    dve.tensor_tensor(PT[:, 1, kb, kb * P:S], t[:, kb % 2, 0:S - kb * P],
                                      PT[:, 0, kb, kb * P:S].bitcast(F32), ALU.subtract).then_inc(cell["pt_split"], 1)

                weigh(0)
                weigh(1)
                pt_low(0)
                if nxt:
                    cell_rows(n + 1, pair if slot == 0 else pair + 1, 1 - slot)
                weigh(2)
                pt_low(1)
                weigh(3)
                pt_low(2)
                pt_low(3)
                dve.wait_ge(cell["gexp"], n + 1)
                dve.wait_ge(cell["pv"], n + 1)
                dve.tensor_tensor(X[:, 1, :], O[1][:, :], X[:, 0, :], ALU.max).then_inc(cell["den"], 1)
                dve.wait_ge(cell["den"], n * 2 + 1)
                dve.scalar_tensor_tensor(X[:, 1, :], O[1][:, :], -1.0, X[:, 1, :], ALU.mult, ALU.max)\
                    .then_inc(cell["den"], 1)
                dve.wait_ge(cell["den_inverse"], n + 1)
                dve.tensor_tensor(Y[:, n, :], O[0][:, :], X[:, 1, :], ALU.mult).then_inc(cell["out"], 1)

            cell_rows(0, 0, 0)
            cell_head(0, 0, 0)
            with dve.Fori(0, (HEADS - 2) // 2) as i:
                cell_head(i * 2 + 1, i, 1)
                cell_head(i * 2 + 2, i + 1, 0)
            cell_head(HEADS - 1, HEADS // 2 - 1, 1, False)
            dve.wait_ge(cell["out"], HEADS)
            for h in range(HEADS):
                dve.wait_ge(cell["root"], h + 1)
                chain.link(dve.scalar_tensor_tensor(Y[:, h, :], Y[:, h, :], col("head_g", h), X[:, h % 2, :],
                                                    ALU.mult, ALU.mult))
                dve.tensor_tensor(Y[:, h, :], Y[:, h, :], QK[:, 8 + h, :], ALU.mult).then_inc(cell["normed"], 1)
                dve.wait_ge(cell["normed"], h + 1)
                if h:
                    plain_low("cells", h - 1, yc)
            plain_low("cells", HEADS - 1, yc)
            dve.wait_ge(s_h, before(MAKES, "cells") + HEADS)
            dve.wait_ge(s_pos, 16)
            chain.link(dve.tensor_copy(ropeF, apiece[:].bitcast(I32)[:, 0, 0:S]))
            chain.link(dve.tensor_scalar(ropeA, ropeF, con[:, CON["inv_freq"]:CON["inv_freq"] + 1], None, ALU.mult))
            chain.link(dve.tensor_scalar(ropeB, ropeA, 1.0 / TURN, ROUND, ALU.mult, ALU.add))
            chain.link(dve.tensor_scalar(ropeB, ropeB, ROUND, None, ALU.subtract))
            for part_of_turn in TURN_PARTS:
                chain.link(dve.scalar_tensor_tensor(ropeA, ropeB, -part_of_turn, ropeA, ALU.mult, ALU.add))
            chain.link(dve.tensor_scalar(ropeA, ropeA, PI_IN, -PI_IN, ALU.min, ALU.max))
            chain.link(dve.scalar_tensor_tensor(ropeB, ropeA, -1.0, ropeA, ALU.mult, ALU.min))
            dve.tensor_scalar(ropeB, ropeB, float(TURN / 4), None, ALU.add).then_inc(s_rope, 1)
            await_rstd("a")
            residual("a", postg(0))
            await_rstd("x_mlp0")
            make_scaled("x_mlp0", xc, preg(1), hl, adash(SH2))
            feed_forward(*FFNS[1])
            await_rstd("mlp0")
            residual("mlp0", postg(1))
            await_rstd("x_b")
            make_scaled("x_kv", xc, preg(2), hl, adash(KVSH))
            make_scaled("x_b", xc, preg(3), hl, adash(LAYER1 + SH1), work=lambda m: QK[:, m, :])

            def rotate(part_, turned, count):
                chain.link(dve.tensor_tensor(part_, part_, cos, ALU.mult))
                chain.link(dve.tensor_tensor(turned, turned, sin, ALU.mult))
                dve.tensor_tensor(part_, part_, turned, ALU.add).then_inc(s_roped, 1)
                dve.wait_ge(s_roped, count)

            dve.wait_ge(s_free, before(PROJ, "kv_a") + 3 + 2)
            rotate(Y[:, 2, :], swapped[0], 1)
            dve.wait_ge(s_kr, 1)
            chain.link(dve.tensor_tensor(KR[:, 1, :], Y[:, 2, :], KR[:, 0, :].bitcast(F32), ALU.subtract))
            await_rstd("c_kv")
            make_scaled("c_kv", yc, vcol("kv_latent_g"), lambda m: HC[:, m, 1, :], zero)
            await_rstd("c_q")
            make_scaled("c_q", lambda m: yc(3 + m), vcol("q_latent_g"), hl, zero,
                        work=lambda m: yc(3 + m))
            for m in range(4):
                dve.wait_ge(s_free, before(PROJ, "q_rope") + m + 3)
                rotate(X[:, m, :], swapped[m % 2], m + 2)
            clear_other_rows(PANEL0["b_out"], 1)
            attention("mla", HEADS)
            make_plain("o_b", yc)
            await_rstd("b")
            residual("b", postg(2))
            await_rstd("x_mlp1")
            make_scaled("x_mlp1", xc, preg(4), hl, adash(LAYER1 + SH2))
            feed_forward(*FFNS[2])
            await_rstd("mlp1")
            residual("mlp1", postg(3))


def _panels(w, chunks=None):
    k, n = w.shape
    return w.reshape(k // P, P, n // P, P).transpose(2, 1, 0, 3).reshape(n // P, P, k)


def _value_panels(w):
    k, n = w.shape
    return w.reshape(k // (2 * P), 2, P, n // S, S).transpose(3, 0, 2, 1, 4).reshape(-1, P, D)


def _few(w, per_panel):
    k, n = w.shape
    a = w.reshape(k // P, P, n // (P * per_panel), per_panel, P).transpose(2, 1, 3, 0, 4)
    a = a.reshape(n // (P * per_panel), P, per_panel * k)
    out = np.zeros((a.shape[0], P, D), np.float32)
    out[:, :, :a.shape[2]] = a
    return out


def _ffn_panels(up, down, per):
    first = up.reshape(-1, 2 * per, P, D)
    second = down.reshape(-1, 2, P, 2, S).transpose(0, 3, 2, 1, 4).reshape(-1, 2, P, D)
    out = [first[0]]
    for g in range(1, len(first)):
        out += [first[g], second[g - 1]]
    return np.concatenate(out + [second[-1]])


def _cols(v):
    return np.ascontiguousarray(v.reshape(-1, P).T)


def kernel(**inputs):
    import concourse.bacc as bacc
    from concourse.bass_utils import run_bass_kernel_spmd

    a = {k: np.asarray(v) for k, v in inputs.items()}
    w_in, a_in = a["w_in"][0], a["a_w_in_2"][0]
    gu = a["w_gate_up"][0]
    gate, up = _panels(gu[:, :DFF1]), _panels(gu[:, DFF1:])
    q_b = a["b_w_q_b_2"][0].reshape(384, HEADS, 192)
    kv_b = a["kv_w_b_2"].reshape(256, HEADS, 256)
    kv_a = a["kv_w_a_2"]
    panels = np.concatenate([
        _panels(np.concatenate([w_in[:, 0:1024], w_in[:, 1544:2568]], 1)),
        _value_panels(np.concatenate([w_in[:, 1024:1536], w_in[:, 2568:3080]], 1)),
        _panels(a["w_mem_kv"][0][:, :D]), _panels(a["w_out"][0]), _value_panels(a["w_mem_kv"][0][:, D:]),
        _panels(a["w_mem_q"][0]), _panels(a["w_mem_o"][0]),
        _ffn_panels(np.stack([gate, up], 1), a["w_down"][0].reshape(-1, P, D), 2),
        _panels(np.concatenate([a_in[:, 0:1024], a_in[:, 2064:3088]], 1)), _value_panels(a_in[:, 1024:2048]),
        _panels(a["a_w_out_2"][0]),
        _ffn_panels(_panels(a["mlp_w1_2"][0]), a["mlp_w2_2"][0].reshape(-1, P, D), 1),
        _panels(np.concatenate([kv_a, kv_a[:, 256:]], 1)),
        _panels(a["b_w_q_a_2"][0]),
        _few(kv_b[:, :, :P].reshape(256, D), 4), _value_panels(kv_b[:, :, P:].reshape(256, D)),
        _few(q_b[:, :, :P].reshape(384, D), 2), _few(q_b[:, :, P:].reshape(384, 512), 2),
        _panels(a["b_w_out_2"][0]),
        _ffn_panels(_panels(a["mlp_w1_2"][1]), a["mlp_w2_2"][1].reshape(-1, P, D), 1),
    ])
    ada = np.concatenate([
        w.T.reshape(-1, P, D)
        for w in (a["ada_w_2"][0], a["kv_ada_w_2"], a["ada_w_2"][1])])
    vecs = np.concatenate([
        _cols(a["g_mix_pre"]), _cols(np.concatenate([a["g_fox_out"][0], a["g_chunk_out"][0]])),
        _cols(a["g_mix_post"]), _cols(a["g_mem_pre"]), _cols(a["g_mem_kv"]), _cols(a["g_mem_post"]),
        _cols(a["g_ffn_pre"]), _cols(a["g_ffn_post"]), _cols(a["norm_g_2"]),
        _cols(np.concatenate([a["ada_b_2"][0], a["kv_ada_b_2"], a["ada_b_2"][1]])), _cols(a["kv_norm_g_2"]),
        _cols(a["a_head_g_2"][0]), _cols(a["kv_latent_g_2"]), _cols(a["b_q_latent_g_2"]),
        np.zeros((P, 8), np.float32), np.broadcast_to(a["b_fgate"][0], (P, 8)),
        np.broadcast_to(a["a_gate_b_2"][0].reshape(16), (P, 16))], 1)
    i = np.arange(P)
    onehot = np.zeros((P, 8), np.float32)
    onehot[:8] = -np.eye(8)
    onehot[32:40] = -np.eye(8)
    causal = np.where(i[None, :] <= i[:, None], 0.0, NEG)
    freq = 10000.0 ** (-(i % 32).astype(np.float32) / np.float32(32))
    cons = np.concatenate([
        np.eye(P), np.ones((P, P)), causal, causal.T, i[:, None] <= np.arange(S)[None, :], onehot,
        freq[:, None], np.where(i % 64 < 32, -1.0, 1.0)[:, None]], 1).astype(np.float32)
    gates_w = np.concatenate([w_in[:, 1536:1544], a_in[:, 2048:2064]], 1).reshape(KC, P, 24).transpose(1, 0, 2)
    dist = i[:, None] + P - np.arange(2 * P)[None, :]
    tile = a["rel_bias"][0][:, np.clip(dist, 1 - CH, REL) + CH - 1]
    tile = np.where((i[:, None] // CH < (np.arange(2 * P)[None, :] - P) // CH)[None], np.float32(NEG), tile)
    bias = tile.transpose(1, 0, 2).reshape(P, 2 * D)
    pos = np.broadcast_to(a["positions_2"].reshape(1, S), (P, S))
    arrays = {"xT": a["x"][0].T, "memT": a["mem"][0].T, "panels": panels, "ada": ada, "c": np.broadcast_to(a["c_2"], (P, D)), "vecs": vecs, "cons": cons,
              "gates_w": gates_w, "bias": bias, "pos": pos}
    arrays = {k: np.ascontiguousarray(v) for k, v in arrays.items()}
    nc = bacc.Bacc("TRN2", target_bir_lowering=False, num_devices=1)
    args = [nc.dram_tensor(k, v.shape, mybir.dt.from_np(v.dtype), kind="ExternalInput").ap() for k, v in arrays.items()]
    out = nc.dram_tensor("outT", (D, S), F32, kind="ExternalOutput").ap()
    program(nc, *args, out)
    r = run_bass_kernel_spmd(nc, [arrays], core_ids=[0])
    return np.ascontiguousarray(r.results[0]["outT"].T)[None]
```
